# Optimizing a Trainium2 kernel written in Bass

```python
import jax, jax.numpy as jnp
from jax import lax
import numpy as np
import math

D_MODEL = 1024
BATCH = 1
SEQ = 256
DEPTH = 2

ROPE_THETA = 500000.0
Q_BLOCK = 128
NEG_INF = -1e30
NORM_EPS = 1e-6
POS_OFFSET_MAX = 512
HEAD_DIM = 64
PARTIAL_ROT = HEAD_DIM // 4
N_BRANCH = 4
BRANCH_W = 4 * HEAD_DIM
D_FF = 4 * D_MODEL

MLA_HEADS = 4
MLA_NOPE = 64
MLA_ROPE = 32
MLA_V = 64
MLA_Q_LORA = 256
MLA_KV_LORA = 128

NSA_HEADS = 4
NSA_CMP_LEN = 32
NSA_CMP_STRIDE = 16
NSA_SEL_LEN = 64
NSA_TOP_N = 8
NSA_WINDOW = 512
NSA_N_PATHS = 3
NSA_FORCED_SCORE = 1e4

FOX_HEADS = 4

DSA_HEADS = 4
IDX_HEADS = 8
IDX_DIM = 32
IDX_ROT = IDX_DIM // 4
DSA_TOP_K = 256
DSA_KEEP_DIV = 4

MLA_COLS = MLA_Q_LORA + MLA_KV_LORA + MLA_ROPE
NSA_COLS = NSA_HEADS * HEAD_DIM + 6 * HEAD_DIM + NSA_N_PATHS * NSA_HEADS
FOX_COLS = 3 * FOX_HEADS * HEAD_DIM + FOX_HEADS
DSA_COLS = DSA_HEADS * HEAD_DIM + 2 * HEAD_DIM + IDX_HEADS * IDX_DIM + IDX_DIM + IDX_HEADS
GATE_COLS = N_BRANCH * D_MODEL
IN_COLS = MLA_COLS + NSA_COLS + FOX_COLS + DSA_COLS + GATE_COLS


def split_cols(z, sizes):
    cuts = [int(c) for c in np.cumsum(sizes)[:-1]]
    return jnp.split(z, cuts, axis=-1)

def rmsnorm(x, g):
    xf = x.astype(jnp.float32)
    y = xf * lax.rsqrt(jnp.mean(xf * xf, axis=-1, keepdims=True) + NORM_EPS)
    return (y * g.astype(jnp.float32)).astype(x.dtype)

def rope_tables(positions, rot_dim):
    inv = ROPE_THETA ** (-jnp.arange(0, rot_dim, 2, dtype=jnp.float32) / rot_dim)
    ang = positions.astype(jnp.float32)[..., None] * inv
    return (jnp.cos(ang), jnp.sin(ang))

def apply_rope(x, rope):
    cos, sin = rope
    half = cos.shape[-1]
    if x.ndim == 4:
        cos, sin = cos[:, :, None, :], sin[:, :, None, :]
    cos, sin = cos.astype(x.dtype), sin.astype(x.dtype)
    x1, x2 = x[..., :half], x[..., half:2 * half]
    return jnp.concatenate([x1 * cos - x2 * sin, x2 * cos + x1 * sin, x[..., 2 * half:]], axis=-1)

def masked_softmax(s, mask):
    s = jnp.where(mask, s, NEG_INF)
    m = jnp.max(s, axis=-1, keepdims=True)
    p = jnp.exp(s - m) * mask
    return p / jnp.maximum(jnp.sum(p, axis=-1, keepdims=True), 1e-30)

def sweep_query_blocks(fn, seq):
    out = lax.map(fn, jnp.arange(seq // Q_BLOCK))
    out = jnp.moveaxis(out, 0, 1)
    return out.reshape((out.shape[0], seq) + out.shape[3:])

def blocked_causal_attention(q, k, v, scale, decay=None):
    S = q.shape[1]
    key_pos = jnp.arange(S)
    decay_t = None if decay is None else jnp.swapaxes(decay, 1, 2)

    def one_block(i):
        start = i * Q_BLOCK
        qb = lax.dynamic_slice_in_dim(q, start, Q_BLOCK, axis=1)
        s = jnp.einsum('bqhd,bkhd->bhqk', qb, k).astype(jnp.float32) * scale
        if decay_t is not None:
            cq = lax.dynamic_slice_in_dim(decay_t, start, Q_BLOCK, axis=2)
            s = s + (cq[..., :, None] - decay_t[..., None, :])
        q_pos = start + jnp.arange(Q_BLOCK)
        mask = key_pos[None, :] <= q_pos[:, None]
        p = jax.nn.softmax(jnp.where(mask, s, NEG_INF), axis=-1)
        return jnp.einsum('bhqk,bkhd->bqhd', p.astype(v.dtype), v)

    return sweep_query_blocks(one_block, S)

def mla_mixer(z, q_norm_g, w_uq, kv_norm_g, w_ukv, rope):
    B, S, _ = z.shape
    H = MLA_HEADS
    c_q, c_kv, k_rope = split_cols(z, [MLA_Q_LORA, MLA_KV_LORA, MLA_ROPE])
    q = (rmsnorm(c_q, q_norm_g) @ w_uq).reshape(B, S, H, MLA_NOPE + MLA_ROPE)
    q = jnp.concatenate([q[..., :MLA_NOPE], apply_rope(q[..., MLA_NOPE:], rope)], axis=-1)
    kv = (rmsnorm(c_kv, kv_norm_g) @ w_ukv).reshape(B, S, H, MLA_NOPE + MLA_V)
    k_rope = apply_rope(k_rope, rope)
    k = jnp.concatenate([kv[..., :MLA_NOPE],
                         jnp.broadcast_to(k_rope[:, :, None, :], (B, S, H, MLA_ROPE))], axis=-1)
    v = kv[..., MLA_NOPE:]
    o = blocked_causal_attention(q, k, v, (MLA_NOPE + MLA_ROPE) ** -0.5)
    return o.reshape(B, S, H * MLA_V)

def nsa_mixer(z, cmp_w, cmp_pe, rope):
    B, S, _ = z.shape
    H, D = NSA_HEADS, HEAD_DIM
    q, kc, vc, ks, vs, kw, vw, g = split_cols(z, [H * D] + [D] * 6 + [NSA_N_PATHS * H])
    q = apply_rope(q.reshape(B, S, H, D), rope)
    kc, ks, kw = apply_rope(kc, rope), apply_rope(ks, rope), apply_rope(kw, rope)
    g = jax.nn.sigmoid(g.reshape(B, S, NSA_N_PATHS, H))
    scale = D ** -0.5
    t_pos = jnp.arange(S)
    bidx = jnp.arange(B)[:, None, None]

    n_cmp = (S - NSA_CMP_LEN) // NSA_CMP_STRIDE + 1
    cmp_start = jnp.arange(n_cmp) * NSA_CMP_STRIDE
    win_idx = cmp_start[:, None] + jnp.arange(NSA_CMP_LEN)[None, :]

    def compress(t, w, pe):
        blocks = t[:, win_idx] + pe
        return blocks.reshape(B, n_cmp, NSA_CMP_LEN * D) @ w

    k_cmp = compress(kc, cmp_w[0], cmp_pe[0])
    v_cmp = compress(vc, cmp_w[1], cmp_pe[1])
    cmp_mask = (cmp_start + NSA_CMP_LEN - 1)[None, :] <= t_pos[:, None]
    s_cmp = jnp.einsum('bthd,bcd->bhtc', q, k_cmp).astype(jnp.float32) * scale
    p_cmp = masked_softmax(s_cmp, cmp_mask)
    o_cmp = jnp.einsum('bhtc,bcd->bthd', p_cmp.astype(v_cmp.dtype), v_cmp)

    n_sb = S // NSA_SEL_LEN
    sb = jnp.arange(n_sb)
    sb_start = sb * NSA_SEL_LEN
    overlap = jnp.maximum(
        jnp.minimum(cmp_start[:, None] + NSA_CMP_LEN, sb_start[None, :] + NSA_SEL_LEN)
        - jnp.maximum(cmp_start[:, None], sb_start[None, :]), 0).astype(jnp.float32) / NSA_CMP_LEN
    imp = jnp.einsum('bhtc,cj->btj', p_cmp, overlap)
    t_blk = t_pos[:, None] // NSA_SEL_LEN
    forced = (sb[None, :] == 0) | (sb[None, :] == t_blk) | (sb[None, :] == t_blk - 1)
    imp = jnp.where(forced, NSA_FORCED_SCORE, imp)
    imp = jnp.where(sb_start[None, :] <= t_pos[:, None], imp, NEG_INF)
    n_top = min(NSA_TOP_N, n_sb)
    _, sel_idx = lax.top_k(imp, n_top)
    k_blk = ks.reshape(B, n_sb, NSA_SEL_LEN, D)
    v_blk = vs.reshape(B, n_sb, NSA_SEL_LEN, D)

    def sel_block(i):
        start = i * Q_BLOCK
        qb = lax.dynamic_slice_in_dim(q, start, Q_BLOCK, axis=1)
        ib = lax.dynamic_slice_in_dim(sel_idx, start, Q_BLOCK, axis=1)
        kg = k_blk[bidx, ib].reshape(B, Q_BLOCK, n_top * NSA_SEL_LEN, D)
        vg = v_blk[bidx, ib].reshape(B, Q_BLOCK, n_top * NSA_SEL_LEN, D)
        qp = start + jnp.arange(Q_BLOCK)
        kpos = (ib[..., None] * NSA_SEL_LEN + jnp.arange(NSA_SEL_LEN)).reshape(B, Q_BLOCK, -1)
        mask = kpos <= qp[None, :, None]
        s = jnp.einsum('bqhd,bqmd->bhqm', qb, kg).astype(jnp.float32) * scale
        p = masked_softmax(s, mask[:, None])
        return jnp.einsum('bhqm,bqmd->bqhd', p.astype(vg.dtype), vg)

    o_sel = sweep_query_blocks(sel_block, S)

    kpad = jnp.pad(kw, ((0, 0), (NSA_WINDOW, 0), (0, 0)))
    vpad = jnp.pad(vw, ((0, 0), (NSA_WINDOW, 0), (0, 0)))

    def win_block(i):
        start = i * Q_BLOCK
        qb = lax.dynamic_slice_in_dim(q, start, Q_BLOCK, axis=1)
        kb = lax.dynamic_slice_in_dim(kpad, start, NSA_WINDOW + Q_BLOCK, axis=1)
        vb = lax.dynamic_slice_in_dim(vpad, start, NSA_WINDOW + Q_BLOCK, axis=1)
        kpos = start - NSA_WINDOW + jnp.arange(NSA_WINDOW + Q_BLOCK)
        qp = start + jnp.arange(Q_BLOCK)
        mask = ((kpos[None, :] <= qp[:, None]) & (kpos[None, :] > qp[:, None] - NSA_WINDOW)
                & (kpos[None, :] >= 0))
        s = jnp.einsum('bqhd,bkd->bhqk', qb, kb).astype(jnp.float32) * scale
        p = masked_softmax(s, mask)
        return jnp.einsum('bhqk,bkd->bqhd', p.astype(vb.dtype), vb)

    o_win = sweep_query_blocks(win_block, S)

    o = (g[:, :, 0, :, None] * o_cmp + g[:, :, 1, :, None] * o_sel
         + g[:, :, 2, :, None] * o_win)
    return o.reshape(B, S, H * D)

def fox_mixer(z, f_bias):
    B, S, _ = z.shape
    H, D = FOX_HEADS, HEAD_DIM
    q, k, v, f = split_cols(z, [H * D, H * D, H * D, H])
    log_f = jax.nn.log_sigmoid((f + f_bias).astype(jnp.float32))
    c = jnp.cumsum(log_f, axis=1)
    o = blocked_causal_attention(q.reshape(B, S, H, D), k.reshape(B, S, H, D),
                                 v.reshape(B, S, H, D), D ** -0.5, decay=c)
    return o.reshape(B, S, H * D)

def dsa_mixer(z, rope_head, rope_idx):
    B, S, _ = z.shape
    H, D = DSA_HEADS, HEAD_DIM
    q, k, v, qi, ki, w = split_cols(z, [H * D, D, D, IDX_HEADS * IDX_DIM, IDX_DIM, IDX_HEADS])
    q = apply_rope(q.reshape(B, S, H, D), rope_head)
    k = apply_rope(k, rope_head)
    qi = apply_rope(qi.reshape(B, S, IDX_HEADS, IDX_DIM), rope_idx)
    ki = apply_rope(ki, rope_idx)
    n_keep = min(DSA_TOP_K, S // DSA_KEEP_DIV)
    scale = D ** -0.5
    key_pos = jnp.arange(S)
    bidx = jnp.arange(B)[:, None, None]

    def one_block(i):
        start = i * Q_BLOCK
        qb = lax.dynamic_slice_in_dim(q, start, Q_BLOCK, axis=1)
        qib = lax.dynamic_slice_in_dim(qi, start, Q_BLOCK, axis=1)
        wb = lax.dynamic_slice_in_dim(w, start, Q_BLOCK, axis=1).astype(jnp.float32)
        logits = jnp.einsum('bqhd,bkd->bqhk', qib, ki).astype(jnp.float32) * IDX_DIM ** -0.5
        score = jnp.einsum('bqhk,bqh->bqk', jax.nn.relu(logits), wb) * IDX_HEADS ** -0.5
        qp = start + jnp.arange(Q_BLOCK)
        score = jnp.where(key_pos[None, None, :] <= qp[None, :, None], score, NEG_INF)
        _, idx = lax.top_k(score, n_keep)
        kg = k[bidx, idx]
        vg = v[bidx, idx]
        s = jnp.einsum('bqhd,bqkd->bhqk', qb, kg).astype(jnp.float32) * scale
        valid = idx <= qp[None, :, None]
        p = masked_softmax(s, valid[:, None])
        return jnp.einsum('bhqk,bqkd->bqhd', p.astype(vg.dtype), vg)

    o = sweep_query_blocks(one_block, S)
    return o.reshape(B, S, H * D)

def first_inputs(seed: int = 0) -> dict:
    key = jax.random.key(seed)
    ks = jax.random.split(key, 18)

    def nrm(k, shape, fan_in):
        return jax.random.normal(k, shape, jnp.float32) * fan_in ** -0.5

    def gain(k, shape):
        return 1.0 + 0.02 * jax.random.normal(k, shape, jnp.float32)

    x = jax.random.normal(ks[0], (BATCH, SEQ, D_MODEL), jnp.float32)
    offset = jax.random.randint(ks[1], (BATCH, 1), 0, POS_OFFSET_MAX, dtype=jnp.int32)
    positions = offset + jnp.arange(SEQ, dtype=jnp.int32)[None, :]
    return {
        "x": x,
        "positions": positions,
        "norm1_g": gain(ks[2], (DEPTH, D_MODEL)),
        "w_in": nrm(ks[3], (DEPTH, D_MODEL, IN_COLS), D_MODEL),
        "mla_q_norm_g": gain(ks[4], (DEPTH, MLA_Q_LORA)),
        "mla_w_uq": nrm(ks[5], (DEPTH, MLA_Q_LORA, MLA_HEADS * (MLA_NOPE + MLA_ROPE)), MLA_Q_LORA),
        "mla_kv_norm_g": gain(ks[6], (DEPTH, MLA_KV_LORA)),
        "mla_w_ukv": nrm(ks[7], (DEPTH, MLA_KV_LORA, MLA_HEADS * (MLA_NOPE + MLA_V)), MLA_KV_LORA),
        "nsa_cmp_pe": 0.1 * jax.random.normal(ks[8], (DEPTH, 2, NSA_CMP_LEN, HEAD_DIM), jnp.float32),
        "nsa_cmp_w": nrm(ks[9], (DEPTH, 2, NSA_CMP_LEN * HEAD_DIM, HEAD_DIM), NSA_CMP_LEN * HEAD_DIM),
        "fox_f_bias": 1.0 + 0.1 * jax.random.normal(ks[10], (DEPTH, FOX_HEADS), jnp.float32),
        "w_branch": nrm(ks[11], (DEPTH, N_BRANCH, BRANCH_W, D_MODEL), BRANCH_W),
        "w_out": nrm(ks[12], (DEPTH, D_MODEL, D_MODEL), D_MODEL),
        "norm2_g": gain(ks[13], (DEPTH, D_MODEL)),
        "w_up": nrm(ks[14], (DEPTH, D_MODEL, D_FF), D_MODEL),
        "w_down": nrm(ks[15], (DEPTH, D_FF, D_MODEL), D_FF),
        "final_g": gain(ks[16], (D_MODEL,)),
    }

def first_block(x, positions, norm1_g, w_in, mla_q_norm_g, mla_w_uq, mla_kv_norm_g, mla_w_ukv,
              nsa_cmp_pe, nsa_cmp_w, fox_f_bias, w_branch, w_out, norm2_g, w_up, w_down, final_g):
    B, S, _ = x.shape
    rope_mla = rope_tables(positions, MLA_ROPE)
    rope_head = rope_tables(positions, PARTIAL_ROT)
    rope_idx = rope_tables(positions, IDX_ROT)
    for l in range(DEPTH):
        h = rmsnorm(x, norm1_g[l])
        z = h @ w_in[l]
        z_mla, z_nsa, z_fox, z_dsa, z_gate = split_cols(
            z, [MLA_COLS, NSA_COLS, FOX_COLS, DSA_COLS, GATE_COLS])
        o_mla = mla_mixer(z_mla, mla_q_norm_g[l], mla_w_uq[l], mla_kv_norm_g[l], mla_w_ukv[l], rope_mla)
        o_nsa = nsa_mixer(z_nsa, nsa_cmp_w[l], nsa_cmp_pe[l], rope_head)
        o_fox = fox_mixer(z_fox, fox_f_bias[l])
        o_dsa = dsa_mixer(z_dsa, rope_head, rope_idx)
        branches = jnp.stack([o_mla, o_nsa, o_fox, o_dsa], axis=2)
        lifted = jnp.einsum('bsnc,ncd->bsnd', branches, w_branch[l])
        gates = jax.nn.sigmoid(z_gate.reshape(B, S, N_BRANCH, D_MODEL))
        mixed = jnp.sum(gates * lifted, axis=2)
        x = x + mixed @ w_out[l]
        h2 = rmsnorm(x, norm2_g[l])
        x = x + jnp.square(jax.nn.relu(h2 @ w_up[l])) @ w_down[l]
    return rmsnorm(x, final_g)


D_MIX = D_MODEL
CONV_DIM = D_MIX // 2
CONV_GROUPS = 8
CONV_WIDTH = 31
GLA_HEADS = 4
GLA_VAL_DIM = D_MIX // 2
GLA_HEAD_V = GLA_VAL_DIM // GLA_HEADS
GLA_KEY_DIM = GLA_VAL_DIM // 2
GLA_HEAD_K = GLA_KEY_DIM // GLA_HEADS
GATE_RANK = 16
GATE_TAU = 16.0
GLA_CHUNK = 64
IN_COLS_2 = 2 * CONV_DIM + 2 * GLA_KEY_DIM + 2 * GLA_VAL_DIM + GATE_RANK
MEM_LEN = 256
X_HEADS = 4
X_HEAD_DIM = D_MODEL // X_HEADS
D_FF_2 = int(math.ceil(8 * D_MODEL / 3 / 256) * 256)
DEEPNORM_ALPHA = (2 * DEPTH) ** 0.25
DEEPNORM_BETA = (8 * DEPTH) ** -0.25
LN_EPS = 1e-5


def layer_norm(x, g, b):
    xf = x.astype(jnp.float32)
    mu = jnp.mean(xf, axis=-1, keepdims=True)
    xc = xf - mu
    var = jnp.mean(xc * xc, axis=-1, keepdims=True)
    return (xc * lax.rsqrt(var + LN_EPS) * g.astype(jnp.float32) + b.astype(jnp.float32)).astype(x.dtype)

def rms_norm(x, g):
    xf = x.astype(jnp.float32)
    ms = jnp.mean(xf * xf, axis=-1, keepdims=True)
    return (xf * lax.rsqrt(ms + LN_EPS) * g.astype(jnp.float32)).astype(x.dtype)

def causal_depthwise_conv(u, w, b):
    c = u.shape[-1]
    y = lax.conv_general_dilated(
        u, w[:, None, :].astype(u.dtype), window_strides=(1,),
        padding=[(w.shape[0] - 1, 0)],
        dimension_numbers=("NWC", "WIO", "NWC"),
        feature_group_count=c)
    return y + b

def gla_chunked(q, k, v, log_a):
    out_dtype = v.dtype
    bsz, t, h, dk = q.shape
    dv = v.shape[-1]
    n = t // GLA_CHUNK

    def to_chunks(z):
        return z.astype(jnp.float32).reshape(bsz, n, GLA_CHUNK, h, z.shape[-1]).transpose(0, 3, 1, 2, 4)

    qc = to_chunks(q) * (dk ** -0.5)
    kc, vc, gc = to_chunks(k), to_chunks(v), to_chunks(log_a)
    bcum = jnp.cumsum(gc, axis=3)
    b_last = bcum[:, :, :, -1:, :]
    qe = qc * jnp.exp(bcum)
    ke = kc * jnp.exp(-bcum)
    kd = kc * jnp.exp(b_last - bcum)
    causal = jnp.tril(jnp.ones((GLA_CHUNK, GLA_CHUNK), dtype=bool))
    att = jnp.einsum("bhncd,bhnsd->bhncs", qe, ke)
    att = jnp.where(causal, att, 0.0)
    o_intra = jnp.einsum("bhncs,bhnse->bhnce", att, vc)
    upd = jnp.einsum("bhncd,bhnce->bhnde", kd, vc)
    decay = jnp.exp(b_last[:, :, :, 0, :])

    def step(state, inp):
        dec, u = inp
        return dec[..., None] * state + u, state

    s0 = jnp.zeros((bsz, h, dk, dv), jnp.float32)
    _, s_prev = lax.scan(step, s0, (jnp.moveaxis(decay, 2, 0), jnp.moveaxis(upd, 2, 0)))
    s_prev = jnp.moveaxis(s_prev, 0, 2)
    o_inter = jnp.einsum("bhncd,bhnde->bhnce", qe, s_prev)
    o = (o_intra + o_inter).transpose(0, 2, 3, 1, 4).reshape(bsz, t, h, dv)
    return o.astype(out_dtype)

def hybrid_mixer(h, w_in, w_a2, b_a, conv_w, conv_b, conv_ln_g, conv_ln_b, gla_norm_g, w_out):
    bsz, t, _ = h.shape
    proj = h @ w_in
    cuts = np.cumsum([CONV_DIM, CONV_DIM, GLA_KEY_DIM, GLA_KEY_DIM, GLA_VAL_DIM, GLA_VAL_DIM]).tolist()
    c_a, c_g, q, k, v, r, a_low = jnp.split(proj, cuts, axis=-1)
    u = c_a * jax.nn.sigmoid(c_g)
    u = causal_depthwise_conv(u, conv_w, conv_b)
    u = jax.nn.silu(layer_norm(u, conv_ln_g, conv_ln_b))
    z = a_low @ w_a2 + b_a
    log_a = jax.nn.log_sigmoid(z.astype(jnp.float32)) / GATE_TAU
    heads = lambda y, d: y.reshape(bsz, t, GLA_HEADS, d)
    o = gla_chunked(heads(q, GLA_HEAD_K), heads(k, GLA_HEAD_K), heads(v, GLA_HEAD_V),
                    heads(log_a, GLA_HEAD_K))
    o = rms_norm(o, gla_norm_g) * jax.nn.silu(heads(r, GLA_HEAD_V))
    o = o.reshape(bsz, t, GLA_VAL_DIM)
    return jnp.concatenate([u, o], axis=-1) @ w_out

def memory_cross_attention(x, mem, w_q, w_kv, w_o):
    bsz, t, _ = x.shape
    q = (x @ w_q).reshape(bsz, t, X_HEADS, X_HEAD_DIM)
    kv = mem @ w_kv
    k, v = jnp.split(kv, 2, axis=-1)
    k = k.reshape(bsz, MEM_LEN, X_HEADS, X_HEAD_DIM)
    v = v.reshape(bsz, MEM_LEN, X_HEADS, X_HEAD_DIM)
    s = jnp.einsum("bthd,bmhd->bhtm", q.astype(jnp.float32), k.astype(jnp.float32)) * (X_HEAD_DIM ** -0.5)
    p = jax.nn.softmax(s, axis=-1).astype(v.dtype)
    o = jnp.einsum("bhtm,bmhd->bthd", p, v).reshape(bsz, t, D_MODEL)
    return o @ w_o

def swiglu(x, w_in, w_out):
    g, u = jnp.split(x @ w_in, 2, axis=-1)
    return (jax.nn.silu(g) * u) @ w_out

def second_inputs(seed: int = 0) -> dict:
    key = jax.random.key(seed)
    ks = jax.random.split(key, 24)
    nrm = lambda k, shape, scale: jax.random.normal(k, shape, jnp.float32) * scale
    gain = lambda k, shape: 1.0 + nrm(k, shape, 0.02)
    L = DEPTH
    return {
        "x": nrm(ks[0], (BATCH, SEQ, D_MODEL), 1.0),
        "mem": nrm(ks[1], (BATCH, MEM_LEN, D_MODEL), 1.0),
        "ln0_g": gain(ks[2], (D_MODEL,)),
        "ln0_b": nrm(ks[3], (D_MODEL,), 0.02),
        "w_in": nrm(ks[4], (L, D_MODEL, IN_COLS_2), D_MODEL ** -0.5),
        "w_a2": nrm(ks[5], (L, GATE_RANK, GLA_KEY_DIM), GATE_RANK ** -0.5),
        "b_a": nrm(ks[6], (L, GLA_KEY_DIM), 0.01),
        "conv_w": nrm(ks[7], (L, CONV_WIDTH, CONV_DIM), CONV_WIDTH ** -0.5),
        "conv_b": nrm(ks[8], (L, CONV_DIM), 0.02),
        "conv_ln_g": gain(ks[9], (L, CONV_DIM)),
        "conv_ln_b": nrm(ks[10], (L, CONV_DIM), 0.02),
        "gla_norm_g": gain(ks[11], (L, GLA_HEAD_V)),
        "w_mix_out": nrm(ks[12], (L, D_MIX, D_MODEL), DEEPNORM_BETA * D_MIX ** -0.5),
        "ln1_g": gain(ks[13], (L, D_MODEL)),
        "ln1_b": nrm(ks[14], (L, D_MODEL), 0.02),
        "w_xq": nrm(ks[15], (L, D_MODEL, D_MODEL), D_MODEL ** -0.5),
        "w_xkv": jnp.concatenate([
            nrm(ks[16], (L, D_MODEL, D_MODEL), D_MODEL ** -0.5),
            nrm(jax.random.fold_in(ks[16], 1), (L, D_MODEL, D_MODEL), DEEPNORM_BETA * D_MODEL ** -0.5)], axis=-1),
        "w_xo": nrm(ks[17], (L, D_MODEL, D_MODEL), DEEPNORM_BETA * D_MODEL ** -0.5),
        "ln2_g": gain(ks[18], (L, D_MODEL)),
        "ln2_b": nrm(ks[19], (L, D_MODEL), 0.02),
        "w_ffn_in": nrm(ks[20], (L, D_MODEL, 2 * D_FF_2), D_MODEL ** -0.5),
        "w_ffn_out": nrm(ks[21], (L, D_FF_2, D_MODEL), DEEPNORM_BETA * D_FF_2 ** -0.5),
        "ln3_g": gain(ks[22], (L, D_MODEL)),
        "ln3_b": nrm(ks[23], (L, D_MODEL), 0.02),
    }

def second_block(x, mem, ln0_g, ln0_b, w_in, w_a2, b_a, conv_w, conv_b, conv_ln_g, conv_ln_b,
              gla_norm_g, w_mix_out, ln1_g, ln1_b, w_xq, w_xkv, w_xo, ln2_g, ln2_b,
              w_ffn_in, w_ffn_out, ln3_g, ln3_b):
    h = layer_norm(x, ln0_g, ln0_b)
    for l in range(DEPTH):
        mix = hybrid_mixer(h, w_in[l], w_a2[l], b_a[l], conv_w[l], conv_b[l], conv_ln_g[l],
                           conv_ln_b[l], gla_norm_g[l], w_mix_out[l])
        h = layer_norm(DEEPNORM_ALPHA * h + mix, ln1_g[l], ln1_b[l])
        xa = memory_cross_attention(h, mem, w_xq[l], w_xkv[l], w_xo[l])
        h = layer_norm(DEEPNORM_ALPHA * h + xa, ln2_g[l], ln2_b[l])
        ff = swiglu(h, w_ffn_in[l], w_ffn_out[l])
        h = layer_norm(DEEPNORM_ALPHA * h + ff, ln3_g[l], ln3_b[l])
    return h


def setup_inputs(seed=0):
    out = dict(first_inputs(seed))
    for name, value in second_inputs(seed + 1).items():
        if name != "x":
            out[name + "_2"] = value
    return out


def reference(
    x, positions, norm1_g, w_in, mla_q_norm_g, mla_w_uq, mla_kv_norm_g, mla_w_ukv, nsa_cmp_pe,
    nsa_cmp_w, fox_f_bias, w_branch, w_out, norm2_g, w_up, w_down, final_g, mem_2, ln0_g_2,
    ln0_b_2, w_in_2, w_a2_2, b_a_2, conv_w_2, conv_b_2, conv_ln_g_2, conv_ln_b_2, gla_norm_g_2,
    w_mix_out_2, ln1_g_2, ln1_b_2, w_xq_2, w_xkv_2, w_xo_2, ln2_g_2, ln2_b_2, w_ffn_in_2,
    w_ffn_out_2, ln3_g_2, ln3_b_2,
):
    x = first_block(
        x, positions, norm1_g, w_in, mla_q_norm_g, mla_w_uq, mla_kv_norm_g, mla_w_ukv,
        nsa_cmp_pe, nsa_cmp_w, fox_f_bias, w_branch, w_out, norm2_g, w_up, w_down, final_g,
    )
    return second_block(
        x, mem_2, ln0_g_2, ln0_b_2, w_in_2, w_a2_2, b_a_2, conv_w_2, conv_b_2, conv_ln_g_2,
        conv_ln_b_2, gla_norm_g_2, w_mix_out_2, ln1_g_2, ln1_b_2, w_xq_2, w_xkv_2, w_xo_2,
        ln2_g_2, ln2_b_2, w_ffn_in_2, w_ffn_out_2, ln3_g_2, ln3_b_2,
    )


_drawn_inputs = setup_inputs


def setup_inputs(seed=0):
    import zlib

    import numpy as np

    out = dict(_drawn_inputs(seed))
    spreads = {}
    factors = {'mla_q_norm_g': 8.0,
     'mla_kv_norm_g': 8.0,
     'fox_f_bias': 3.611,
     'b_a_2': 8.0,
     'conv_b_2': 5.669,
     'conv_ln_g_2': 8.0,
     'conv_ln_b_2': 8.0,
     'gla_norm_g_2': 8.0}
    for name, (base, spread) in spreads.items():
        noise = np.random.default_rng([zlib.crc32(name.encode()), seed]).standard_normal(out[name].shape)
        drawn = base * np.exp(spread * noise) if base else spread * noise
        out[name] = __import__('jax').numpy.asarray(drawn.astype(out[name].dtype))
    for name, factor in factors.items():
        out[name] = (out[name] * factor).astype(out[name].dtype)
    return out
```

```python
from contextlib import ExitStack

import numpy as np

import concourse.bass as bass
from concourse import mybir

F32 = mybir.dt.float32
I32 = mybir.dt.int32
ALU = mybir.AluOpType
ACT = mybir.ActivationFunctionType
AX = mybir.AxisListType.X

P = 128
SEQ = 256
T = SEQ // P
D = 1024
KT = D // P
HEADS = 4
HD = 64
MASKED = -1e30
TAKEN = -3e38
BANK = 512

MLA_Q, MLA_KV, MLA_R = 256, 128, 32
MLA_HD = HD + MLA_R
MLA0 = 0
NSA0 = MLA_Q + MLA_KV + MLA_R
FOX0 = NSA0 + 4 * HD + 6 * HD + 12
DSA0 = FOX0 + 3 * HEADS * HD + HEADS
GATE0 = DSA0 + 4 * HD + 2 * HD + 8 * 32 + 32 + 8
IN1 = GATE0 + 4 * D
NSA_Q, NSA_KC, NSA_VC, NSA_KS, NSA_VS, NSA_KW, NSA_VW, NSA_G = [NSA0 + c for c in (0, 256, 320, 384, 448, 512, 576, 640)]
FOX_Q, FOX_K, FOX_V, FOX_F = [FOX0 + c for c in (0, 256, 512, 768)]
DSA_Q, DSA_K, DSA_V, DSA_QI, DSA_KI, DSA_W = [DSA0 + c for c in (0, 256, 320, 384, 640, 672)]
IDX_HEADS, IDX_DIM, KEEP = 8, 32, 64
CMP_LEN, CMP_STRIDE = 32, 16
NCMP = (SEQ - CMP_LEN) // CMP_STRIDE + 1
CMP_PAIRS = CMP_LEN // 2
D_FF = 4096
ROPES = ((0, 16), (16, 8), (24, 4))
NFREQ = 28
THETA = 500000.0
NORM_EPS = 1e-6

CONV = 512
TAPS = 31
PAD = TAPS - 1
CT = CONV // P
GK, GV = 256, 512
RANK = 16
CHUNK = 64
DFF2 = 2816
FT2 = DFF2 // P
XH, XD = 4, 256
IN2 = 2 * CONV + 2 * GK + 2 * GV + RANK
ALPHA = 4 ** 0.25
LN_EPS = 1e-5
SLOTS = 4
ARENA = 27700
ROUND = 1.5 * 2 ** 23
TWO_PI = (6.28125, 0.0019350051879882812, 3.019915981956752e-07)
PI_BELOW = 3.1415925

S_NSA_Q, S_KS, S_KW, S_DSA_Q, S_DSA_K, S_KI, S_QI, S_KC, S_VC, S_FOX_Q, S_FOX_K, S_MLA_Q, S_MLA_K = 0, 2, 3, 4, 6, 7, 8, 10, 11, 12, 14, 16, 20
N_ATT_T = 24
BY_SLOT = (0, 2, 1, 3)


def cmp_final(l, t):
    return T * l + t + 1


class Turns:

    def __init__(self, banks, plan, filled, moved):
        self.banks, self.plan, self.filled, self.moved = banks, plan, filled, moved
        self.at = {key: u for u, (key, _) in enumerate(plan)}
        self.count, seen = [], {}
        for _, engine in plan:
            seen[engine] = seen.get(engine, 0) + 1
            self.count.append(seen[engine])
        assert len(self.at) == len(plan)

    def bank(self, key):
        return self.banks[self.at[key] % len(self.banks)]

    def open(self, pe, key):
        u = self.at[key] - len(self.banks)
        if u >= 0:
            pe.wait_ge(self.moved[self.plan[u][1]], self.count[u])
        return self.bank(key)

    def wait_filled(self, eng, key):
        eng.wait_ge(self.filled, self.at[key] + 1)
        return self.bank(key)

    def wait_moved(self, eng, key):
        u = self.at[key]
        eng.wait_ge(self.moved[self.plan[u][1]], self.count[u])


class Chain:

    def __init__(self, eng, sem):
        self.eng, self.sem, self.n = eng, sem, 0

    def __call__(self, ins):
        self.n += 1
        ins.then_inc(self.sem, 1)

    def settle(self, but=0):
        if self.n > but:
            self.eng.wait_ge(self.sem, self.n - but)


PATHS1 = [("fox", 0), ("fox", 1), ("win", 0), ("win", 1), ("mla", 0), ("mla", 1), ("sel", 0), ("sel", 1),
          ("cmp", 0), ("cmp", 1), ("dsa", 0), ("dsa", 1)]
BRANCH = {"mla": 0, "sel": 1, "win": 1, "cmp": 1, "fox": 2, "dsa": 3}
SCALE = {"mla": MLA_HD ** -0.5, "sel": HD ** -0.5, "win": HD ** -0.5, "cmp": HD ** -0.5, "fox": HD ** -0.5, "dsa": HD ** -0.5}
GATE_TILES = 4 * D // BANK
GATES_AFTER = [1, 1, 1, 1, 1, 1, 1, 1, 1, 1, 2, 2]
Z_TILES = [(j * BANK, min(BANK, GATE0 - j * BANK)) for j in range(-(-GATE0 // BANK))]


def plans(L1, L2):
    lin, small = [], []
    for l in range(L1):
        small += [(("n1", l, t, f), "dve") for t in range(T) for f in range(2)]
        lin += [(("z", l, j, t), "act") for j in range(3) for t in range(T)]
        small += [(("cT", l, t), "dve") for t in range(T)]
        lin += [(("z", l, 3, t), "act") for t in range(T)]
        lin += [((w, l, t), "act") for t in range(T) for w in ("uq", "ukv")]
        lin += [(("z", l, 4, t), "act") for t in range(T)]
        small += [(("cq", l), "dve")]
        lin += [(("ck", l, f), "dve") for f in range(2)]
        small += [((w, l, t), "act") for w in ("foxT", "nsa", "idx") for t in range(T)]
        lin += [(("gate", l, 0, t), "act") for t in range(T)]
        small += [(("comp", l), "dve")]
        small += [((w, l, t), "act") for w in ("mq", "mk", "dsa") for t in range(T)]
        lin += [(("idx", l, t, f), "act") for t in range(T) for f in range(4)]
        g = 2
        for i, (path, t) in enumerate(PATHS1):
            for _ in range(GATES_AFTER[i] if i else 1):
                if g < 2 * GATE_TILES:
                    lin.append((("gate", l, g // 2, g % 2), "act"))
                    g += 1
            small += [(("PT", l, i, kb), "act") for kb in range(1 if path == "cmp" else t + 1)]
            small += [(("PV", l, i), "dve")]
        assert g == 2 * GATE_TILES
        small += [(("oT", l, b), "act") for b in range(4)]
        lin += [(("lift", l, f, b, t), "dve") for f in range(2) for b in range(4) for t in range(T)]
        small += [(("mixT", l, t, f), "act") for t in range(T) for f in range(2)]
        lin += [(("out", l, f, t), "dve") for f in range(2) for t in range(T)]
        small += [(("n2", l, t, f), "dve") for t in range(T) for f in range(2)]
        lin += [(("up", l, j, b), "act") for j in range(D_FF // BANK) for b in range(2)]
        lin += [(("down", l, t, f), "dve") for t in range(T) for f in range(2)]
    small += [(("memT", t, f), "act") for t in range(T) for f in range(2)]
    for l in range(L2):
        small += [(("hT", l, t, f), "act") for t in range(T) for f in range(2)]
        small += [(("alow", l), "act")]
        lin += [(("cg", l, t), "act") for t in range(T)]
        lin += [(("ca", l, t), "dve") for t in range(T)]
        small += [(("uT", l, t), "act") for t in range(T)]
        small += [(("zlow", l, t), "dve") for t in range(T)]
        lin += [(("qk", l, t), "act") for t in range(T)]
        lin += [(("v", l, t), "act") for t in range(T)]
        lin += [(("bc", l, t), "act") for t in range(T)]
        small += [(("blast", l), "act")]
        lin += [(("r", l, t), "dve") for t in range(T)]
        small += [(("qeT", l, t), "act") for t in range(T)]
        lin += [(("att", l, t, e), "dve") for t in range(T) for e in range(2)]
        lin += [(("upd", l, c), "dve") for c in range(3)]
        lin += [(("xk", l, b), "act") for b in range(4)]
        lin += [(("xv", l, f, t), "act") for f in range(2) for t in range(T)]
        lin += [(("go", l, t, e), "dve") for t in range(T) for e in range(2)]
        small += [(("goT", l, t), "act") for t in range(T)]
        small += [(("cmean", l), "dve"), (("cvar", l), "dve")]
        lin += [(("mix", l, f, t), "dve") for f in range(2) for t in range(T)]
        small += [(("h1T", l, t, f), "act") for t in range(T) for f in range(2)]
        lin += [(("xq", l, b), "act") for b in range(4)]
        for t in range(T):
            small += [(("xPT", l, t, m), "act") for m in range(2)]
            lin += [(("xO", l, t, f), "act") for f in range(2)]
        lin += [(("xo", l, f, t), "dve") for f in range(2) for t in range(T)]
        small += [(("h2T", l, t, f), "act") for t in range(T) for f in range(2)]
        lin += [(("ffn", l, f), "dve") for f in range(FT2)]
        lin += [(("ffo", l, t, f), "dve") for t in range(T) for f in range(2)]
    return lin, small


def two_decoders(nc, a, out, L1=2, L2=2):
    ctx = ExitStack()
    with ctx:
        def sb(name, shape, dt=F32):
            return ctx.enter_context(nc.sbuf_tensor(name, shape, dt))

        def sem(name):
            return ctx.enter_context(nc.semaphore(name))

        LAYERS = a["w_in"].shape[0]
        ring = sb("ring", [P, SLOTS, KT * BANK])
        x = sb("x", [P, T, D])
        hn = sb("hn", [P, T, D])
        hT = sb("hT", [P, KT, SEQ])
        ident = sb("ident", [P, P])
        causal = sb("causal", [P, SEQ])
        upto = sb("upto", [P, SEQ])
        ones = upto[:, P:SEQ]
        cmp_bias = sb("cmp_bias", [P, T, NCMP])
        cmp_keep = sb("cmp_keep", [P, T, NCMP])
        blk_upto = sb("blk_upto", [P, P])
        blk_after = sb("blk_after", [P, P])
        blk_sum = sb("blk_sum", [P, 2])
        minus_half = sb("minus_half", [P, 1])
        N_NORMS = 3 * L1 + 2 + 5 * L2
        stats = sb("stats", [P, N_NORMS, 16])
        softmax_s = sb("softmax_s", [P, 2, 4, HEADS])
        g1 = sb("g1", [P, 2, LAYERS, KT])
        gqkv = sb("gqkv", [P, LAYERS, 3])
        fbias = sb("fbias", [P, LAYERS, HEADS])
        peT = sb("peT", [P, LAYERS, 2, CMP_PAIRS])
        conv_wT = sb("conv_wT", [P, LAYERS, CT, TAPS])
        conv_p = sb("conv_p", [P, 3, LAYERS, CT])
        gla_g = sb("gla_g", [P, LAYERS, P])
        wa2 = sb("wa2", [32, LAYERS, GK])
        pos_i = sb("pos_i", [P, T], I32)
        pos_f = sb("pos_f", [P, T])
        freq = sb("freq", [P, NFREQ])
        ang = sb("ang", [P, T, NFREQ])
        red = sb("red", [P, 2, T, NFREQ])
        halves = sb("halves", [P, T, 2, 6])
        turns = sb("turns", [P, 2, T, NFREQ])
        rope = sb("rope", [P, 2, T, NFREQ])
        arena = sb("arena", [P, ARENA])

        def cut(lo, n, pattern=None, **sizes):
            v = arena[:, lo:lo + n]
            return v.rearrange(pattern, **sizes) if pattern else v

        z = cut(0, T * GATE0, "p (t n) -> p t n", t=T)
        GATE_AT = T * GATE0
        gate = cut(GATE_AT, T * 4 * D, "p (t n) -> p t n", t=T)
        PROBS_AT = GATE_AT + T * 4 * D
        probs = cut(PROBS_AT, 2 * HEADS * SEQ, "p (b h k) -> p b h k", b=2, h=HEADS)
        PT_AT = PROBS_AT + 2 * HEADS * SEQ
        PT = cut(PT_AT, 2 * T * HEADS * P, "p (b m h q) -> p b m h q", b=2, m=T, h=HEADS)
        ATT_AT = PT_AT + 2 * T * HEADS * P
        attT = cut(ATT_AT, N_ATT_T * SEQ, "p (s q) -> p s q", s=N_ATT_T)
        MORE = ATT_AT + N_ATT_T * SEQ
        mv = cut(MORE, T * 256, "p (t n) -> p t n", t=T)
        d8 = [cut(MORE + 512, 512, "p (h k) -> p h k", h=HEADS), cut(MORE + 1024, 1024, "p (h k) -> p h k", h=HEADS)]
        index_bias = [cut(MORE + 2048, P), cut(MORE + 2048 + P, SEQ)]
        cmpR = cut(MORE + 2432, 2 * CMP_PAIRS * NCMP, "p (w a c) -> p w a c", w=2, a=CMP_PAIRS)
        kcmpT = cut(MORE + 2912, NCMP)
        vcmp = cut(MORE + 2928, HD)
        lf = cut(MORE + 2992, 3 * T * HEADS, "p (s t h) -> p s t h", s=3, t=T)
        cq8 = cut(MORE + 3016, T * HEADS, "p (t h) -> p t h", t=T)
        gn = cut(MORE + 3024, T * 12, "p (t g) -> p t g", t=T)
        best = cut(MORE + 3048, 8)
        cT = cut(MORE + 3312, 3 * SEQ, "p (k s) -> p k s", k=3)
        otmp = cut(MORE + 3056, 256, "p (h d) -> p h d", h=HEADS)
        LATE = 4 * D - 3 * BANK
        mqk = cut(GATE_AT + 4 * D + LATE, 3 * BANK, "p (t h d) -> p t h d", t=T, h=8)
        rope_tmp = cut(GATE_AT + LATE, 4 * P, "p (s n) -> p s n", s=4)
        relu_l = cut(GATE_AT + LATE + 512, 2 * 2 * SEQ, "p (b h k) -> p b h k", b=2, h=2)
        stage = cut(PT_AT, T * 6 * P, "p (t s n) -> p t s n", t=T, s=6)
        decay_rows = [cut(PROBS_AT, HEADS * SEQ, "p (h k) -> p h k", h=HEADS), cut(PROBS_AT + HEADS * SEQ, HEADS * P, "p (h k) -> p h k", h=HEADS)]
        osb = hn[:, :, :].rearrange("p t (b h d) -> p t b h d", b=4, h=HEADS)
        upT = cut(GATE_AT, T * 4 * D, "p (k s) -> p k s", s=SEQ)
        lng = cut(0, 4 * D, "p (b w n) -> p b w n", b=2, w=2)
        memT = cut(4096, 2048, "p (k s) -> p k s", s=SEQ)
        xkT = cut(6144, 2048, "p (k s) -> p k s", s=SEQ)
        xv = cut(8192, 2048, "p (t n) -> p t n", t=T)
        qez = cut(10240, 1024, "p (g c k) -> p g c k", g=2, c=4)
        gattT = cut(11264, 1024, "p (t h c) -> p t h c", t=T, h=HEADS)
        state = cut(12288, 768, "p (c g e) -> p c g e", c=3, g=2)
        dec = cut(13056, 8, "p (g c) -> p g c", g=2)
        qeT = cut(PROBS_AT, 512, "p (g s) -> p g s", g=2)
        keT = cut(PROBS_AT + 512, 512, "p (g s) -> p g s", g=2)
        alT = arena[0:32, PROBS_AT + 1024:PROBS_AT + 1024 + SEQ]
        mean_c = cut(PT_AT, SEQ)
        var_c = cut(PT_AT + SEQ, SEQ)
        rstd_c = cut(PT_AT + 2 * SEQ, SEQ)
        gla_junk = cut(PT_AT + 1024, P)
        Z2 = ATT_AT
        u2 = cut(Z2, 1024, "p (t n) -> p t n", t=T)
        go2 = u2
        sg2 = cut(Z2 + 1024, 1024, "p (t n) -> p t n", t=T)
        sq2 = cut(Z2 + 1024, 1024, "p (c s) -> p c s", c=CT)
        la = cut(Z2 + 2048, 1536, "p (s t n) -> p s t n", s=3, t=T)
        ex2 = cut(Z2 + 3584, 1536, "p (s t n) -> p s t n", s=3, t=T)
        sr2 = cut(Z2 + 5120, 1024, "p (t n) -> p t n", t=T)
        v2 = cut(Z2 + 6144, 1024, "p (t n) -> p t n", t=T)
        qk2 = cut(Z2 + 7168, 1024, "p (t n) -> p t n", t=T)
        ffT = cut(Z2, FT2 * SEQ, "p (k s) -> p k s", s=SEQ)
        xqT = cut(Z2 + 6144, 2048, "p (k s) -> p k s", s=SEQ)
        uT = cut(Z2 + 8192, CT * (PAD + SEQ), "p (c s) -> p c s", c=CT)
        acc = cut(Z2 + 8192 + CT * (PAD + SEQ), CT * SEQ, "p (c s) -> p c s", c=CT)
        ffs = cut(Z2 + 8192 + CT * (PAD + SEQ), 512, "p (b s) -> p b s", b=2)

        ps = ctx.enter_context(nc.psum_tensor("ps", [P, 8, BANK], F32))
        scores = ps[:, 6:8, :].rearrange("p b (h k) -> p (b h) k", h=2)

        lin_plan, small_plan = plans(L1, L2)
        lin = Turns([ps[:, b, :] for b in range(4)], lin_plan, sem("lin_filled"), {e: sem(f"lin_moved_by_{e}") for e in ("act", "dve")})
        small = Turns([ps[:, b, :] for b in (4, 5)], small_plan, sem("small_filled"), {e: sem(f"small_moved_by_{e}") for e in ("act", "dve")})
        slot_loaded = [sem(f"slot_loaded_{i}") for i in range(SLOTS)]
        long_used = sem("long_sum_tiles_used")
        x_loaded = sem("x_loaded")
        pos_loaded = sem("pos_loaded")
        params_loaded = sem("params_loaded")
        params2_loaded = sem("params2_loaded")
        consts_made = sem("consts_made")
        angles_made = sem("angles_made")
        rope_tables = sem("rope_tables")
        squares_summed = sem("squares_summed")
        mean_ready = sem("mean_ready")
        rstd_ready = sem("rstd_ready")
        normed = sem("normed")
        fox_logits = sem("fox_logits")
        fox_log = sem("fox_log")
        decay_ready = sem("decay_rows_ready")
        staged = sem("staged")
        mla_roped = sem("mla_roped")
        cmp_rows = sem("cmp_rows")
        nsa_tanh = sem("nsa_tanh")
        index_used = sem("index_logits_used")
        scores_filled = sem("scores_filled")
        bias_ready = sem("softmax_bias_ready")
        probs_made = sem("probs_made")
        probs_final = sem("probs_final")
        gated = sem("gates_summed")
        squared = sem("up_squared")
        x_updated = sem("x_updated")
        mem_loaded = sem("mem_loaded")
        lng_loaded = [sem(f"gains_loaded_{i}") for i in range(2)]
        pads_zeroed = sem("pads_zeroed")
        low_log = sem("low_log")
        la_ready = sem("la_ready")
        decays_exp = sem("decays_exp")
        r_tanh = sem("r_tanh")
        cg_tanh = sem("cg_tanh")
        ff_tanh = sem("ff_tanh")
        qkd_ready = sem("qkd_ready")
        state_ready = sem("state_ready")
        go_moved = sem("go_moved")
        go_ready = sem("go_ready")
        conv_summed = sem("conv_summed")
        conv_centred = sem("conv_centred")
        conv_squared = sem("conv_squared")
        conv_var = sem("conv_var")
        conv_affine = sem("conv_affine")
        conv_tanh = sem("conv_tanh")
        conv_out = sem("conv_out")
        u_ready = sem("u_ready")
        dve_step, act_step, pool_step = sem("dve_step"), sem("act_step"), sem("pool_step")
        stored = sem("stored")

        stream = []

        def slot_of(n):
            return ring[:, n % SLOTS, :]

        def rows(w, n0, nn, k0=0, kn=KT):
            return w[k0 * P:(k0 + kn) * P, n0:n0 + nn].rearrange("(k p) n -> p k n", p=P)

        def view(n, kn, nn, off=0):
            return slot_of(n)[:, off:off + kn * nn].rearrange("p (k n) -> p k n", k=kn)

        def tile(key, parts, last):
            stream.append((key, parts, last))

        def whole(key, w, n0, nn, last, k0=0, kn=KT):
            tile(key, [(view(len(stream), kn, nn), rows(w, n0, nn, k0, kn))], last)

        for l in range(L1):
            w_in = a["w_in"][l]
            for j, (c0, cn) in enumerate(Z_TILES[:4]):
                whole(("z", l, j), w_in, c0, cn, (lin, ("z", l, j, 1)))
            n = len(stream)
            tile(("u", l), [(view(n, 2, 384), rows(a["mla_w_uq"][l], 0, 384, 0, 2)),
                            (view(n, 1, 512, 768), rows(a["mla_w_ukv"][l], 0, 512, 0, 1))], (lin, ("ukv", l, 1)))
            whole(("z", l, 4), w_in, *Z_TILES[4], (lin, ("z", l, 4, 1)))
            whole(("gate", l, 0), w_in, GATE0, BANK, (lin, ("gate", l, 0, 1)))
            slot = slot_of(len(stream))
            ck = a["nsa_cmp_w"][l, 0].rearrange("(a p) e -> p a e", p=P)
            cv = a["nsa_cmp_w"][l, 1].rearrange("(a p) e -> p a e", p=P)
            kd = slot[:, 0:CMP_PAIRS * P].rearrange("p (a e) -> p a e", e=P)
            vd = slot[:, CMP_PAIRS * P:CMP_PAIRS * (P + HD)].rearrange("p (a e) -> p a e", e=HD)
            tile(("cmp", l), [(kd[:, :, 0:HD], ck), (kd[:, :, HD:P], ck), (vd, cv)], (small, ("comp", l)))
            for j in range(1, GATE_TILES):
                whole(("gate", l, j), w_in, GATE0 + j * BANK, BANK, (lin, ("gate", l, j, 1)))
            w_br = a["w_branch"][l].rearrange("b (c p) n -> p (b c) n", p=P)
            for f in range(2):
                tile(("lift", l, f), [(view(len(stream), KT, BANK), w_br[:, :, f * BANK:(f + 1) * BANK])], (lin, ("lift", l, f, 3, 1)))
            for f in range(2):
                whole(("out", l, f), a["w_out"][l], f * BANK, BANK, (lin, ("out", l, f, 1)))
            for j in range(D_FF // BANK):
                whole(("up", l, j), a["w_up"][l], j * BANK, BANK, (lin, ("up", l, j, 1)))
            for j in range(D_FF // BANK):
                whole(("down", l, j), a["w_down"][l], 0, D, None if j + 1 < D_FF // BANK else (lin, ("down", l, 1, 1)), 4 * j, 4)
        for l in range(L2):
            w2 = a["w_in_2"][l]
            whole(("alow", l), w2, IN2 - RANK, RANK, (small, ("alow", l)))
            for key, c0 in (("cg", CONV), ("ca", 0), ("qk", 2 * CONV), ("v", 2 * CONV + 2 * GK), ("r", 2 * CONV + 2 * GK + GV)):
                whole((key, l), w2, c0, BANK, (lin, (key, l, 1)))
            for f in range(2):
                whole(("xk", l, f), a["w_xkv_2"][l], f * BANK, BANK, (lin, ("xk", l, 2 * f + 1)))
            for f in range(2):
                whole(("xv", l, f), a["w_xkv_2"][l], D + f * BANK, BANK, (lin, ("xv", l, f, 1)))
            for f in range(2):
                whole(("mix", l, f), a["w_mix_out_2"][l], f * BANK, BANK, (lin, ("mix", l, f, 1)))
            for f in range(2):
                whole(("xq", l, f), a["w_xq_2"][l], f * BANK, BANK, (lin, ("xq", l, 2 * f + 1)))
            for f in range(2):
                whole(("xo", l, f), a["w_xo_2"][l], f * BANK, BANK, (lin, ("xo", l, f, 1)))
            for j in range(FT2 // 2):
                v = view(len(stream), KT, BANK)
                tile(("ffn", l, j), [(v[:, :, 0:SEQ], rows(a["w_ffn_in_2"][l], j * SEQ, SEQ)),
                                     (v[:, :, SEQ:BANK], rows(a["w_ffn_in_2"][l], DFF2 + j * SEQ, SEQ))], (lin, ("ffn", l, 2 * j + 1)))
            for j in range(-(-FT2 // 4)):
                whole(("ffo", l, j), a["w_ffn_out_2"][l], 0, D, None if 4 * j + 4 < FT2 else (lin, ("ffo", l, 1, 1)), 4 * j, min(4, FT2 - 4 * j))
        place = {key: n for n, (key, _, _) in enumerate(stream)}
        long_at = {key: i for i, key in enumerate(k for k, _, last in stream if last is None)}
        due, loads = [], [0] * SLOTS
        for n, (_, parts, _) in enumerate(stream):
            loads[n % SLOTS] += 16 * len(parts)
            due.append(loads[n % SLOTS])

        def arrived(eng, key):
            n = place[key]
            eng.wait_ge(slot_loaded[n % SLOTS], due[n])
            return n

        norms = [(w, l) for l in range(L1) for w in ("n1", "mla", "n2")] + ["final", "ln0"] \
            + [(w, l) for l in range(L2) for w in ("gla", "conv", "ln1", "ln2", "ln3")]
        norm_at = {key: n for n, key in enumerate(norms)}
        SQUARES = {"n1": 2, "mla": 4, "n2": 2, "gla": 8}
        sq_due, s = {}, 0
        for key in norms:
            s += 2 if key == "final" else SQUARES.get(key[0], 0)
            sq_due[key] = s
        normed_due = {(w, l): [6 * l + 2 * i + t + 1 for t in range(T)] for l in range(L1) for i, w in enumerate(("n1", "mla", "n2"))}
        updates = [(w, l) for l in range(L1) for w in ("out", "down")] + ["final", "ln0"] + [(w, l) for l in range(L2) for w in ("ln1", "ln2", "ln3")]
        update_at = {key: n + 1 for n, key in enumerate(updates)}
        gains = ["final", "ln0"] + [(w, l) for l in range(L2) for w in ("ln1", "ln2", "ln3")]
        gains_due, s = {}, [0, 0]
        for n, key in enumerate(gains):
            s[n % 2] += 16 if n == 0 else 32
            gains_due[key] = s[n % 2]
        NP1 = len(PATHS1)
        LAST_ATT1 = L1 * NP1

        def att1(l, i):
            return l * NP1 + i

        def att2(l, t):
            return LAST_ATT1 + l * T + t

        block = ctx.enter_context(nc.Block())

        @block.sync
        def _(sp):
            sp.dma_start(pos_i[:, :], a["positions"][0].rearrange("(t p) -> p t", p=P), allow_slow_non_contiguous=True).then_inc(pos_loaded, 16)
            sp.dma_start(x[:, :, :], a["x"][0].rearrange("(t p) n -> p t n", p=P)).then_inc(x_loaded, 16)
            for n, (_, parts, _) in enumerate(stream):
                if n >= SLOTS:
                    key, _, last = stream[n - SLOTS]
                    if last is None:
                        sp.wait_ge(long_used, long_at[key] + 1)
                    else:
                        sp.wait_ge(last[0].filled, last[0].at[last[1]] + 1)
                for dst, src in parts:
                    sp.dma_start(dst, src).then_inc(slot_loaded[n % SLOTS], 16)
            sp.wait_ge(x_updated, len(updates))
            sp.dma_start(out[0].rearrange("(t p) n -> p t n", p=P), x[:, :, :]).then_inc(stored, 16)
            sp.wait_ge(stored, 16)

        @block.tensor
        def _(pe):
            def by_tokens(key, xT, w, t, kn, n, c0=0):
                bank = lin.open(pe, key)
                for k in range(kn):
                    m = pe.matmul(bank[:, 0:n], xT[:, k, t * P:(t + 1) * P], w[:, k, c0:c0 + n], start=(k == 0), stop=(k == kn - 1))
                m.then_inc(lin.filled, 1)

            def by_features(key, xT, w, c0s):
                bank = lin.open(pe, key)
                for i, c0 in enumerate(c0s):
                    for k in range(KT):
                        m = pe.matmul(bank[:, i * SEQ:(i + 1) * SEQ], w[:, k, c0:c0 + P], xT[:, k, :], start=(k == 0), stop=(k == KT - 1))
                m.then_inc(lin.filled, 1)

            def turn_over(key, sources):
                bank = small.open(pe, key)
                for i, src in enumerate(sources):
                    m = pe.transpose(bank[0:src.shape[-1], i * P:i * P + src.shape[0]], src, ident[:, :])
                m.then_inc(small.filled, 1)

            def long_sum(name, l, xT, n_k):
                keys = [(name, l, t, f) for t in range(T) for f in range(2)]
                banks = [lin.open(pe, key) for key in keys]
                for j in range(-(-n_k // 4)):
                    n = arrived(pe, (name, l, j))
                    kn = min(4, n_k - 4 * j)
                    w = view(n, kn, D)
                    for i, (t, f) in enumerate((t, f) for t in range(T) for f in range(2)):
                        for k in range(kn):
                            m = pe.matmul(banks[i], xT[:, 4 * j + k, t * P:(t + 1) * P], w[:, k, f * BANK:(f + 1) * BANK],
                                          start=(j + k == 0), stop=(4 * j + k == n_k - 1))
                        if 4 * j + kn == n_k:
                            m.then_inc(lin.filled, 1)
                    if 4 * j + kn < n_k:
                        m.then_inc(long_used, 1)

            pe.wait_ge(consts_made, 1)
            for l in range(L1):
                nn = norm_at[("n1", l)]
                for t in range(T):
                    pe.wait_ge(normed, normed_due[("n1", l)][t])
                    for f in range(2):
                        turn_over(("n1", l, t, f), [hn[:, t, (4 * f + i) * P:(4 * f + i + 1) * P] for i in range(4)])
                small.wait_moved(pe, ("n1", l, 1, 1))

                def z_tile(j):
                    n = arrived(pe, ("z", l, j))
                    for t in range(T):
                        by_tokens(("z", l, j, t), hT, view(n, KT, Z_TILES[j][1]), t, KT, Z_TILES[j][1])

                def gate_unit(g):
                    j, t = g // 2, g % 2
                    n = arrived(pe, ("gate", l, j))
                    by_tokens(("gate", l, j, t), hT, view(n, KT, BANK), t, KT, BANK)

                for j in range(3):
                    z_tile(j)
                for t in range(T):
                    pe.wait_ge(normed, normed_due[("mla", l)][t])
                    turn_over(("cT", l, t), [z[:, t, i * P:(i + 1) * P] for i in range(3)])
                z_tile(3)
                n = arrived(pe, ("u", l))
                for t in range(T):
                    small.wait_moved(pe, ("cT", l, t))
                    by_tokens(("uq", l, t), cT, view(n, 2, 384), t, 2, 384)
                    by_tokens(("ukv", l, t), cT[:, 2:3, :], view(n, 1, 512, 768), t, 1, 512)
                z_tile(4)
                pe.wait_ge(decay_ready, l + 1)
                bank = small.open(pe, ("cq", l))
                pe.matmul(bank[:, 0:4], upto[:, 0:P], lf[:, 2, 0, :], start=True, stop=True)
                pe.matmul(bank[:, 4:8], ones, lf[:, 2, 0, :], start=True, stop=False)
                pe.matmul(bank[:, 4:8], upto[:, 0:P], lf[:, 2, 1, :], start=False, stop=True).then_inc(small.filled, 1)
                for f in range(2):
                    bank = lin.open(pe, ("ck", l, f)).rearrange("p (h k) -> p h k", h=2)
                    pe.matmul(bank, ones, decay_rows[0][:, 2 * f:2 * f + 2, :], start=True, stop=False)
                    for h in range(2):
                        m = pe.matmul(bank[:, h, P:SEQ], ones, decay_rows[1][:, 2 * f + h, :], start=False, stop=(h == 1))
                    m.then_inc(lin.filled, 1)
                for t in range(T):
                    turn_over(("foxT", l, t), [z[:, t, FOX_Q + i * P:FOX_Q + (i + 1) * P] for i in range(4)])
                pe.wait_ge(staged, l + 1)
                for t in range(T):
                    turn_over(("nsa", l, t), [z[:, t, NSA_Q:NSA_Q + P], z[:, t, NSA_Q + P:NSA_Q + 2 * P], stage[:, t, 0, :], stage[:, t, 1, :]])
                for t in range(T):
                    turn_over(("idx", l, t), [z[:, t, DSA_QI:DSA_QI + P], z[:, t, DSA_QI + P:DSA_QI + 2 * P], stage[:, t, 4, :], stage[:, t, 5, :]])
                gate_unit(0)
                gate_unit(1)
                n = arrived(pe, ("cmp", l))
                pe.wait_ge(cmp_rows, l + 1)
                kd = slot_of(n)[:, 0:CMP_PAIRS * P].rearrange("p (a e) -> p a e", e=P)
                vd = slot_of(n)[:, CMP_PAIRS * P:CMP_PAIRS * (P + HD)].rearrange("p (a e) -> p a e", e=HD)
                bank = small.open(pe, ("comp", l))
                for i in range(CMP_PAIRS):
                    pe.matmul(bank[:, 0:NCMP], kd[:, i, :], cmpR[:, 0, i, :], start=(i == 0), stop=(i == CMP_PAIRS - 1))
                for i in range(CMP_PAIRS):
                    m = pe.matmul(bank[0:NCMP, 64:64 + HD], cmpR[:, 1, i, :], vd[:, i, :], start=(i == 0), stop=(i == CMP_PAIRS - 1))
                m.then_inc(small.filled, 1)
                pe.wait_ge(mla_roped, l + 1)
                for w, h0 in (("mq", 0), ("mk", 4)):
                    for t in range(T):
                        turn_over((w, l, t), [mqk[:, t, h0 + h, :] for h in range(4)])
                for t in range(T):
                    turn_over(("dsa", l, t), [z[:, t, DSA_Q:DSA_Q + P], z[:, t, DSA_Q + P:DSA_Q + 2 * P], stage[:, t, 2, :], stage[:, t, 3, :]])
                small.wait_moved(pe, ("dsa", l, 1))
                for t in range(T):
                    nk = P * (t + 1)
                    for f in range(4):
                        bank = lin.open(pe, ("idx", l, t, f))
                        for i in range(2):
                            h = f + 4 * i
                            r = slice(IDX_DIM * (h % 4), IDX_DIM * (h % 4 + 1))
                            m = pe.matmul(bank[:, i * SEQ:i * SEQ + nk], attT[r, S_QI + h // 4, t * P:(t + 1) * P], attT[r, S_KI, 0:nk], start=True, stop=True)
                        m.then_inc(lin.filled, 1)
                small.wait_moved(pe, ("comp", l))
                g = 2
                for i, (path, t) in enumerate(PATHS1):
                    aa = att1(l, i)
                    nk = NCMP if path == "cmp" else P * (t + 1)
                    if aa:
                        pe.wait_ge(probs_made, aa)
                    for s, h in enumerate(BY_SLOT):
                        r = slice(HD * (h % 2), HD * (h % 2 + 1))
                        tq = slice(t * P, (t + 1) * P)
                        if path == "mla":
                            q, k = attT[0:MLA_HD, S_MLA_Q + h, tq], attT[0:MLA_HD, S_MLA_K + h, 0:nk]
                        elif path == "fox":
                            q, k = attT[r, S_FOX_Q + h // 2, tq], attT[r, S_FOX_K + h // 2, 0:nk]
                        elif path == "dsa":
                            q, k = attT[r, S_DSA_Q + h // 2, tq], attT[r, S_DSA_K, 0:nk]
                        elif path == "cmp":
                            q, k = attT[r, S_NSA_Q + h // 2, tq], kcmpT[r, :]
                        else:
                            q, k = attT[r, S_NSA_Q + h // 2, tq], attT[r, S_KS if path == "sel" else S_KW, 0:nk]
                        m = pe.matmul(scores[:, s, 0:nk], q, k, start=True, stop=True)
                    m.then_inc(scores_filled, 1)
                    for _ in range(GATES_AFTER[i]):
                        if g < 2 * GATE_TILES:
                            gate_unit(g)
                            g += 1
                    b = aa % 2
                    if path == "cmp":
                        pe.wait_ge(probs_final, cmp_final(l, t))
                        turn_over(("PT", l, i, 0), [probs[:, b, h, 0:NCMP] for h in range(HEADS)])
                    else:
                        pe.wait_ge(probs_made, aa + 1)
                        for kb in range(t + 1):
                            turn_over(("PT", l, i, kb), [probs[:, b, h, kb * P:(kb + 1) * P] for h in range(HEADS)])
                    kbs = 1 if path == "cmp" else t + 1
                    bank = small.open(pe, ("PV", l, i))
                    small.wait_moved(pe, ("PT", l, i, kbs - 1))
                    for s, h in enumerate(BY_SLOT):
                        for kb in range(kbs):
                            if path == "cmp":
                                p, v = PT[0:NCMP, b, 0, s, :], vcmp[0:NCMP, :]
                            else:
                                p = PT[:, b, kb, s, :]
                                c = {"mla": 0, "fox": FOX_V + h * HD, "sel": NSA_VS, "win": NSA_VW, "dsa": DSA_V}[path]
                                v = mv[:, kb, h * HD:(h + 1) * HD] if path == "mla" else z[:, kb, c:c + HD]
                            m = pe.matmul(bank[:, h * HD:(h + 1) * HD], p, v, start=(kb == 0), stop=(kb == kbs - 1))
                    m.then_inc(small.filled, 1)
                assert g == 2 * GATE_TILES
                small.wait_moved(pe, ("PV", l, NP1 - 1))
                for b in range(4):
                    turn_over(("oT", l, b), [osb[:, t, b, 2 * c:2 * c + 2, :].rearrange("p h d -> p (h d)") for c in range(2) for t in range(T)])
                for f in range(2):
                    n = arrived(pe, ("lift", l, f))
                    w = view(n, KT, BANK)
                    for b in range(4):
                        if f == 0:
                            small.wait_moved(pe, ("oT", l, b))
                        for t in range(T):
                            by_tokens(("lift", l, f, b, t), hT[:, 2 * b:2 * b + 2, :], w[:, 2 * b:2 * b + 2, :], t, 2, BANK)
                for t in range(T):
                    for f in range(2):
                        pe.wait_ge(gated, 4 * l + 2 * f + t + 1)
                        turn_over(("mixT", l, t, f), [gate[:, t, f * BANK + i * P:f * BANK + (i + 1) * P] for i in range(4)])
                small.wait_moved(pe, ("mixT", l, 1, 1))
                for f in range(2):
                    n = arrived(pe, ("out", l, f))
                    for t in range(T):
                        by_tokens(("out", l, f, t), hT, view(n, KT, BANK), t, KT, BANK)
                for t in range(T):
                    pe.wait_ge(normed, normed_due[("n2", l)][t])
                    for f in range(2):
                        turn_over(("n2", l, t, f), [hn[:, t, (4 * f + i) * P:(4 * f + i + 1) * P] for i in range(4)])
                small.wait_moved(pe, ("n2", l, 1, 1))
                for j in range(D_FF // BANK):
                    n = arrived(pe, ("up", l, j))
                    for b in range(2):
                        by_features(("up", l, j, b), hT, view(n, KT, BANK), [2 * b * P, (2 * b + 1) * P])
                pe.wait_ge(squared, (l + 1) * (D_FF // SEQ))
                long_sum("down", l, upT, D_FF // P)

            pe.wait_ge(mem_loaded, 16)
            for t in range(T):
                for f in range(2):
                    turn_over(("memT", t, f), [hn[:, t, (4 * f + i) * P:(4 * f + i + 1) * P] for i in range(4)])
            for l in range(L2):
                def turn_x(name, update):
                    pe.wait_ge(x_updated, update_at[update])
                    for t in range(T):
                        for f in range(2):
                            turn_over((name, l, t, f), [x[:, t, (4 * f + i) * P:(4 * f + i + 1) * P] for i in range(4)])
                    small.wait_moved(pe, (name, l, 1, 1))

                turn_x("hT", "ln0" if l == 0 else ("ln3", l - 1))
                n = arrived(pe, ("alow", l))
                bank = small.open(pe, ("alow", l))
                w = view(n, KT, RANK)
                for k in range(KT):
                    m = pe.matmul(bank[0:RANK, 0:SEQ], w[:, k, :], hT[:, k, :], start=(k == 0), stop=(k == KT - 1))
                m.then_inc(small.filled, 1)

                def proj(key):
                    n = arrived(pe, (key, l))
                    for t in range(T):
                        by_tokens((key, l, t), hT, view(n, KT, BANK), t, KT, BANK)

                proj("cg")
                proj("ca")
                for t in range(T):
                    lin.wait_moved(pe, ("ca", l, t))
                    turn_over(("uT", l, t), [u2[:, t, i * P:(i + 1) * P] for i in range(4)])
                small.wait_moved(pe, ("alow", l))
                for t in range(T):
                    bank = small.open(pe, ("zlow", l, t))
                    pe.matmul(bank[:, 0:GK], alT[0:RANK + 1, t * P:(t + 1) * P], wa2[0:RANK + 1, l, :], start=True, stop=True).then_inc(small.filled, 1)
                proj("qk")
                proj("v")
                for t in range(T):
                    pe.wait_ge(la_ready, T * l + t + 1)
                    bank = lin.open(pe, ("bc", l, t))
                    pe.matmul(bank[:, 0:GK], blk_upto[:, :], la[:, 0, t, :], start=True, stop=True)
                    pe.matmul(bank[:, GK:2 * GK], blk_after[:, :], la[:, 0, t, :], start=True, stop=True).then_inc(lin.filled, 1)
                bank = small.open(pe, ("blast", l))
                for g in range(2):
                    for t in range(T):
                        m = pe.matmul(bank[:, 4 * g + 2 * t:4 * g + 2 * t + 2], la[:, 0, t, g * P:(g + 1) * P], blk_sum[:, :], start=True, stop=True)
                m.then_inc(small.filled, 1)
                proj("r")
                for t in range(T):
                    pe.wait_ge(qkd_ready, T * l + t + 1)
                    turn_over(("qeT", l, t), [ex2[:, s, t, g * P:(g + 1) * P] for s in range(2) for g in range(2)])
                for t in range(T):
                    small.wait_moved(pe, ("qeT", l, t))
                    for e in range(2):
                        r = slice(HD * e, HD * (e + 1))
                        bank = lin.open(pe, ("att", l, t, e))
                        for g in range(2):
                            m = pe.matmul(bank[:, g * P:(g + 1) * P], keT[r, g, t * P:(t + 1) * P], qeT[r, g, t * P:(t + 1) * P], start=True, stop=True)
                        m.then_inc(lin.filled, 1)
                lin.wait_moved(pe, ("v", l, 1))
                for c in range(3):
                    bank = lin.open(pe, ("upd", l, c))
                    r = slice(CHUNK * (c % 2), CHUNK * (c % 2 + 1))
                    for g in range(2):
                        m = pe.matmul(bank[:, g * SEQ:(g + 1) * SEQ], ex2[r, 2, c // 2, g * P:(g + 1) * P], v2[r, c // 2, g * SEQ:(g + 1) * SEQ], start=True, stop=True)
                    m.then_inc(lin.filled, 1)
                small.wait_moved(pe, ("memT", 1, 1))
                for f in range(2):
                    n = arrived(pe, ("xk", l, f))
                    for b in range(2):
                        by_features(("xk", l, 2 * f + b), memT, view(n, KT, BANK), [2 * b * P, (2 * b + 1) * P])
                for f in range(2):
                    n = arrived(pe, ("xv", l, f))
                    for t in range(T):
                        by_tokens(("xv", l, f, t), memT, view(n, KT, BANK), t, KT, BANK)
                lin.wait_moved(pe, ("upd", l, 2))
                for t in range(T):
                    for e in range(2):
                        lin.wait_moved(pe, ("att", l, t, e))
                        bank = lin.open(pe, ("go", l, t, e))
                        r = slice(HD * e, HD * (e + 1))
                        chunks = [c for c in (2 * t, 2 * t + 1) if c > 0]
                        for g in range(2):
                            h = 2 * g + e
                            o = bank[:, g * P:(g + 1) * P]
                            pe.matmul(o, gattT[:, t, h, :], v2[:, t, h * P:(h + 1) * P], start=True, stop=False)
                            for c in chunks:
                                m = pe.matmul(o, qez[r, g, c, :], state[r, c - 1, g, :], start=False, stop=(c == chunks[-1]))
                        m.then_inc(lin.filled, 1)
                for t in range(T):
                    pe.wait_ge(go_ready, T * l + t + 1)
                    turn_over(("goT", l, t), [go2[:, t, i * P:(i + 1) * P] for i in range(4)])
                for key, src, ready in (("cmean", acc, conv_summed), ("cvar", sq2, conv_squared)):
                    pe.wait_ge(ready, l + 1)
                    bank = small.open(pe, (key, l))
                    for c in range(CT):
                        m = pe.matmul(bank[:, 0:SEQ], ones, src[:, c, :], start=(c == 0), stop=(c == CT - 1))
                    m.then_inc(small.filled, 1)
                pe.wait_ge(conv_out, l + 1)
                small.wait_moved(pe, ("goT", l, 1))
                for f in range(2):
                    n = arrived(pe, ("mix", l, f))
                    for t in range(T):
                        by_tokens(("mix", l, f, t), hT, view(n, KT, BANK), t, KT, BANK)
                turn_x("h1T", ("ln1", l))
                for f in range(2):
                    n = arrived(pe, ("xq", l, f))
                    for b in range(2):
                        by_features(("xq", l, 2 * f + b), hT, view(n, KT, BANK), [2 * b * P, (2 * b + 1) * P])
                lin.wait_moved(pe, ("xq", l, 3))
                lin.wait_moved(pe, ("xv", l, 1, 1))

                def x_scores(t):
                    pe.wait_ge(probs_made, att2(l, t))
                    for h in range(XH):
                        for k in range(2):
                            m = pe.matmul(scores[:, h, :], xqT[:, 2 * h + k, t * P:(t + 1) * P], xkT[:, 2 * h + k, :], start=(k == 0), stop=(k == 1))
                    m.then_inc(scores_filled, 1)

                def x_out(t):
                    b = att2(l, t) % 2
                    pe.wait_ge(probs_final, T * L1 + T * l + t + 1)
                    for kb in range(T):
                        turn_over(("xPT", l, t, kb), [probs[:, b, h, kb * P:(kb + 1) * P] for h in range(XH)])
                    small.wait_moved(pe, ("xPT", l, t, 1))
                    for f in range(2):
                        bank = lin.open(pe, ("xO", l, t, f))
                        for i in range(4):
                            h, c = 2 * f + i // 2, i % 2
                            for kb in range(T):
                                m = pe.matmul(bank[:, i * P:(i + 1) * P], xv[:, kb, h * XD + c * P:h * XD + (c + 1) * P], PT[:, b, kb, h, :], start=(kb == 0), stop=(kb == 1))
                        m.then_inc(lin.filled, 1)

                x_scores(0)
                x_scores(1)
                x_out(0)
                x_out(1)
                lin.wait_moved(pe, ("xO", l, 1, 1))
                for f in range(2):
                    n = arrived(pe, ("xo", l, f))
                    for t in range(T):
                        by_tokens(("xo", l, f, t), hT, view(n, KT, BANK), t, KT, BANK)
                turn_x("h2T", ("ln2", l))
                for j in range(FT2 // 2):
                    n = arrived(pe, ("ffn", l, j))
                    for b in range(2):
                        by_features(("ffn", l, 2 * j + b), hT, view(n, KT, BANK), [b * P, SEQ + b * P])
                lin.wait_moved(pe, ("ffn", l, FT2 - 1))
                long_sum("ffo", l, ffT, FT2)

        @block.scalar
        def _(act):
            step = Chain(act, act_step)

            for l in range(LAYERS):
                for w, name in enumerate(("norm1_g", "norm2_g")):
                    act.dma_start(g1[:, w, l, :], a[name][l].rearrange("(k p) -> p k", p=P), allow_slow_non_contiguous=True).then_inc(params_loaded, 16)
                act.dma_start(gqkv[:, l, 0:2], a["mla_q_norm_g"][l].rearrange("(k p) -> p k", p=P), allow_slow_non_contiguous=True).then_inc(params_loaded, 16)
                act.dma_start(gqkv[:, l, 2:3], a["mla_kv_norm_g"][l].rearrange("(k p) -> p k", p=P), allow_slow_non_contiguous=True).then_inc(params_loaded, 16)
                act.dma_start(fbias[:, l, :], a["fox_f_bias"][l].partition_broadcast(P)).then_inc(params_loaded, 16)
                for w in range(2):
                    act.dma_start(peT[:, l, w, :], a["nsa_cmp_pe"][l, w].rearrange("(i e) d -> (e d) i", e=2), allow_slow_non_contiguous=True).then_inc(params_loaded, 16)
            for l in range(LAYERS):
                for c in range(CT):
                    act.dma_start(conv_wT[:, l, c, :], a["conv_w_2"][l, :, c * P:(c + 1) * P].rearrange("j p -> p j"), allow_slow_non_contiguous=True).then_inc(params2_loaded, 16)
                for w, name in enumerate(("conv_b_2", "conv_ln_g_2", "conv_ln_b_2")):
                    act.dma_start(conv_p[:, w, l, :], a[name][l].rearrange("(k p) -> p k", p=P), allow_slow_non_contiguous=True).then_inc(params2_loaded, 16)
                act.dma_start(gla_g[:, l, :], a["gla_norm_g_2"][l].partition_broadcast(P)).then_inc(params2_loaded, 16)
                act.dma_start(wa2[0:RANK, l, :], a["w_a2_2"][l]).then_inc(params2_loaded, 16)
                act.dma_start(wa2[RANK:RANK + 1, l, :], a["b_a_2"][l:l + 1, :]).then_inc(params2_loaded, 16)

            def move(turns_, key, dst, take=lambda b: b, func=ACT.Copy, scale=1.0):
                bank = turns_.wait_filled(act, key)
                act.activation(dst, take(bank), func, scale=scale).then_inc(turns_.moved["act"], 1)

            def four(bank):
                return bank.rearrange("p (i q) -> p i q", i=4)

            def softmax_exp(aa, scale, nk, sums=True):
                b = aa % 2
                act.wait_ge(bias_ready, aa + 1)
                for h in range(HEADS):
                    m = act.activation(probs[:, b, h, 0:nk], scores[:, h, 0:nk], ACT.Exp, bias=softmax_s[:, b, 1, h:h + 1], scale=scale,
                                       accum_out=softmax_s[:, b, 2, h:h + 1] if sums else None)
                m.then_inc(probs_made, 1)

            junk = probs[:, 0, :, :].rearrange("p h k -> p (h k)")

            def squares(key, sources):
                nn = norm_at[key]
                done = sq_due[key] - len(sources)
                for i, src in enumerate(sources):
                    if done + i:
                        act.wait_ge(squares_summed, done + i)
                    act.activation(junk[:, 0:src.shape[-1]], src, ACT.Square, accum_out=stats[:, nn, i:i + 1]).then_inc(squares_summed, 1)

            act.wait_ge(angles_made, 1)
            act.activation(rope[:, :, :, :], red[:, :, :, :], ACT.Sin).then_inc(rope_tables, 1)

            for l in range(L1):
                if l == 0:
                    act.wait_ge(x_loaded, 16)
                else:
                    act.wait_ge(x_updated, update_at[("down", l - 1)])
                squares(("n1", l), [x[:, t, :] for t in range(T)])

                def z_out(j):
                    c0, cn = Z_TILES[j]
                    for t in range(T):
                        move(lin, ("z", l, j, t), z[:, t, c0:c0 + cn], lambda b: b[:, 0:cn])

                z_out(0)
                lin.wait_moved(act, ("z", l, 0, 1))
                squares(("mla", l), [z[:, t, 0:MLA_Q] for t in range(T)] + [z[:, t, MLA_Q:MLA_Q + MLA_KV] for t in range(T)])
                z_out(1)
                z_out(2)
                lin.wait_moved(act, ("z", l, 2, 1))
                act.activation(gn, z[:, :, NSA_G:NSA_G + 12], ACT.Tanh, scale=0.5).then_inc(nsa_tanh, 1)
                z_out(3)
                act.wait_ge(fox_logits, l + 1)
                step(act.activation(lf[:, 1], lf[:, 0], ACT.Abs))
                step.settle()
                step(act.activation(lf[:, 1], lf[:, 1], ACT.Exp, scale=-1.0))
                step.settle()
                act.activation(lf[:, 1], lf[:, 1], ACT.Ln, bias=1.0).then_inc(fox_log, 1)
                for t in range(T):
                    move(lin, ("uq", l, t), mqk[:, t, 0:4, :], lambda b: b[:, 0:384].rearrange("p (h d) -> p h d", h=HEADS))
                    bank = lin.wait_filled(act, ("ukv", l, t)).rearrange("p (h w d) -> p h w d", h=HEADS, w=2)
                    act.activation(mqk[:, t, 4:8, 0:HD], bank[:, :, 0, :], ACT.Copy)
                    act.activation(mv[:, t, :].rearrange("p (h d) -> p h d", h=HEADS), bank[:, :, 1, :], ACT.Copy).then_inc(lin.moved["act"], 1)
                z_out(4)
                for w, s in (("foxT", S_FOX_Q), ("nsa", S_NSA_Q), ("idx", S_QI)):
                    for t in range(T):
                        move(small, (w, l, t), attT[:, s:s + 4, t * P:(t + 1) * P], four)

                def gate_out(g):
                    j, t = g // 2, g % 2
                    move(lin, ("gate", l, j, t), gate[:, t, j * BANK:(j + 1) * BANK], func=ACT.Tanh, scale=0.5)

                gate_out(0)
                gate_out(1)
                for w, s in (("mq", S_MLA_Q), ("mk", S_MLA_K)):
                    for t in range(T):
                        move(small, (w, l, t), attT[0:MLA_HD, s:s + 4, t * P:(t + 1) * P], lambda b: four(b[0:MLA_HD]))
                for t in range(T):
                    move(small, ("dsa", l, t), attT[:, S_DSA_Q:S_DSA_Q + 4, t * P:(t + 1) * P], four)
                for t in range(T):
                    nk = P * (t + 1)
                    for f in range(4):
                        n = 8 * l + 4 * t + f
                        if n >= 2:
                            act.wait_ge(index_used, n - 1)
                        move(lin, ("idx", l, t, f), relu_l[:, n % 2, :, 0:nk], lambda b: b.rearrange("p (h k) -> p h k", h=2)[:, :, 0:nk],
                             func=ACT.Relu, scale=IDX_DIM ** -0.5 * IDX_HEADS ** -0.5)
                act.wait_ge(index_used, 8 * (l + 1))
                g = 2
                for i, (path, t) in enumerate(PATHS1):
                    aa = att1(l, i)
                    b = aa % 2
                    softmax_exp(aa, SCALE[path], NCMP if path == "cmp" else P * (t + 1), sums=path != "cmp")
                    for _ in range(GATES_AFTER[i]):
                        if g < 2 * GATE_TILES:
                            gate_out(g)
                            g += 1
                    if path == "cmp":
                        move(small, ("PT", l, i, 0), PT[0:NCMP, b, 0], lambda bk: four(bk[0:NCMP]))
                    else:
                        for kb in range(t + 1):
                            move(small, ("PT", l, i, kb), PT[:, b, kb], four)
                for b in range(4):
                    move(small, ("oT", l, b), hT[:, 2 * b:2 * b + 2, :], lambda bk: bk.rearrange("p (c q) -> p c q", c=2))
                for t in range(T):
                    for f in range(2):
                        move(small, ("mixT", l, t, f), hT[:, 4 * f:4 * f + 4, t * P:(t + 1) * P], four, scale=0.5)
                act.wait_ge(x_updated, update_at[("out", l)])
                squares(("n2", l), [x[:, t, :] for t in range(T)])
                for j in range(D_FF // BANK):
                    for b in range(2):
                        move(lin, ("up", l, j, b), upT[:, 4 * j + 2 * b:4 * j + 2 * b + 2, :], lambda bk: bk.rearrange("p (c q) -> p c q", c=2), func=ACT.Relu)
            act.wait_ge(x_updated, update_at[("down", L1 - 1)])
            squares("final", [x[:, t, :] for t in range(T)])

            def turned(name, l):
                for t in range(T):
                    for f in range(2):
                        key = (name, l, t, f) if l is not None else (name, t, f)
                        dst = hT if l is not None else memT
                        move(small, key, dst[:, 4 * f:4 * f + 4, t * P:(t + 1) * P], four)

            turned("memT", None)
            for l in range(L2):
                turned("hT", l)
                act.wait_ge(pads_zeroed, l + 1)
                move(small, ("alow", l), alT[0:RANK, :], lambda b: b[0:RANK, 0:SEQ])
                for t in range(T):
                    move(lin, ("cg", l, t), sg2[:, t, :], func=ACT.Tanh, scale=0.5)
                for t in range(T):
                    move(small, ("uT", l, t), uT[:, :, PAD + t * P:PAD + (t + 1) * P], four, scale=0.5)
                for t in range(T):
                    small.wait_moved(act, ("zlow", l, t))
                    step(act.activation(la[:, 1, t, :], la[:, 0, t, :], ACT.Abs))
                    step.settle()
                    step(act.activation(la[:, 1, t, :], la[:, 1, t, :], ACT.Exp, scale=-1.0))
                    step.settle()
                    act.activation(la[:, 1, t, :], la[:, 1, t, :], ACT.Ln, bias=1.0).then_inc(low_log, 1)
                for t in range(T):
                    move(lin, ("qk", l, t), qk2[:, t, :])
                for t in range(T):
                    move(lin, ("v", l, t), v2[:, t, :])
                for t in range(T):
                    bank = lin.wait_filled(act, ("bc", l, t))
                    act.activation(ex2[:, 0, t, :], bank[:, 0:GK], ACT.Exp, scale=1 / 16)
                    act.activation(ex2[:, 1, t, :], bank[:, 0:GK], ACT.Exp, scale=-1 / 16)
                    act.activation(ex2[:, 2, t, :], bank[:, GK:], ACT.Exp, scale=1 / 16).then_inc(lin.moved["act"], 1)
                move(small, ("blast", l), dec, lambda b: b[:, 0:8].rearrange("p (g c) -> p g c", g=2), func=ACT.Exp, scale=1 / 16)
                for t in range(T):
                    bank = lin.wait_filled(act, ("r", l, t))
                    act.activation(sr2[:, t, :], bank, ACT.Tanh, scale=0.5).then_inc(r_tanh, 1)
                for t in range(T):
                    bank = four(small.wait_filled(act, ("qeT", l, t)))
                    act.activation(qeT[:, :, t * P:(t + 1) * P], bank[:, 0:2, :], ACT.Copy)
                    act.activation(keT[:, :, t * P:(t + 1) * P], bank[:, 2:4, :], ACT.Copy)
                    act.activation(qez[:, :, 2 * t, 0:CHUNK], bank[:, 0:2, 0:CHUNK], ACT.Copy)
                    act.activation(qez[:, :, 2 * t + 1, CHUNK:], bank[:, 0:2, CHUNK:], ACT.Copy).then_inc(small.moved["act"], 1)
                for b in range(4):
                    move(lin, ("xk", l, b), xkT[:, 2 * b:2 * b + 2, :], lambda bk: bk.rearrange("p (c q) -> p c q", c=2))
                for f in range(2):
                    for t in range(T):
                        move(lin, ("xv", l, f, t), xv[:, t, f * BANK:(f + 1) * BANK])
                lin.wait_moved(act, ("go", l, 1, 1))
                nn = norm_at[("gla", l)]
                for t in range(T):
                    for h in range(HEADS):
                        act.wait_ge(squares_summed, sq_due[("gla", l)] - T * HEADS + HEADS * t + h)
                        act.activation(gla_junk, go2[:, t, h * P:(h + 1) * P], ACT.Square, accum_out=stats[:, nn, 4 * t + h:4 * t + h + 1]).then_inc(squares_summed, 1)
                for t in range(T):
                    move(small, ("goT", l, t), hT[:, 4:8, t * P:(t + 1) * P], four)
                act.wait_ge(conv_centred, l + 1)
                act.activation(sq2[:, :, :], acc[:, :, :], ACT.Square).then_inc(conv_squared, 1)
                act.wait_ge(conv_affine, l + 1)
                act.activation(sq2[:, :, :], acc[:, :, :], ACT.Tanh, scale=0.5).then_inc(conv_tanh, 1)
                turned("h1T", l)
                for b in range(4):
                    move(lin, ("xq", l, b), xqT[:, 2 * b:2 * b + 2, :], lambda bk: bk.rearrange("p (c q) -> p c q", c=2))
                for t in range(T):
                    softmax_exp(att2(l, t), XD ** -0.5, SEQ)
                for t in range(T):
                    b = att2(l, t) % 2
                    for kb in range(T):
                        move(small, ("xPT", l, t, kb), PT[:, b, kb], four)
                    for f in range(2):
                        move(lin, ("xO", l, t, f), hT[:, 4 * f:4 * f + 4, t * P:(t + 1) * P], four)
                turned("h2T", l)
                for f in range(FT2):
                    bank = lin.wait_filled(act, ("ffn", l, f))
                    if f >= 2:
                        lin.wait_moved(act, ("ffn", l, f - 2))
                    act.activation(ffs[:, f % 2, :], bank[:, 0:SEQ], ACT.Tanh, scale=0.5).then_inc(ff_tanh, 1)

        @block.vector
        def _(dve):
            step = Chain(dve, dve_step)

            def moved(ins, turns_):
                ins.then_inc(turns_.moved["dve"], 1)

            def four(bank):
                return bank.rearrange("p (i q) -> p i q", i=4)

            dve.wait_ge(pos_loaded, 16)
            dve.wait_ge(consts_made, 1)
            step(dve.tensor_copy(pos_f[:, :], pos_i[:, :]))
            step.settle()
            for t in range(T):
                step(dve.tensor_scalar(ang[:, t, :], freq[:, :], pos_f[:, t:t + 1], None, ALU.mult))
            step.settle()
            for s, quarter in ((0, 0.0), (1, 0.25)):
                step(dve.tensor_scalar(turns[:, s], ang[:, :, :], 1 / (2 * np.pi), quarter, ALU.mult, ALU.add))
            step.settle()
            step(dve.tensor_scalar(turns[:, :], turns[:, :], ROUND, None, ALU.add))
            step.settle()
            step(dve.tensor_scalar(turns[:, :], turns[:, :], -ROUND, None, ALU.add))
            step.settle()
            for s in range(2):
                step(dve.scalar_tensor_tensor(out=red[:, s], in0=turns[:, s], scalar=-TWO_PI[0], in1=ang[:, :, :], op0=ALU.mult, op1=ALU.add))
            for part in TWO_PI[1:]:
                step.settle()
                step(dve.scalar_tensor_tensor(out=red[:, :], in0=turns[:, :], scalar=-part, in1=red[:, :], op0=ALU.mult, op1=ALU.add))
            step.settle()
            step(dve.tensor_scalar(red[:, 1], red[:, 1], np.pi / 2, None, ALU.add))
            step.settle()
            dve.tensor_scalar(red[:, :], red[:, :], PI_BELOW, -PI_BELOW, ALU.min, ALU.max).then_inc(angles_made, 1)

            def norm_mean(key, parts):
                nn = norm_at[key]
                dve.wait_ge(squares_summed, sq_due[key])
                for i, (src, dst, n, eps) in enumerate(parts):
                    m = dve.tensor_scalar(stats[:, nn, dst], stats[:, nn, src], 1.0 / n, eps, ALU.mult, ALU.add)
                m.then_inc(mean_ready, 1)
                dve.wait_ge(rstd_ready, nn + 1)
                return nn

            def rms_rows(key):
                nn = norm_mean(key, [(slice(0, 2), slice(8, 10), D, NORM_EPS)])
                for t in range(T):
                    dve.tensor_scalar(hn[:, t, :], x[:, t, :], stats[:, nn, 12 + t:13 + t], None, ALU.mult).then_inc(normed, 1)

            def gained(name, l, w):
                for t in range(T):
                    for f in range(2):
                        bank = four(small.wait_filled(dve, (name, l, t, f)))
                        moved(dve.tensor_tensor(hT[:, 4 * f:4 * f + 4, t * P:(t + 1) * P], bank,
                                                g1[:, w, l, 4 * f:4 * f + 4].unsqueeze(2).to_broadcast([P, 4, P]), ALU.mult), small)

            def softmax_bias(aa, nk, scale, bias=None, k0=0):
                b = aa % 2
                dve.wait_ge(scores_filled, aa + 1)
                if bias is not None:
                    step(dve.tensor_tensor(scores[:, :, k0:nk], scores[:, :, k0:nk], bias, ALU.add))
                    step.settle()
                step(dve.tensor_reduce(softmax_s[:, b, 0, :], scores[:, :, 0:nk], AX, ALU.max, negate=True))
                step.settle()
                dve.tensor_scalar(softmax_s[:, b, 1, :], softmax_s[:, b, 0, :], scale, None, ALU.mult).then_inc(bias_ready, 1)

            def heads(v, n):
                return v.unsqueeze(1).to_broadcast([P, HEADS, n])

            def take_top(t):
                nk = P * (t + 1)
                s = index_bias[t]
                for _ in range(KEEP // 8):
                    step(dve.max(best, s))
                    step.settle()
                    step(dve.match_replace(s, best, s, TAKEN))
                    step.settle()
                step(dve.tensor_scalar(s, s, TAKEN / 2, MASKED, ALU.is_gt, ALU.mult))
                step.settle()
                step(dve.tensor_tensor(s, s, causal[:, SEQ - nk:SEQ], ALU.min))
                step.settle()

            dve.wait_ge(params_loaded, 16 * 7 * LAYERS)
            for l in range(L1):
                rms_rows(("n1", l))
                gained("n1", l, 0)
                nn = norm_mean(("mla", l), [(slice(0, 2), slice(8, 10), MLA_Q, NORM_EPS), (slice(2, 4), slice(10, 12), MLA_KV, NORM_EPS)])
                for t in range(T):
                    dve.tensor_scalar(z[:, t, 0:MLA_Q], z[:, t, 0:MLA_Q], stats[:, nn, 12 + t:13 + t], None, ALU.mult)
                    dve.tensor_scalar(z[:, t, MLA_Q:MLA_Q + MLA_KV], z[:, t, MLA_Q:MLA_Q + MLA_KV], stats[:, nn, 14 + t:15 + t], None, ALU.mult).then_inc(normed, 1)
                for t in range(T):
                    bank = small.wait_filled(dve, ("cT", l, t))[:, 0:3 * P].rearrange("p (i q) -> p i q", i=3)
                    moved(dve.tensor_tensor(cT[:, :, t * P:(t + 1) * P], bank, gqkv[:, l, :].unsqueeze(2).to_broadcast([P, 3, P]), ALU.mult), small)
                lin.wait_moved(dve, ("z", l, 3, 1))
                dve.tensor_tensor(lf[:, 0], z[:, :, FOX_F:FOX_F + HEADS], fbias[:, l, :].unsqueeze(1).to_broadcast([P, T, HEADS]), ALU.add).then_inc(fox_logits, 1)
                dve.wait_ge(nsa_tanh, l + 1)
                step(dve.tensor_scalar(gn, gn, 0.5, 0.5, ALU.mult, ALU.add))
                dve.wait_ge(fox_log, l + 1)
                step(dve.scalar_tensor_tensor(out=lf[:, 2], in0=lf[:, 0], scalar=0.0, in1=lf[:, 1], op0=ALU.min, op1=ALU.subtract))
                step.settle()
                for s, w in ((0, SEQ), (1, P)):
                    for i, h in enumerate(BY_SLOT):
                        m = dve.tensor_scalar(decay_rows[s][:, i, :], upto[:, 0:w], lf[:, 2, s, h:h + 1], -(HD ** 0.5), ALU.mult, ALU.mult)
                m.then_inc(decay_ready, 1)
                bank = small.wait_filled(dve, ("cq", l))
                moved(dve.tensor_scalar(cq8, bank[:, 0:8].rearrange("p (t h) -> p t h", t=T), HD ** 0.5, None, ALU.mult), small)
                small.wait_moved(dve, ("cq", l))
                for f in range(2):
                    bank = lin.wait_filled(dve, ("ck", l, f)).rearrange("p (h k) -> p h k", h=2)
                    for i in range(2):
                        h = BY_SLOT[2 * f + i]
                        for t in range(T):
                            nk = P * (t + 1)
                            m = dve.scalar_tensor_tensor(out=d8[t][:, 2 * f + i, :], in0=bank[:, i, 0:nk], scalar=cq8[:, t, h:h + 1],
                                                         in1=causal[:, SEQ - nk:SEQ], op0=ALU.add, op1=ALU.add)
                    moved(m, lin)
                small.wait_moved(dve, ("idx", l, 1))
                for w, s in enumerate((S_KC, S_VC)):
                    for e in range(2):
                        r = slice(HD * e, HD * (e + 1))
                        src = attT[r, s, :].rearrange("p (c i e) -> p i c e", i=8, e=2)
                        for i1 in range(2):
                            m = dve.tensor_tensor(cmpR[r, w, 8 * i1:8 * i1 + 8, :], src[:, :, i1:i1 + NCMP, e],
                                                  peT[r, l, w, 8 * i1:8 * i1 + 8].unsqueeze(2).to_broadcast([HD, 8, NCMP]), ALU.add)
                m.then_inc(cmp_rows, 1)
                bank = small.wait_filled(dve, ("comp", l))
                dve.tensor_copy(kcmpT, bank[:, 0:NCMP])
                moved(dve.tensor_copy(vcmp[0:NCMP], bank[0:NCMP, 64:64 + HD]), small)
                for t in range(T):
                    nk = P * (t + 1)
                    for f in range(4):
                        n = 8 * l + 4 * t + f
                        lin.wait_moved(dve, ("idx", l, t, f))
                        for i in range(2):
                            h = f + 4 * i
                            w = z[:, t, DSA_W + h:DSA_W + h + 1]
                            if h == 0:
                                step(dve.tensor_scalar(index_bias[t], relu_l[:, n % 2, i, 0:nk], w, None, ALU.mult))
                            else:
                                m = dve.scalar_tensor_tensor(out=index_bias[t], in0=relu_l[:, n % 2, i, 0:nk], scalar=w, in1=index_bias[t], op0=ALU.mult, op1=ALU.add)
                                if i == 0:
                                    step(m)
                                else:
                                    m.then_inc(index_used, 1)
                            if i == 0:
                                step.settle()
                        dve.wait_ge(index_used, n + 1)
                    step(dve.tensor_tensor(index_bias[t], index_bias[t], causal[:, SEQ - nk:SEQ], ALU.add))
                    step.settle()
                seen = set()
                for i, (path, t) in enumerate(PATHS1):
                    aa = att1(l, i)
                    b = aa % 2
                    nk = NCMP if path == "cmp" else P * (t + 1)
                    if path == "fox":
                        softmax_bias(aa, nk, SCALE[path], d8[t])
                    elif path == "dsa":
                        softmax_bias(aa, nk, SCALE[path], heads(index_bias[t], nk))
                    elif path == "cmp":
                        softmax_bias(aa, nk, SCALE[path], heads(cmp_bias[:, t, :], NCMP))
                    else:
                        softmax_bias(aa, nk, SCALE[path], heads(causal[:, P:SEQ], P), t * P)
                    if i in (2, 4):
                        take_top(i // 2 - 1)
                    dve.wait_ge(probs_made, aa + 1)
                    total, weight = softmax_s[:, b, 2, :], softmax_s[:, b, 3, :]
                    if path == "cmp":
                        dve.tensor_tensor(probs[:, b, :, 0:NCMP], probs[:, b, :, 0:NCMP], heads(cmp_keep[:, t, :], NCMP), ALU.mult).then_inc(probs_final, 1)
                        dve.wait_ge(probs_final, cmp_final(l, t))
                        step(dve.tensor_reduce(total, probs[:, b, :, 0:NCMP], AX, ALU.add))
                        step.settle()
                        step(dve.tensor_scalar(total, total, 1e-30, None, ALU.max))
                        step.settle()
                    step(dve.reciprocal(weight, total))
                    if BRANCH[path] == 1:
                        g0 = HEADS * ("cmp", "sel", "win").index(path)
                        step.settle()
                        step(dve.tensor_tensor(weight.rearrange("p (e i) -> p e i", e=2), weight.rearrange("p (e i) -> p e i", e=2),
                                               gn[:, t, g0:g0 + HEADS].rearrange("p (i e) -> p e i", e=2), ALU.mult))
                    step.settle()
                    bank = small.wait_filled(dve, ("PV", l, i))[:, 0:HEADS * HD].rearrange("p (i e d) -> p i e d", i=2, e=2)
                    dst = osb[:, t, BRANCH[path]].rearrange("p (i e) d -> p i e d", e=2)
                    wide = weight.rearrange("p (e i) -> p i e", e=2).unsqueeze(3).to_broadcast([P, 2, 2, HD])
                    if (BRANCH[path], t) in seen:
                        moved(dve.tensor_tensor(otmp.rearrange("p (i e) d -> p i e d", e=2), bank, wide, ALU.mult), small)
                        small.wait_moved(dve, ("PV", l, i))
                        step(dve.tensor_tensor(osb[:, t, BRANCH[path]], osb[:, t, BRANCH[path]], otmp, ALU.add))
                    else:
                        moved(dve.tensor_tensor(dst, bank, wide, ALU.mult), small)
                    seen.add((BRANCH[path], t))
                for f in range(2):
                    for b in range(4):
                        for t in range(T):
                            gv = gate[:, t, b * D + f * BANK:b * D + (f + 1) * BANK]
                            bank = lin.wait_filled(dve, ("lift", l, f, b, t))
                            moved(dve.scalar_tensor_tensor(out=gv, in0=gv, scalar=1.0, in1=bank, op0=ALU.add, op1=ALU.mult), lin)
                for f in range(2):
                    for t in range(T):
                        bank = lin.wait_filled(dve, ("out", l, f, t))
                        xv_ = x[:, t, f * BANK:(f + 1) * BANK]
                        m = dve.tensor_tensor(xv_, bank, xv_, ALU.add)
                        moved(m, lin)
                lin.wait_moved(dve, ("out", l, 1, 1))
                dve.sem_inc(x_updated, 1)
                rms_rows(("n2", l))
                gained("n2", l, 1)
                for j in range(D_FF // BANK):
                    for b in range(2):
                        lin.wait_moved(dve, ("up", l, j, b))
                        v = upT[:, 4 * j + 2 * b:4 * j + 2 * b + 2, :]
                        dve.tensor_tensor(v, v, v, ALU.mult).then_inc(squared, 1)
                for t in range(T):
                    for f in range(2):
                        bank = lin.wait_filled(dve, ("down", l, t, f))
                        xv_ = x[:, t, f * BANK:(f + 1) * BANK]
                        moved(dve.tensor_tensor(xv_, bank, xv_, ALU.add), lin)
                lin.wait_moved(dve, ("down", l, 1, 1))
                dve.sem_inc(x_updated, 1)
            nn = norm_mean("final", [(slice(0, 2), slice(8, 10), D, NORM_EPS)])
            dve.wait_ge(lng_loaded[0], gains_due["final"])
            for t in range(T):
                step(dve.scalar_tensor_tensor(out=x[:, t, :], in0=x[:, t, :], scalar=stats[:, nn, 12 + t:13 + t], in1=lng[:, 0, 0, :], op0=ALU.mult, op1=ALU.mult))
            step.settle()
            dve.sem_inc(x_updated, 1)

            def layer_norm(key):
                nn = norm_at[key]
                for t in range(T):
                    for f in range(2):
                        step(dve.bn_stats(halves[:, t, f, :], x[:, t, f * BANK:(f + 1) * BANK]))
                step.settle()
                for t in range(T):
                    step(dve.bn_aggr(stats[:, nn, 2 * t:2 * t + 2], halves[:, t, :, :]))
                step.settle()
                dve.tensor_scalar(stats[:, nn, 8:10], stats[:, nn, 0:4].rearrange("p (t w) -> p t w", w=2)[:, :, 1], LN_EPS, None, ALU.add).then_inc(mean_ready, 1)
                dve.wait_ge(rstd_ready, nn + 1)
                for t in range(T):
                    step(dve.tensor_scalar(x[:, t, :], x[:, t, :], stats[:, nn, 2 * t:2 * t + 1], stats[:, nn, 12 + t:13 + t], ALU.subtract, ALU.mult))
                b = gains.index(key) % 2
                dve.wait_ge(lng_loaded[b], gains_due[key])
                for w, op in ((0, ALU.mult), (1, ALU.add)):
                    for t in range(T):
                        step.settle(1)
                        step(dve.tensor_tensor(x[:, t, :], x[:, t, :], lng[:, b, w, :], op))
                step.settle()
                dve.sem_inc(x_updated, 1)

            def residual(name, l, t, f):
                bank = lin.wait_filled(dve, (name, l, t, f) if name == "ffo" else (name, l, f, t))
                xv_ = x[:, t, f * BANK:(f + 1) * BANK]
                moved(dve.scalar_tensor_tensor(out=xv_, in0=xv_, scalar=ALPHA, in1=bank, op0=ALU.mult, op1=ALU.add), lin)

            layer_norm("ln0")
            dve.wait_ge(params2_loaded, 16 * (CT + 6) * LAYERS)
            for l in range(L2):
                for t in range(T):
                    lin.wait_moved(dve, ("cg", l, t))
                    bank = lin.wait_filled(dve, ("ca", l, t))
                    moved(dve.scalar_tensor_tensor(out=u2[:, t, :], in0=sg2[:, t, :], scalar=1.0, in1=bank, op0=ALU.add, op1=ALU.mult), lin)
                for t in range(T):
                    bank = small.wait_filled(dve, ("zlow", l, t))
                    moved(dve.tensor_copy(la[:, 0, t, :], bank[:, 0:GK]), small)
                for t in range(T):
                    dve.wait_ge(low_log, T * l + t + 1)
                    dve.scalar_tensor_tensor(out=la[:, 0, t, :], in0=la[:, 0, t, :], scalar=0.0, in1=la[:, 1, t, :], op0=ALU.min, op1=ALU.subtract).then_inc(la_ready, 1)
                for t in range(T):
                    lin.wait_moved(dve, ("bc", l, t))
                    dve.scalar_tensor_tensor(out=ex2[:, 0, t, :], in0=qk2[:, t, 0:GK], scalar=HD ** -0.5, in1=ex2[:, 0, t, :], op0=ALU.mult, op1=ALU.mult)
                    dve.tensor_tensor(ex2[:, 1, t, :], qk2[:, t, GK:], ex2[:, 1, t, :], ALU.mult)
                    dve.tensor_tensor(ex2[:, 2, t, :], qk2[:, t, GK:], ex2[:, 2, t, :], ALU.mult).then_inc(qkd_ready, 1)
                for t in range(T):
                    dve.wait_ge(r_tanh, T * l + t + 1)
                    bank = lin.wait_filled(dve, ("r", l, t))
                    moved(dve.scalar_tensor_tensor(out=sr2[:, t, :], in0=sr2[:, t, :], scalar=1.0, in1=bank, op0=ALU.add, op1=ALU.mult), lin)
                dve.wait_ge(pads_zeroed, l + 1)
                for t in range(T):
                    for e in range(2):
                        bank = lin.wait_filled(dve, ("att", l, t, e))[:, 0:2 * P].rearrange("p (g c) -> p g c", g=2)
                        moved(dve.copy_predicated(gattT[:, t, :, :].rearrange("p (g e) c -> p g e c", e=2)[:, :, e, :],
                                                  blk_upto[:, :].unsqueeze(1).to_broadcast([P, 2, P]).bitcast(I32), bank), lin)
                small.wait_moved(dve, ("blast", l))
                for c in range(3):
                    bank = lin.wait_filled(dve, ("upd", l, c)).rearrange("p (g e n) -> p g e n", g=2, e=2)
                    for e in range(2):
                        r = slice(HD * e, HD * (e + 1))
                        if c == 0:
                            m = dve.tensor_copy(state[r, c, :, :], bank[r, :, e, :])
                        else:
                            for g in range(2):
                                m = dve.scalar_tensor_tensor(out=state[r, c, g, :], in0=state[r, c - 1, g, :], scalar=dec[r, g, c:c + 1], in1=bank[r, g, e, :], op0=ALU.mult, op1=ALU.add)
                    moved(m, lin)
                    lin.wait_moved(dve, ("upd", l, c))
                small.wait_moved(dve, ("uT", l, 1))
                for j in range(TAPS):
                    for c in range(CT):
                        src, w = uT[:, c, j:j + SEQ], conv_wT[:, l, c, j:j + 1]
                        if j == 0:
                            step(dve.tensor_scalar(acc[:, c, :], src, w, conv_p[:, 0, l, c:c + 1], ALU.mult, ALU.add))
                        else:
                            step.settle(CT - 1)
                            step(dve.scalar_tensor_tensor(out=acc[:, c, :], in0=src, scalar=w, in1=acc[:, c, :], op0=ALU.mult, op1=ALU.add))
                step.settle()
                dve.sem_inc(conv_summed, 1)
                for t in range(T):
                    for e in range(2):
                        bank = lin.wait_filled(dve, ("go", l, t, e))[:, 0:2 * P].rearrange("p (g n) -> p g n", g=2)
                        moved(dve.tensor_copy(go2[:, t, :].rearrange("p (g e n) -> p g e n", g=2, e=2)[:, :, e, :], bank), lin)
                nn = norm_mean(("gla", l), [(slice(0, 8), slice(0, 8), P, LN_EPS)])
                for t in range(T):
                    v = four(go2[:, t, :])
                    step(dve.tensor_tensor(v, v, stats[:, nn, 8 + 4 * t:12 + 4 * t].unsqueeze(2).to_broadcast([P, HEADS, P]), ALU.mult))
                    step.settle()
                    step(dve.tensor_tensor(v, v, heads(gla_g[:, l, :], P), ALU.mult))
                    step.settle()
                    dve.scalar_tensor_tensor(out=go2[:, t, :], in0=go2[:, t, :], scalar=0.5, in1=sr2[:, t, :], op0=ALU.mult, op1=ALU.mult).then_inc(go_ready, 1)

                def channels(v):
                    return v.unsqueeze(1).to_broadcast([P, CT, SEQ])

                bank = small.wait_filled(dve, ("cmean", l))
                moved(dve.tensor_scalar(mean_c, bank[:, 0:SEQ], 1.0 / CONV, None, ALU.mult), small)
                small.wait_moved(dve, ("cmean", l))
                dve.tensor_tensor(acc[:, :, :], acc[:, :, :], channels(mean_c), ALU.subtract).then_inc(conv_centred, 1)
                bank = small.wait_filled(dve, ("cvar", l))
                moved(dve.tensor_scalar(var_c, bank[:, 0:SEQ], 1.0 / CONV, LN_EPS, ALU.mult, ALU.add), small)
                small.wait_moved(dve, ("cvar", l))
                dve.sem_inc(mean_ready, 1)
                dve.wait_ge(rstd_ready, norm_at[("conv", l)] + 1)
                step(dve.tensor_tensor(acc[:, :, :], acc[:, :, :], channels(rstd_c), ALU.mult))
                step.settle()
                for c in range(CT):
                    m = dve.tensor_scalar(acc[:, c, :], acc[:, c, :], conv_p[:, 1, l, c:c + 1], conv_p[:, 2, l, c:c + 1], ALU.mult, ALU.add)
                m.then_inc(conv_affine, 1)
                dve.wait_ge(conv_tanh, l + 1)
                step(dve.tensor_scalar(sq2[:, :, :], sq2[:, :, :], 0.5, 0.5, ALU.mult, ALU.add))
                step.settle()
                dve.tensor_tensor(hT[:, 0:CT, :], acc[:, :, :], sq2[:, :, :], ALU.mult).then_inc(conv_out, 1)
                for f in range(2):
                    for t in range(T):
                        residual("mix", l, t, f)
                lin.wait_moved(dve, ("mix", l, 1, 1))
                layer_norm(("ln1", l))
                for t in range(T):
                    softmax_bias(att2(l, t), SEQ, XD ** -0.5)
                for t in range(T):
                    aa = att2(l, t)
                    b = aa % 2
                    dve.wait_ge(probs_made, aa + 1)
                    step(dve.reciprocal(softmax_s[:, b, 3, :], softmax_s[:, b, 2, :]))
                    step.settle()
                    dve.tensor_tensor(probs[:, b], probs[:, b], softmax_s[:, b, 3, :].unsqueeze(2).to_broadcast([P, XH, SEQ]), ALU.mult).then_inc(probs_final, 1)
                for f in range(2):
                    for t in range(T):
                        residual("xo", l, t, f)
                lin.wait_moved(dve, ("xo", l, 1, 1))
                layer_norm(("ln2", l))
                for f in range(FT2):
                    dve.wait_ge(ff_tanh, FT2 * l + f + 1)
                    bank = lin.wait_filled(dve, ("ffn", l, f))
                    step(dve.scalar_tensor_tensor(out=ffs[:, f % 2, :], in0=ffs[:, f % 2, :], scalar=1.0, in1=bank[:, 0:SEQ], op0=ALU.add, op1=ALU.mult))
                    step.settle()
                    moved(dve.scalar_tensor_tensor(out=ffT[:, f, :], in0=ffs[:, f % 2, :], scalar=0.5, in1=bank[:, SEQ:], op0=ALU.mult, op1=ALU.mult), lin)
                for t in range(T):
                    for f in range(2):
                        residual("ffo", l, t, f)
                lin.wait_moved(dve, ("ffo", l, 1, 1))
                layer_norm(("ln3", l))

        @block.gpsimd
        def _(pool):
            step = Chain(pool, pool_step)

            def select(v, keep, fill, base, per_row, per_column):
                step.settle()
                step(pool.affine_select(out=v, in_=v, pattern=[[per_column, v.shape[-1]]], compare_op=keep, fill=fill, base=base, channel_multiplier=per_row))

            for v, value in ((ident[:, :], 0.0), (causal[:, :], 0.0), (upto[:, :], 1.0), (cmp_bias[:, :, :], 0.0), (cmp_keep[:, :, :], 1.0),
                             (blk_upto[:, :], 1.0), (blk_after[:, :], 1.0), (blk_sum[:, :], 1.0), (minus_half[:, :], -0.5)):
                step(pool.memset(v, value))
            for first, half in ROPES:
                for i in range(half):
                    step(pool.memset(freq[:, first + i:first + i + 1], float(np.float32(THETA) ** (-np.float32(i) / np.float32(half)))))
            select(ident[:, :], ALU.not_equal, 1.0, 0, 1, -1)
            select(causal[:, P:SEQ], ALU.is_ge, MASKED, 0, 1, -1)
            select(upto[:, 0:P], ALU.is_ge, 0.0, 0, -1, 1)
            for t in range(T):
                select(cmp_bias[:, t, :], ALU.is_ge, MASKED, P * t - (CMP_LEN - 1), 1, -CMP_STRIDE)
                select(cmp_keep[:, t, :], ALU.is_ge, 0.0, P * t - (CMP_LEN - 1), 1, -CMP_STRIDE)
            select(blk_upto[:, :], ALU.is_ge, 0.0, 0, -1, 1)
            select(blk_upto[:, CHUNK:], ALU.is_ge, 0.0, -CHUNK, 1, 0)
            select(blk_after[:, :], ALU.is_ge, 0.0, -1, 1, -1)
            select(blk_after[:, 0:CHUNK], ALU.is_ge, 0.0, CHUNK - 1, -1, 0)
            select(blk_sum[:, 0:1], ALU.is_ge, 0.0, CHUNK - 1, -1, 0)
            select(blk_sum[:, 1:2], ALU.is_ge, 0.0, -CHUNK, 1, 0)
            step.settle()
            pool.sem_inc(consts_made, 1)

            def root(key, src=slice(8, 10), dst=slice(12, 14)):
                nn = norm_at[key]
                pool.wait_ge(mean_ready, nn + 1)
                n = src.stop - src.start
                pool.tensor_tensor(stats[:, nn, dst], stats[:, nn, src], minus_half[:, 0:1].to_broadcast([P, n]), ALU.pow).then_inc(rstd_ready, 1)

            def rotate(v, kind):
                first, half = kind
                n = v.shape[2]
                shape = [P, T, n, half]
                sin = rope[:, 0, :, first:first + half].unsqueeze(2).to_broadcast(shape)
                cos = rope[:, 1, :, first:first + half].unsqueeze(2).to_broadcast(shape)
                tmp = [rope_tmp[:, s, 0:T * n * half].rearrange("p (t h d) -> p t h d", t=T, h=n) for s in range(4)]
                x1, x2 = v[:, :, :, 0:half], v[:, :, :, half:2 * half]
                for dst, src, table in zip(tmp, (x1, x2, x2, x1), (cos, sin, cos, sin)):
                    step(pool.tensor_tensor(dst, src, table, ALU.mult))
                step.settle()
                step(pool.tensor_tensor(x1, tmp[0], tmp[1], ALU.subtract))
                step(pool.tensor_tensor(x2, tmp[2], tmp[3], ALU.add))
                step.settle()

            def by_head(c0, n, d):
                return z[:, :, c0:c0 + n * d].rearrange("p t (h d) -> p t h d", d=d)

            MLA_ROPE, HEAD_ROPE, IDX_ROPE = ROPES
            pool.wait_ge(rope_tables, 1)
            for l in range(L1):
                root(("n1", l))
                root(("mla", l), slice(8, 12), slice(12, 16))
                lin.wait_moved(pool, ("z", l, 2, 1))
                rotate(by_head(MLA_Q + MLA_KV, 1, MLA_R), MLA_ROPE)
                rotate(by_head(NSA_Q, 4, HD), HEAD_ROPE)
                rotate(by_head(NSA_KC, 3, 2 * HD), HEAD_ROPE)
                for t in range(T):
                    step(pool.tensor_copy(stage[:, t, 0:2, :].rearrange("p w (r d) -> p w r d", r=2),
                                          z[:, t, NSA_KS:NSA_KS + 4 * HD].rearrange("p (w d) -> p w d", w=2)[:, :, 0:HD].unsqueeze(2).to_broadcast([P, 2, 2, HD])))
                    step(pool.tensor_copy(stage[:, t, 4:6, :].rearrange("p w (r d) -> p w r d", r=2),
                                          z[:, t, NSA_KC:NSA_KC + 2 * HD].rearrange("p (w d) -> p w d", w=2).unsqueeze(2).to_broadcast([P, 2, 2, HD])))
                lin.wait_moved(pool, ("ukv", l, 1))
                rotate(mqk[:, :, 0:HEADS, HD:MLA_HD], MLA_ROPE)
                for t in range(T):
                    m = pool.tensor_copy(mqk[:, t, HEADS:2 * HEADS, HD:MLA_HD], z[:, t, MLA_Q + MLA_KV:NSA0].unsqueeze(1).to_broadcast([P, HEADS, MLA_R]))
                    if t == 0:
                        step(m)
                m.then_inc(mla_roped, 1)
                lin.wait_moved(pool, ("z", l, 4, 1))
                rotate(by_head(DSA_Q, 5, HD), HEAD_ROPE)
                rotate(by_head(DSA_QI, IDX_HEADS + 1, IDX_DIM), IDX_ROPE)
                for t in range(T):
                    step(pool.tensor_copy(stage[:, t, 2, :].rearrange("p (r d) -> p r d", r=2), z[:, t, DSA_K:DSA_K + HD].unsqueeze(1).to_broadcast([P, 2, HD])))
                    step(pool.tensor_copy(stage[:, t, 3, :].rearrange("p (r d) -> p r d", r=4), z[:, t, DSA_KI:DSA_KI + IDX_DIM].unsqueeze(1).to_broadcast([P, 4, IDX_DIM])))
                step.settle()
                pool.sem_inc(staged, 1)
                for f in range(2):
                    for t in range(T):
                        lin.wait_moved(pool, ("lift", l, f, 3, t))
                        part = [gate[:, t, b * D + f * BANK:b * D + (f + 1) * BANK] for b in range(4)]
                        step(pool.tensor_tensor(part[0], part[0], part[1], ALU.add))
                        step(pool.tensor_tensor(part[2], part[2], part[3], ALU.add))
                        step.settle()
                        pool.tensor_tensor(part[0], part[0], part[2], ALU.add).then_inc(gated, 1)
                root(("n2", l))

            def load_gains(n):
                key = gains[n]
                if key == "final":
                    srcs = [a["final_g"]]
                elif key == "ln0":
                    srcs = [a["ln0_g_2"], a["ln0_b_2"]]
                else:
                    srcs = [a[key[0] + "_g_2"][key[1]], a[key[0] + "_b_2"][key[1]]]
                for w, src in enumerate(srcs):
                    pool.dma_start(lng[:, n % 2, w, :], src.partition_broadcast(P)).then_inc(lng_loaded[n % 2], 16)

            def after(key):
                n = gains.index(key)
                if n + 2 < len(gains):
                    pool.wait_ge(x_updated, update_at[key])
                    load_gains(n + 2)

            pool.wait_ge(small.filled, small.at[("n2", L1 - 1, 1, 1)] + 1)
            pool.dma_start(hn[:, :, :], a["mem_2"][0].rearrange("(t p) n -> p t n", p=P)).then_inc(mem_loaded, 16)
            load_gains(0)
            load_gains(1)
            root("final")
            after("final")
            root("ln0")
            after("ln0")
            for l in range(L2):
                if l == 0:
                    step(pool.memset(qez, 0.0))
                    step(pool.memset(gattT, 0.0))
                    step(pool.memset(uT[:, :, 0:PAD], 0.0))
                step(pool.memset(alT, 1.0))
                step.settle()
                pool.sem_inc(pads_zeroed, 1)
                root(("gla", l), slice(0, 8), slice(8, 16))
                pool.wait_ge(mean_ready, norm_at[("conv", l)] + 1)
                pool.tensor_tensor(rstd_c, var_c, minus_half[:, 0:1].to_broadcast([P, SEQ]), ALU.pow).then_inc(rstd_ready, 1)
                for w in ("ln1", "ln2", "ln3"):
                    root((w, l))
                    after((w, l))


_OUTS = [((1, SEQ, D), "float32")]
_INS = ["x", "positions", "norm1_g", "w_in", "mla_q_norm_g", "mla_w_uq", "mla_kv_norm_g", "mla_w_ukv", "nsa_cmp_pe", "nsa_cmp_w",
        "fox_f_bias", "w_branch", "w_out", "norm2_g", "w_up", "w_down", "final_g", "mem_2", "ln0_g_2", "ln0_b_2", "w_in_2", "w_a2_2",
        "b_a_2", "conv_w_2", "conv_b_2", "conv_ln_g_2", "conv_ln_b_2", "gla_norm_g_2", "w_mix_out_2", "ln1_g_2", "ln1_b_2", "w_xq_2",
        "w_xkv_2", "w_xo_2", "ln2_g_2", "ln2_b_2", "w_ffn_in_2", "w_ffn_out_2", "ln3_g_2", "ln3_b_2"]


def kernel(**inputs):
    from concourse import bacc
    from concourse.bass_utils import run_bass_kernel_spmd

    nc = bacc.Bacc("TRN2", target_bir_lowering=False, num_devices=1)
    arrays, aps = {}, {}
    for name in _INS:
        arr = np.ascontiguousarray(inputs[name])
        arrays[f"in_{name}"] = arr
        aps[name] = nc.dram_tensor(f"in_{name}", arr.shape, mybir.dt.from_np(arr.dtype), kind="ExternalInput").ap()
    out = nc.dram_tensor("out", _OUTS[0][0], F32, kind="ExternalOutput").ap()
    two_decoders(nc, aps, out)
    r = run_bass_kernel_spmd(nc, [arrays], core_ids=[0])
    return r.results[0]["out"]
```

```python
from contextlib import ExitStack

import numpy as np

import concourse.bass as bass
from concourse import mybir

F32 = mybir.dt.float32
I32 = mybir.dt.int32
F32R = mybir.dt.float32r
ALU = mybir.AluOpType
ACT = mybir.ActivationFunctionType
AX = mybir.AxisListType.X

P = 128
SEQ = 256
T = SEQ // P
D = 1024
KT = D // P
HEADS = 4
HD = 64
MASKED = -1e30
TAKEN = -3e38
BANK = 512

MLA_Q, MLA_KV, MLA_R = 256, 128, 32
MLA_HD = HD + MLA_R
MLA0 = 0
NSA0 = MLA_Q + MLA_KV + MLA_R
FOX0 = NSA0 + 4 * HD + 6 * HD + 12
DSA0 = FOX0 + 3 * HEADS * HD + HEADS
GATE0 = DSA0 + 4 * HD + 2 * HD + 8 * 32 + 32 + 8
IN1 = GATE0 + 4 * D
NSA_Q, NSA_KC, NSA_VC, NSA_KS, NSA_VS, NSA_KW, NSA_VW, NSA_G = [NSA0 + c for c in (0, 256, 320, 384, 448, 512, 576, 640)]
FOX_Q, FOX_K, FOX_V, FOX_F = [FOX0 + c for c in (0, 256, 512, 768)]
DSA_Q, DSA_K, DSA_V, DSA_QI, DSA_KI, DSA_W = [DSA0 + c for c in (0, 256, 320, 384, 640, 672)]
IDX_HEADS, IDX_DIM, KEEP = 8, 32, 64
CMP_LEN, CMP_STRIDE = 32, 16
NCMP = (SEQ - CMP_LEN) // CMP_STRIDE + 1
CMP_PAIRS = CMP_LEN // 2
D_FF = 4096
ROPES = ((0, 16), (16, 8), (24, 4))
NFREQ = 28
THETA = 500000.0
NORM_EPS = 1e-6

CONV = 512
TAPS = 31
PAD = TAPS - 1
CT = CONV // P
GK, GV = 256, 512
RANK = 16
CHUNK = 64
DFF2 = 2816
FT2 = DFF2 // P
XH, XD = 4, 256
IN2 = 2 * CONV + 2 * GK + 2 * GV + RANK
ALPHA = 4 ** 0.25
LN_EPS = 1e-5
SLOTS = 2
PIECES = 4
PIECE = KT * BANK // 4
ARENA = 27700
ROUND = 1.5 * 2 ** 23
TWO_PI = (6.28125, 0.0019350051879882812, 3.019915981956752e-07)
PI_BELOW = 3.1415925

S_NSA_Q, S_KS, S_KW, S_DSA_Q, S_DSA_K, S_KI, S_QI, S_KC, S_VC, S_FOX_Q, S_FOX_K, S_MLA_Q, S_MLA_K = 0, 2, 3, 4, 6, 7, 8, 10, 11, 12, 14, 16, 20
N_ATT_T = 24
BY_SLOT = (0, 2, 1, 3)


def cmp_final(l, t):
    return T * l + t + 1


class Turns:

    def __init__(self, banks, plan, filled, moved):
        self.banks, self.plan, self.filled, self.moved = banks, plan, filled, moved
        self.at = {key: u for u, (key, _) in enumerate(plan)}
        self.count, seen = [], {}
        for _, engine in plan:
            seen[engine] = seen.get(engine, 0) + 1
            self.count.append(seen[engine])
        assert len(self.at) == len(plan)

    def bank(self, key):
        return self.banks[self.at[key] % len(self.banks)]

    def open(self, pe, key):
        u = self.at[key] - len(self.banks)
        if u >= 0:
            pe.wait_ge(self.moved[self.plan[u][1]], self.count[u])
        return self.bank(key)

    def wait_filled(self, eng, key):
        eng.wait_ge(self.filled, self.at[key] + 1)
        return self.bank(key)

    def wait_moved(self, eng, key):
        u = self.at[key]
        eng.wait_ge(self.moved[self.plan[u][1]], self.count[u])


class Chain:

    def __init__(self, eng, sem):
        self.eng, self.sem, self.n = eng, sem, 0

    def __call__(self, ins):
        self.n += 1
        ins.then_inc(self.sem, 1)

    def settle(self, but=0):
        if self.n > but:
            self.eng.wait_ge(self.sem, self.n - but)


PATHS1 = [("fox", 0), ("fox", 1), ("win", 0), ("win", 1), ("mla", 0), ("mla", 1), ("sel", 0), ("sel", 1),
          ("cmp", 0), ("cmp", 1), ("dsa", 0), ("dsa", 1)]
BRANCH = {"mla": 0, "sel": 1, "win": 1, "cmp": 1, "fox": 2, "dsa": 3}
SCALE = {"mla": MLA_HD ** -0.5, "sel": HD ** -0.5, "win": HD ** -0.5, "cmp": HD ** -0.5, "fox": HD ** -0.5, "dsa": HD ** -0.5}
GATE_TILES = 4 * D // BANK
GATES_AFTER = [1, 1, 1, 1, 1, 1, 1, 1, 1, 1, 2, 2]
Z_TILES = [(j * BANK, min(BANK, GATE0 - j * BANK)) for j in range(-(-GATE0 // BANK))]


def plans(L1, L2):
    lin, small = [], []
    for l in range(L1):
        small += [(("n1", l, t, f), "dve") for t in range(T) for f in range(2)]
        lin += [(("z", l, j, t), "act") for j in range(3) for t in range(T)]
        small += [(("cT", l, t), "dve") for t in range(T)]
        lin += [(("z", l, 3, t), "act") for t in range(T)]
        lin += [((w, l, t), "act") for t in range(T) for w in ("uq", "ukv")]
        lin += [(("z", l, 4, t), "act") for t in range(T)]
        small += [(("cq", l), "dve")]
        lin += [(("ck", l, f), "dve") for f in range(2)]
        small += [((w, l, t), "act") for w in ("foxT", "nsa", "idx") for t in range(T)]
        lin += [(("gate", l, 0, t), "act") for t in range(T)]
        small += [(("comp", l), "dve")]
        small += [((w, l, t), "act") for w in ("mq", "mk", "dsa") for t in range(T)]
        lin += [(("idx", l, t, f), "act") for t in range(T) for f in range(4)]
        g = 2
        for i, (path, t) in enumerate(PATHS1):
            for _ in range(GATES_AFTER[i] if i else 1):
                if g < 2 * GATE_TILES:
                    lin.append((("gate", l, g // 2, g % 2), "act"))
                    g += 1
            small += [(("PT", l, i, kb), "act") for kb in range(1 if path == "cmp" else t + 1)]
            small += [(("PV", l, i), "dve")]
        assert g == 2 * GATE_TILES
        small += [(("oT", l, b), "dve") for b in range(4)]
        lin += [(("lift", l, f, b, t), "dve") for f in range(2) for b in range(4) for t in range(T)]
        small += [(("mixT", l, t, f), "dve") for t in range(T) for f in range(2)]
        lin += [(("out", l, t, f), "dve") for t in range(T) for f in range(2)]
        small += [(("n2", l, t, f), "dve") for t in range(T) for f in range(2)]
        lin += [(("up", l, j, b), "dve") for j in range(D_FF // BANK) for b in range(2)]
        if l == L1 - 1:
            small += [(("memT", t, f), "dve") for t in range(T) for f in range(2)]
        lin += [(("down", l, t, f), "dve") for t in range(T) for f in range(2)]
    for l in range(L2):
        small += [(("hT", l, t, f), "dve") for t in range(T) for f in range(2)]
        small += [(("alow", l), "act")]
        lin += [(("cg", l, t), "act") for t in range(T)]
        lin += [(("ca", l, t), "dve") for t in range(T)]
        small += [(("uT", l, t), "act") for t in range(T)]
        small += [(("zlow", l, t), "dve") for t in range(T)]
        lin += [(("qk", l, t), "act") for t in range(T)]
        lin += [(("v", l, t), "act") for t in range(T)]
        lin += [(("bc", l, t), "act") for t in range(T)]
        small += [(("blast", l), "act")]
        lin += [(("r", l, t), "dve") for t in range(T)]
        small += [(("qeT", l, t), "act") for t in range(T)]
        lin += [(("att", l, t, e), "dve") for t in range(T) for e in range(2)]
        lin += [(("upd", l, c), "dve") for c in range(3)]
        lin += [(("xk", l, b), "act") for b in range(4)]
        lin += [(("xv", l, 0, t), "act") for t in range(T)]
        lin += [(("go", l, t, e), "dve") for t in range(T) for e in range(2)]
        small += [(("cmean", l), "dve")]
        lin += [(("xv", l, 1, t), "act") for t in range(T)]
        small += [(("goT", l, t), "dve") for t in range(T)]
        small += [(("cvar", l), "dve"), (("crstd", l), "dve")]
        lin += [(("mix", l, t, f), "dve") for t in range(T) for f in range(2)]
        small += [(("h1T", l, t, f), "dve") for t in range(T) for f in range(2)]
        lin += [(("xq", l, b), "act") for b in range(4)]
        for t in range(T):
            small += [(("xPT", l, t, m), "act") for m in range(2)]
            lin += [(("xO", l, t, f), "dve") for f in range(2)]
        lin += [(("xo", l, t, f), "dve") for t in range(T) for f in range(2)]
        small += [(("h2T", l, t, f), "dve") for t in range(T) for f in range(2)]
        lin += [(("ffn", l, f), "dve") for f in range(FT2)]
        lin += [(("ffo", l, t, f), "dve") for t in range(T) for f in range(2)]
    return lin, small


def two_decoders(nc, a, out, L1=2, L2=2):
    ctx = ExitStack()
    with ctx:
        def sb(name, shape, dt=F32):
            return ctx.enter_context(nc.sbuf_tensor(name, shape, dt))

        def sem(name):
            return ctx.enter_context(nc.semaphore(name))

        LAYERS = a["w_in"].shape[0]
        RING_AT = 0
        W_HI_AT = RING_AT + SLOTS * KT * BANK
        W_LO_AT = W_HI_AT + PIECES * PIECE
        HT_AT = W_LO_AT + PIECES * PIECE
        HN_AT = HT_AT + KT * SEQ
        ARENA_AT = HN_AT + T * D
        base = -(-nc.sbuf_base // 32) * 32
        sb("slab", [P, ARENA_AT + ARENA])

        def placed(name, shape, at, dt=F32R):
            return nc.alloc_sbuf_tensor_at(name, [P] + shape, dt, offset=base + 4 * at)

        ring = placed("ring", [SLOTS, KT * BANK], RING_AT, F32)
        w_hi = placed("w_hi", [PIECES, PIECE], W_HI_AT)
        w_lo = placed("w_lo", [PIECES, PIECE], W_LO_AT)
        hT = placed("hT", [KT, SEQ], HT_AT, F32)
        hn = placed("hn", [T, D], HN_AT, F32)
        hT_hi = placed("hT_hi", [KT, SEQ], HT_AT)
        hT_lo = placed("hT_lo", [KT, SEQ], ARENA_AT + 6144)
        hT_lo2 = placed("hT_lo2", [KT, SEQ], ARENA_AT + 19376)
        mem_hi = placed("mem_hi", [T, KT, P], ARENA_AT + 4096)
        mem_lo = placed("mem_lo", [T, KT, P], HN_AT)
        up_hi = placed("up_hi", [D_FF // P, SEQ], ARENA_AT + 8192)
        up_lo = placed("up_lo", [D_FF // P, SEQ], ARENA_AT + 8192 + 2 * D_FF)
        FF_AT = T * GATE0 + T * 4 * D
        ff_hi = placed("ff_hi", [FT2, SEQ], ARENA_AT + FF_AT)
        ff_lo = placed("ff_lo", [FT2, SEQ], ARENA_AT + FF_AT + FT2 * SEQ)
        x = sb("x", [P, T, D])
        ident = sb("ident", [P, P])
        causal = sb("causal", [P, SEQ])
        upto = sb("upto", [P, SEQ])
        ones = upto[:, P:SEQ]
        cmp_bias = sb("cmp_bias", [P, T, NCMP])
        cmp_keep = sb("cmp_keep", [P, T, NCMP])
        blk_upto = sb("blk_upto", [P, P])
        blk_after = sb("blk_after", [P, P])
        blk_sum = sb("blk_sum", [P, 2])
        minus_half = sb("minus_half", [P, 1])
        N_NORMS = 3 * L1 + 2 + 5 * L2
        stats = sb("stats", [P, N_NORMS, 16])
        softmax_s = sb("softmax_s", [P, 2, 4, HEADS])
        g1 = sb("g1", [P, 2, LAYERS, KT])
        gqkv = sb("gqkv", [P, LAYERS, 3])
        fbias = sb("fbias", [P, LAYERS, HEADS])
        peT = sb("peT", [P, LAYERS, 2, CMP_PAIRS])
        conv_wT = sb("conv_wT", [P, LAYERS, CT, TAPS])
        conv_p = sb("conv_p", [P, 3, LAYERS, CT])
        gla_g = sb("gla_g", [P, LAYERS, P])
        wa2 = sb("wa2", [32, LAYERS, GK])
        pos_i = sb("pos_i", [P, T], I32)
        pos_f = sb("pos_f", [P, T])
        freq = sb("freq", [P, NFREQ])
        ang = sb("ang", [P, T, NFREQ])
        red = sb("red", [P, 2, T, NFREQ])
        halves = sb("halves", [P, T, 2, 6])
        turns = sb("turns", [P, 2, T, NFREQ])
        rope = sb("rope", [P, 2, T, NFREQ])
        arena = placed("arena", [ARENA], ARENA_AT, F32)

        def cut(lo, n, pattern=None, **sizes):
            v = arena[:, lo:lo + n]
            return v.rearrange(pattern, **sizes) if pattern else v

        z = cut(0, T * GATE0, "p (t n) -> p t n", t=T)
        GATE_AT = T * GATE0
        gate = cut(GATE_AT, T * 4 * D, "p (t n) -> p t n", t=T)
        PROBS_AT = GATE_AT + T * 4 * D
        probs = cut(PROBS_AT, 2 * HEADS * SEQ, "p (b h k) -> p b h k", b=2, h=HEADS)
        PT_AT = PROBS_AT + 2 * HEADS * SEQ
        PT = cut(PT_AT, 2 * T * HEADS * P, "p (b m h q) -> p b m h q", b=2, m=T, h=HEADS)
        ATT_AT = PT_AT + 2 * T * HEADS * P
        attT = cut(ATT_AT, N_ATT_T * SEQ, "p (s q) -> p s q", s=N_ATT_T)
        MORE = ATT_AT + N_ATT_T * SEQ
        mv = cut(MORE, T * 256, "p (t n) -> p t n", t=T)
        d8 = [cut(MORE + 512, 512, "p (h k) -> p h k", h=HEADS), cut(MORE + 1024, 1024, "p (h k) -> p h k", h=HEADS)]
        index_bias = [cut(MORE + 2048, P), cut(MORE + 2048 + P, SEQ)]
        cmpR = cut(MORE + 2432, 2 * CMP_PAIRS * NCMP, "p (w a c) -> p w a c", w=2, a=CMP_PAIRS)
        kcmpT = cut(MORE + 2912, NCMP)
        vcmp = cut(MORE + 2928, HD)
        lf = cut(MORE + 2992, 3 * T * HEADS, "p (s t h) -> p s t h", s=3, t=T)
        cq8 = cut(MORE + 3016, T * HEADS, "p (t h) -> p t h", t=T)
        gn = cut(MORE + 3024, T * 12, "p (t g) -> p t g", t=T)
        best = cut(MORE + 3048, 8)
        cT = cut(MORE + 3312, 3 * SEQ, "p (k s) -> p k s", k=3)
        otmp = cut(MORE + 3056, 256, "p (h d) -> p h d", h=HEADS)
        LATE = 4 * D - 3 * BANK
        mqk = cut(GATE_AT + 4 * D + LATE, 3 * BANK, "p (t h d) -> p t h d", t=T, h=8)
        rope_tmp = cut(GATE_AT + LATE, 4 * P, "p (s n) -> p s n", s=4)
        relu_l = cut(GATE_AT + LATE + 512, 2 * 2 * SEQ, "p (b h k) -> p b h k", b=2, h=2)
        stage = cut(PT_AT, T * 6 * P, "p (t s n) -> p t s n", t=T, s=6)
        decay_rows = [cut(PROBS_AT, HEADS * SEQ, "p (h k) -> p h k", h=HEADS), cut(PROBS_AT + HEADS * SEQ, HEADS * P, "p (h k) -> p h k", h=HEADS)]
        osb = hn[:, :, :].rearrange("p t (b h d) -> p t b h d", b=4, h=HEADS)
        up_sq = cut(8192 + 4 * D_FF, 2 * BANK, "p (b n) -> p b n", b=2)
        gainedT = cut(8192 + 4 * D_FF + 2 * BANK, 2 * BANK, "p (b n) -> p b n", b=2)
        lng = cut(0, 4 * D, "p (b w n) -> p b w n", b=2, w=2)
        xkT = cut(6144, 2048, "p (k s) -> p k s", s=SEQ)
        xv = cut(8192, 2048, "p (t n) -> p t n", t=T)
        qez = cut(10240, 1024, "p (g c k) -> p g c k", g=2, c=4)
        gattT = cut(11264, 1024, "p (t h c) -> p t h c", t=T, h=HEADS)
        state = cut(12288, 768, "p (c g e) -> p c g e", c=3, g=2)
        dec = cut(13056, 8, "p (g c) -> p g c", g=2)
        qeT = cut(PROBS_AT, 512, "p (g s) -> p g s", g=2)
        keT = cut(PROBS_AT + 512, 512, "p (g s) -> p g s", g=2)
        alT = arena[0:32, PROBS_AT + 1024:PROBS_AT + 1024 + SEQ]
        mean_c = cut(PT_AT, SEQ)
        root_diag = cut(PT_AT + SEQ, T * P, "p (t n) -> p t n", t=T)
        gla_junk = cut(PT_AT + 1024, P)
        Z2 = ATT_AT
        u2 = cut(Z2, 1024, "p (t n) -> p t n", t=T)
        go2 = u2
        sg2 = cut(Z2 + 1024, 1024, "p (t n) -> p t n", t=T)
        sq2 = cut(Z2 + 1024, 1024, "p (c s) -> p c s", c=CT)
        la = cut(Z2 + 2048, 1536, "p (s t n) -> p s t n", s=3, t=T)
        ex2 = cut(Z2 + 3584, 1536, "p (s t n) -> p s t n", s=3, t=T)
        sr2 = cut(Z2 + 5120, 1024, "p (t n) -> p t n", t=T)
        v2 = cut(Z2 + 6144, 1024, "p (t n) -> p t n", t=T)
        qk2 = cut(Z2 + 7168, 1024, "p (t n) -> p t n", t=T)
        xqT = cut(Z2 + 6144, 2048, "p (k s) -> p k s", s=SEQ)
        uT = cut(Z2 + 8192, CT * (PAD + SEQ), "p (c s) -> p c s", c=CT)
        acc = cut(Z2 + 8192 + CT * (PAD + SEQ), CT * SEQ, "p (c s) -> p c s", c=CT)
        ffs = cut(Z2 + 8192 + CT * (PAD + SEQ), 512, "p (b s) -> p b s", b=2)
        ffp = cut(Z2 + 8192 + CT * (PAD + SEQ) + 512, 512, "p (b s) -> p b s", b=2)

        ps = ctx.enter_context(nc.psum_tensor("ps", [P, 8, BANK], F32))
        scores = ps[:, 6:8, :].rearrange("p b (h k) -> p (b h) k", h=2)

        lin_plan, small_plan = plans(L1, L2)
        lin = Turns([ps[:, b, :] for b in range(4)], lin_plan, sem("lin_filled"), {e: sem(f"lin_moved_by_{e}") for e in ("act", "dve")})
        small = Turns([ps[:, b, :] for b in (4, 5)], small_plan, sem("small_filled"), {e: sem(f"small_moved_by_{e}") for e in ("act", "dve")})
        slot_loaded = [sem(f"slot_loaded_{i}") for i in range(SLOTS)]
        hi_ready = sem("weight_hi_ready")
        lo_ready = {e: sem(f"weight_lo_ready_by_{e}") for e in ("dve", "pool")}
        pieces_used = sem("weight_pieces_used")
        rounded = sem("activations_rounded")
        made = sem("activations_made")
        relued = sem("up_relued")
        split = sem("activations_split")
        x_loaded = [sem(f"x_loaded_{t}") for t in range(T)]
        pos_loaded = sem("pos_loaded")
        first_gain_loaded = sem("first_gain_loaded")
        params_loaded = sem("params_loaded")
        ident_made = sem("ident_made")
        params2_loaded = sem("params2_loaded")
        consts_made = sem("consts_made")
        angles_made = sem("angles_made")
        rope_tables = sem("rope_tables")
        squares_summed = sem("squares_summed")
        mean_ready = sem("mean_ready")
        rstd_ready = sem("rstd_ready")
        normed = sem("normed")
        fox_logits = sem("fox_logits")
        fox_log = sem("fox_log")
        decay_ready = sem("decay_rows_ready")
        staged = sem("staged")
        mla_roped = sem("mla_roped")
        cmp_rows = sem("cmp_rows")
        nsa_tanh = sem("nsa_tanh")
        index_used = sem("index_logits_used")
        scores_filled = sem("scores_filled")
        bias_ready = sem("softmax_bias_ready")
        probs_made = sem("probs_made")
        probs_final = sem("probs_final")
        gated = sem("gates_summed")
        x_updated = sem("x_updated")
        mem_loaded = sem("mem_loaded")
        lng_loaded = [sem(f"gains_loaded_{i}") for i in range(2)]
        pads_zeroed = sem("pads_zeroed")
        low_log = sem("low_log")
        la_ready = sem("la_ready")
        decays_exp = sem("decays_exp")
        r_tanh = sem("r_tanh")
        cg_tanh = sem("cg_tanh")
        ff_tanh = sem("ff_tanh")
        qkd_ready = sem("qkd_ready")
        state_ready = sem("state_ready")
        go_moved = sem("go_moved")
        go_ready = sem("go_ready")
        conv_summed = sem("conv_summed")
        conv_centred = sem("conv_centred")
        conv_squared = sem("conv_squared")
        root_spread = sem("root_spread")
        conv_affine = sem("conv_affine")
        conv_tanh = sem("conv_tanh")
        conv_out = sem("conv_out")
        u_ready = sem("u_ready")
        dve_step, act_step, pool_step = sem("dve_step"), sem("act_step"), sem("pool_step")
        stored = sem("stored")

        stream = []

        def slot_of(n):
            return ring[:, n % SLOTS, :]

        def rows(w, n0, nn, k0=0, kn=KT):
            return w[k0 * P:(k0 + kn) * P, n0:n0 + nn].rearrange("(k p) n -> p k n", p=P)

        def view(n, kn, nn, off=0):
            return slot_of(n)[:, off:off + kn * nn].rearrange("p (k n) -> p k n", k=kn)

        first_piece, piece_done, lo_due, used = {}, [], [], 0
        lo_count = {"dve": 0, "pool": 0}

        def tile(key, parts, last, pieces=0, lo="dve"):
            nonlocal used
            for _ in range(pieces):
                lo_count[lo] += 1
                lo_due.append((lo_ready[lo], lo_count[lo]))
            if pieces:
                first_piece[key] = (len(piece_done), pieces)
                for i in range(pieces):
                    if key[0] == "lift":
                        piece_done.append((lin.filled, lin.at[key + (i, 1)] + 1))
                    elif last is not None and i == pieces - 1:
                        piece_done.append((last[0].filled, last[0].at[last[1]] + 1))
                    else:
                        used += 1
                        piece_done.append((pieces_used, used))
            stream.append((key, parts, last))

        def whole(key, w, n0, nn, last, k0=0, kn=KT, pieces=0, lo="dve"):
            tile(key, [(view(len(stream), kn, nn), rows(w, n0, nn, k0, kn))], last, pieces, lo)

        def square(name, l, w, k0s, lo="dve"):
            for j, k0 in enumerate(k0s):
                whole((name, l, j), w, 0, D, None if j == 0 else (lin, (name, l, 1, 1)), k0, 4, 4, lo)

        for l in range(L1):
            w_in = a["w_in"][l]
            for j, (c0, cn) in enumerate(Z_TILES[:4]):
                whole(("z", l, j), w_in, c0, cn, (lin, ("z", l, j, 1)))
            n = len(stream)
            tile(("u", l), [(view(n, 2, 384), rows(a["mla_w_uq"][l], 0, 384, 0, 2)),
                            (view(n, 1, 512, 768), rows(a["mla_w_ukv"][l], 0, 512, 0, 1))], (lin, ("ukv", l, 1)))
            whole(("z", l, 4), w_in, *Z_TILES[4], (lin, ("z", l, 4, 1)))
            whole(("gate", l, 0), w_in, GATE0, BANK, (lin, ("gate", l, 0, 1)))
            slot = slot_of(len(stream))
            ck = a["nsa_cmp_w"][l, 0].rearrange("(a p) e -> p a e", p=P)
            cv = a["nsa_cmp_w"][l, 1].rearrange("(a p) e -> p a e", p=P)
            kd = slot[:, 0:CMP_PAIRS * P].rearrange("p (a e) -> p a e", e=P)
            vd = slot[:, CMP_PAIRS * P:CMP_PAIRS * (P + HD)].rearrange("p (a e) -> p a e", e=HD)
            tile(("cmp", l), [(kd[:, :, 0:HD], ck), (kd[:, :, HD:P], ck), (vd, cv)], (small, ("comp", l)))
            for j in range(1, GATE_TILES):
                whole(("gate", l, j), w_in, GATE0 + j * BANK, BANK, (lin, ("gate", l, j, 1)))
            w_br = a["w_branch"][l].rearrange("b (c p) n -> p (b c) n", p=P)
            for f in range(2):
                tile(("lift", l, f), [(view(len(stream), KT, BANK), w_br[:, :, f * BANK:(f + 1) * BANK])], (lin, ("lift", l, f, 3, 1)), 4)
            square("out", l, a["w_out"][l], (0, 4))
            for j in range(D_FF // BANK):
                whole(("up", l, j), a["w_up"][l], j * BANK, BANK, (lin, ("up", l, j, 1)), pieces=4, lo="dve" if j else "pool")
            for j in range(D_FF // BANK):
                whole(("down", l, j), a["w_down"][l], 0, D, None if j + 1 < D_FF // BANK else (lin, ("down", l, 1, 1)), 4 * j, 4, pieces=4)
        for l in range(L2):
            w2 = a["w_in_2"][l]
            whole(("alow", l), w2, IN2 - RANK, RANK, (small, ("alow", l)))
            for key, c0 in (("cg", CONV), ("ca", 0), ("qk", 2 * CONV), ("v", 2 * CONV + 2 * GK), ("r", 2 * CONV + 2 * GK + GV)):
                whole((key, l), w2, c0, BANK, (lin, (key, l, 1)), pieces=4, lo="pool" if key == "cg" else "dve")
            for f in range(2):
                whole(("xk", l, f), a["w_xkv_2"][l], f * BANK, BANK, (lin, ("xk", l, 2 * f + 1)), pieces=4, lo="pool" if f else "dve")
            for f in range(2):
                whole(("xv", l, f), a["w_xkv_2"][l], D + f * BANK, BANK, (lin, ("xv", l, f, 1)), pieces=4, lo="pool")
            square("mix", l, a["w_mix_out_2"][l], (CT, 0), "pool")
            for f in range(2):
                whole(("xq", l, f), a["w_xq_2"][l], f * BANK, BANK, (lin, ("xq", l, 2 * f + 1)), pieces=4, lo="dve" if f else "pool")
            square("xo", l, a["w_xo_2"][l], (0, 4))
            for j in range(FT2 // 2):
                v = view(len(stream), KT, BANK)
                tile(("ffn", l, j), [(v[:, :, 0:SEQ], rows(a["w_ffn_in_2"][l], j * SEQ, SEQ)),
                                     (v[:, :, SEQ:BANK], rows(a["w_ffn_in_2"][l], DFF2 + j * SEQ, SEQ))], (lin, ("ffn", l, 2 * j + 1)), 4, "dve" if j else "pool")
            for j in range(-(-FT2 // 4)):
                whole(("ffo", l, j), a["w_ffn_out_2"][l], 0, D, None if 4 * j + 4 < FT2 else (lin, ("ffo", l, 1, 1)), 4 * j, min(4, FT2 - 4 * j), pieces=min(4, FT2 - 4 * j))
        place = {key: n for n, (key, _, _) in enumerate(stream)}
        due, loads = [], [0] * SLOTS
        for n, (_, parts, _) in enumerate(stream):
            loads[n % SLOTS] += 16 * len(parts)
            due.append(loads[n % SLOTS])

        def arrived(eng, key):
            n = place[key]
            eng.wait_ge(slot_loaded[n % SLOTS], due[n])
            return n

        parts, from_sbuf = [], []
        for l in range(L1):
            parts += [("oT", l, b) for b in range(4)] + [("mixT", l, t, f) for t in range(T) for f in range(2)]
            made_here = [("n2", l, t, f) for t in range(T) for f in range(2)] + [("up", l, j, b) for j in range(D_FF // BANK) for b in range(2)]
            parts += made_here
            from_sbuf += made_here
        parts += [("memT", t, f) for t in range(T) for f in range(2)]
        for l in range(L2):
            parts += [("hT", l, t, f) for t in range(T) for f in range(2)] + [("goT", l, t) for t in range(T)] + [("conv", l)]
            parts += [("h1T", l, t, f) for t in range(T) for f in range(2)] + [("xO", l, t, f) for t in range(T) for f in range(2)]
            parts += [("h2T", l, t, f) for t in range(T) for f in range(2)] + [("ffn", l, f) for f in range(FT2)]
            from_sbuf += [("conv", l)] + [("ffn", l, f) for f in range(FT2)]
        part_at = {key: n + 1 for n, key in enumerate(parts)}
        split_at = {key: n + 1 for n, key in enumerate(from_sbuf)}
        made_at = {key: n + 1 for n, key in enumerate(k for k in from_sbuf if k[0] in ("n2", "up"))}

        norms = [(w, l) for l in range(L1) for w in ("n1", "mla", "n2")] + ["final", "ln0"] \
            + [(w, l) for l in range(L2) for w in ("gla", "conv", "ln1", "ln2", "ln3")]
        norm_at = {key: n for n, key in enumerate(norms)}
        SQUARES = {"n1": 2, "mla": 4, "n2": 2, "gla": 8}
        sq_due, s = {}, 0
        for key in norms:
            s += 2 if key == "final" else SQUARES.get(key[0], 0)
            sq_due[key] = s
        BY_ROWS = ("n1", "n2", "final", "ln0", "ln1", "ln2", "ln3")
        roots = [(key, t) for key in norms for t in range(T if (key if isinstance(key, str) else key[0]) in BY_ROWS else 1)]
        i = roots.index(("final", 0))
        roots[i:i + 2 * T] = [(key, t) for t in range(T) for key in ("final", "ln0")]
        root_at = {key: n + 1 for n, key in enumerate(roots)}
        normed_due = {(w, l): [6 * l + 2 * i + t + 1 for t in range(T)] for l in range(L1) for i, w in enumerate(("n1", "mla", "n2"))}
        updates = [(w, l) for l in range(L1) for w in ("out", "down")] + ["final", "ln0"] + [(w, l) for l in range(L2) for w in ("ln1", "ln2", "ln3")]
        update_at, s = {}, 0
        for keys in [[k] for k in updates if k not in ("final", "ln0")][:2 * L1] + [["final", "ln0"]] + [[k] for k in updates if k[0] in ("ln1", "ln2", "ln3")]:
            for t in range(T):
                for k in keys:
                    s += 1
                    update_at[k, t] = s
        gains = ["final", "ln0"] + [(w, l) for l in range(L2) for w in ("ln1", "ln2", "ln3")]
        gains_due, s = {}, [0, 0]
        for n, key in enumerate(gains):
            s[n % 2] += 16 if n == 0 else 32
            gains_due[key] = s[n % 2]
        NP1 = len(PATHS1)
        LAST_ATT1 = L1 * NP1

        def att1(l, i):
            return l * NP1 + i

        def att2(l, t):
            return LAST_ATT1 + l * T + t

        block = ctx.enter_context(nc.Block())

        @block.sync
        def _(sp):
            for t in range(T):
                sp.dma_start(x[:, t, :], a["x"][0, t * P:(t + 1) * P, :]).then_inc(x_loaded[t], 16)
            for n, (_, parts, _) in enumerate(stream):
                if n >= SLOTS:
                    key, _, last = stream[n - SLOTS]
                    if key in first_piece:
                        sp.wait_ge(*lo_due[sum(first_piece[key]) - 1])
                    else:
                        sp.wait_ge(last[0].filled, last[0].at[last[1]] + 1)
                for dst, src in parts:
                    sp.dma_start(dst, src).then_inc(slot_loaded[n % SLOTS], 16)
            for t in range(T):
                sp.wait_ge(x_updated, T * (len(updates) - 1) + t + 1)
                sp.dma_start(out[0, t * P:(t + 1) * P, :], x[:, t, :]).then_inc(stored, 16)
            sp.wait_ge(stored, 16 * T)

        @block.tensor
        def _(pe):
            def by_tokens(key, xT, w, t, kn, n, c0=0):
                bank = lin.open(pe, key)
                for k in range(kn):
                    m = pe.matmul(bank[:, 0:n], xT[:, k, t * P:(t + 1) * P], w[:, k, c0:c0 + n], start=(k == 0), stop=(k == kn - 1))
                m.then_inc(lin.filled, 1)

            def turn_over(key, sources):
                bank = small.open(pe, key)
                for i, src in enumerate(sources):
                    m = pe.transpose(bank[0:src.shape[-1], i * P:i * P + src.shape[0]], src, ident[:, :])
                m.then_inc(small.filled, 1)

            def products(hi, lo, x_hi, x_lo):
                return ((hi, x_hi), (hi, x_lo), (lo, x_hi))

            def weight_piece(key, i, kn):
                q = first_piece[key][0] + i
                pe.wait_ge(*lo_due[q])
                return [w[:, q % PIECES, :].rearrange("p (k n) -> p k n", k=kn) for w in (w_hi, w_lo)]

            def split_tokens(tile_key, keys, x_hi, x_lo):
                banks = [lin.open(pe, key) for key in keys]
                for i in range(4):
                    pieces = weight_piece(tile_key, i, 2)
                    for t, bank in enumerate(banks):
                        for k in range(2):
                            for j, (v, w) in enumerate(products(x_hi, x_lo, *pieces)):
                                m = pe.matmul(bank, v(2 * i + k, t), w[:, k, :], start=(i + k + j == 0), stop=(i == 3 and k == 1 and j == 2))
                        if i == 3:
                            m.then_inc(lin.filled, 1)
                    if i < 3:
                        m.then_inc(pieces_used, 1)

            def by_tile(v):
                return lambda k, t: v[:, k, t * P:(t + 1) * P]

            def split_features(tile_key, keys, columns, x_hi=lambda k: hT_hi[:, k, :], x_lo=lambda k: hT_lo[:, k, :]):
                banks = [lin.open(pe, key) for key in keys]
                for i in range(4):
                    hi, lo = weight_piece(tile_key, i, 2)
                    for bank, c0s in zip(banks, columns):
                        for n, c0 in enumerate(c0s):
                            for k in range(2):
                                for j, (w, v) in enumerate(products(hi, lo, x_hi, x_lo)):
                                    m = pe.matmul(bank[:, n * SEQ:(n + 1) * SEQ], w[:, k, c0:c0 + P], v(2 * i + k),
                                                  start=(i + n + k + j == 0), stop=(i == 3 and n == 1 and k == 1 and j == 2), skip_group_check=True)
                        if i == 3:
                            m.then_inc(lin.filled, 1)
                    if i < 3:
                        m.then_inc(pieces_used, 1)

            def long_sum(name, l, x_hi, x_lo, n_k, ready, k0s=None, after_piece=None):
                keys = [(name, l, t, f) for t in range(T) for f in range(2)]
                banks = [None] * 4
                n_tiles = -(-n_k // 4)
                for j in range(n_tiles):
                    kn = min(4, n_k - 4 * j)
                    last = j == n_tiles - 1
                    at = [(t, f) for t in range(T) for f in range(2)]
                    ready(j, kn)
                    k0 = k0s[j] if k0s else 4 * j
                    pieces = [None] * kn
                    order = [(k, i) for i in range(4) for k in range(kn)] if last else [(k, i) for k in range(kn) for i in range(4)]
                    if j == 0 and n_tiles > 2:
                        order = [(k, i) for pair in ((0, 1), (2, 3)) for k in range(kn) for i in pair]
                    for k, i in order:
                        if pieces[k] is None:
                            pieces[k] = weight_piece((name, l, j), k, 1)
                        t, f = at[i]
                        if banks[i] is None:
                            banks[i] = lin.open(pe, keys[i])
                        for w, (xs, ws) in enumerate(products(x_hi, x_lo, *pieces[k])):
                            m = pe.matmul(banks[i], xs[:, k0 + k, t * P:(t + 1) * P], ws[:, 0, f * BANK:(f + 1) * BANK],
                                          start=(j + k + w == 0), stop=(last and k == kn - 1 and w == 2))
                        if last:
                            if k == kn - 1:
                                m.then_inc(lin.filled, 1)
                            elif i == 3:
                                m.then_inc(pieces_used, 1)
                        elif i == 3:
                            m.then_inc(pieces_used, 1)
                            if after_piece:
                                after_piece(j, k)

            pe.wait_ge(ident_made, 1)
            for l in range(L1):
                nn = norm_at[("n1", l)]
                for t in range(T):
                    pe.wait_ge(normed, normed_due[("n1", l)][t])
                    for f in range(2):
                        turn_over(("n1", l, t, f), [hn[:, t, (4 * f + i) * P:(4 * f + i + 1) * P] for i in range(4)])
                small.wait_moved(pe, ("n1", l, 1, 1))

                def z_tile(j):
                    n = arrived(pe, ("z", l, j))
                    for t in range(T):
                        by_tokens(("z", l, j, t), hT, view(n, KT, Z_TILES[j][1]), t, KT, Z_TILES[j][1])

                def gate_unit(g):
                    j, t = g // 2, g % 2
                    n = arrived(pe, ("gate", l, j))
                    by_tokens(("gate", l, j, t), hT, view(n, KT, BANK), t, KT, BANK)

                for j in range(3):
                    z_tile(j)
                if l == 0:
                    pe.wait_ge(consts_made, 1)
                for t in range(T):
                    pe.wait_ge(normed, normed_due[("mla", l)][t])
                    turn_over(("cT", l, t), [z[:, t, i * P:(i + 1) * P] for i in range(3)])
                z_tile(3)
                n = arrived(pe, ("u", l))
                for t in range(T):
                    small.wait_moved(pe, ("cT", l, t))
                    by_tokens(("uq", l, t), cT, view(n, 2, 384), t, 2, 384)
                    by_tokens(("ukv", l, t), cT[:, 2:3, :], view(n, 1, 512, 768), t, 1, 512)
                z_tile(4)
                pe.wait_ge(decay_ready, l + 1)
                bank = small.open(pe, ("cq", l))
                pe.matmul(bank[:, 0:4], upto[:, 0:P], lf[:, 2, 0, :], start=True, stop=True)
                pe.matmul(bank[:, 4:8], ones, lf[:, 2, 0, :], start=True, stop=False)
                pe.matmul(bank[:, 4:8], upto[:, 0:P], lf[:, 2, 1, :], start=False, stop=True).then_inc(small.filled, 1)
                for f in range(2):
                    bank = lin.open(pe, ("ck", l, f)).rearrange("p (h k) -> p h k", h=2)
                    pe.matmul(bank, ones, decay_rows[0][:, 2 * f:2 * f + 2, :], start=True, stop=False)
                    for h in range(2):
                        m = pe.matmul(bank[:, h, P:SEQ], ones, decay_rows[1][:, 2 * f + h, :], start=False, stop=(h == 1))
                    m.then_inc(lin.filled, 1)
                for t in range(T):
                    turn_over(("foxT", l, t), [z[:, t, FOX_Q + i * P:FOX_Q + (i + 1) * P] for i in range(4)])
                pe.wait_ge(staged, l + 1)
                for t in range(T):
                    turn_over(("nsa", l, t), [z[:, t, NSA_Q:NSA_Q + P], z[:, t, NSA_Q + P:NSA_Q + 2 * P], stage[:, t, 0, :], stage[:, t, 1, :]])
                for t in range(T):
                    turn_over(("idx", l, t), [z[:, t, DSA_QI:DSA_QI + P], z[:, t, DSA_QI + P:DSA_QI + 2 * P], stage[:, t, 4, :], stage[:, t, 5, :]])
                gate_unit(0)
                gate_unit(1)
                n = arrived(pe, ("cmp", l))
                pe.wait_ge(cmp_rows, l + 1)
                kd = slot_of(n)[:, 0:CMP_PAIRS * P].rearrange("p (a e) -> p a e", e=P)
                vd = slot_of(n)[:, CMP_PAIRS * P:CMP_PAIRS * (P + HD)].rearrange("p (a e) -> p a e", e=HD)
                bank = small.open(pe, ("comp", l))
                for i in range(CMP_PAIRS):
                    pe.matmul(bank[:, 0:NCMP], kd[:, i, :], cmpR[:, 0, i, :], start=(i == 0), stop=(i == CMP_PAIRS - 1))
                for i in range(CMP_PAIRS):
                    m = pe.matmul(bank[0:NCMP, 64:64 + HD], cmpR[:, 1, i, :], vd[:, i, :], start=(i == 0), stop=(i == CMP_PAIRS - 1))
                m.then_inc(small.filled, 1)
                pe.wait_ge(mla_roped, l + 1)
                for w, h0 in (("mq", 0), ("mk", 4)):
                    for t in range(T):
                        turn_over((w, l, t), [mqk[:, t, h0 + h, :] for h in range(4)])
                for t in range(T):
                    turn_over(("dsa", l, t), [z[:, t, DSA_Q:DSA_Q + P], z[:, t, DSA_Q + P:DSA_Q + 2 * P], stage[:, t, 2, :], stage[:, t, 3, :]])
                small.wait_moved(pe, ("dsa", l, 1))
                for t in range(T):
                    nk = P * (t + 1)
                    for f in range(4):
                        bank = lin.open(pe, ("idx", l, t, f))
                        for i in range(2):
                            h = f + 4 * i
                            r = slice(IDX_DIM * (h % 4), IDX_DIM * (h % 4 + 1))
                            m = pe.matmul(bank[:, i * SEQ:i * SEQ + nk], attT[r, S_QI + h // 4, t * P:(t + 1) * P], attT[r, S_KI, 0:nk], start=True, stop=True)
                        m.then_inc(lin.filled, 1)
                small.wait_moved(pe, ("comp", l))
                g = 2
                for i, (path, t) in enumerate(PATHS1):
                    aa = att1(l, i)
                    nk = NCMP if path == "cmp" else P * (t + 1)
                    if aa:
                        pe.wait_ge(probs_made, aa)
                    for s, h in enumerate(BY_SLOT):
                        r = slice(HD * (h % 2), HD * (h % 2 + 1))
                        tq = slice(t * P, (t + 1) * P)
                        if path == "mla":
                            q, k = attT[0:MLA_HD, S_MLA_Q + h, tq], attT[0:MLA_HD, S_MLA_K + h, 0:nk]
                        elif path == "fox":
                            q, k = attT[r, S_FOX_Q + h // 2, tq], attT[r, S_FOX_K + h // 2, 0:nk]
                        elif path == "dsa":
                            q, k = attT[r, S_DSA_Q + h // 2, tq], attT[r, S_DSA_K, 0:nk]
                        elif path == "cmp":
                            q, k = attT[r, S_NSA_Q + h // 2, tq], kcmpT[r, :]
                        else:
                            q, k = attT[r, S_NSA_Q + h // 2, tq], attT[r, S_KS if path == "sel" else S_KW, 0:nk]
                        m = pe.matmul(scores[:, s, 0:nk], q, k, start=True, stop=True)
                    m.then_inc(scores_filled, 1)
                    for _ in range(GATES_AFTER[i]):
                        if g < 2 * GATE_TILES:
                            gate_unit(g)
                            g += 1
                    b = aa % 2
                    if path == "cmp":
                        pe.wait_ge(probs_final, cmp_final(l, t))
                        turn_over(("PT", l, i, 0), [probs[:, b, h, 0:NCMP] for h in range(HEADS)])
                    else:
                        pe.wait_ge(probs_made, aa + 1)
                        for kb in range(t + 1):
                            turn_over(("PT", l, i, kb), [probs[:, b, h, kb * P:(kb + 1) * P] for h in range(HEADS)])
                    kbs = 1 if path == "cmp" else t + 1
                    bank = small.open(pe, ("PV", l, i))
                    small.wait_moved(pe, ("PT", l, i, kbs - 1))
                    for s, h in enumerate(BY_SLOT):
                        for kb in range(kbs):
                            if path == "cmp":
                                p, v = PT[0:NCMP, b, 0, s, :], vcmp[0:NCMP, :]
                            else:
                                p = PT[:, b, kb, s, :]
                                c = {"mla": 0, "fox": FOX_V + h * HD, "sel": NSA_VS, "win": NSA_VW, "dsa": DSA_V}[path]
                                v = mv[:, kb, h * HD:(h + 1) * HD] if path == "mla" else z[:, kb, c:c + HD]
                            m = pe.matmul(bank[:, h * HD:(h + 1) * HD], p, v, start=(kb == 0), stop=(kb == kbs - 1))
                    m.then_inc(small.filled, 1)
                assert g == 2 * GATE_TILES
                small.wait_moved(pe, ("PV", l, NP1 - 1))
                for b in range(4):
                    turn_over(("oT", l, b), [osb[:, t, b, 2 * c:2 * c + 2, :].rearrange("p h d -> p (h d)") for c in range(2) for t in range(T)])
                for f in range(2):
                    for b in range(4):
                        if f == 0:
                            small.wait_moved(pe, ("oT", l, b))
                        banks = [lin.open(pe, ("lift", l, f, b, t)) for t in range(T)]
                        pieces = weight_piece(("lift", l, f), b, 2)
                        for t in range(T):
                            for k in range(2):
                                for j, (v, w) in enumerate(products(hT_hi, hT_lo2, *pieces)):
                                    m = pe.matmul(banks[t], v[:, 2 * b + k, t * P:(t + 1) * P], w[:, k, :], start=(k + j == 0), stop=(k == 1 and j == 2))
                            m.then_inc(lin.filled, 1)
                for t in range(T):
                    for f in range(2):
                        pe.wait_ge(gated, 4 * l + 2 * f + t + 1)
                        turn_over(("mixT", l, t, f), [gate[:, t, f * BANK + i * P:f * BANK + (i + 1) * P] for i in range(4)])
                small.wait_moved(pe, ("mixT", l, 1, 1))
                long_sum("out", l, hT_hi, hT_lo2, KT, lambda j, kn: None)
                for t in range(T):
                    pe.wait_ge(normed, normed_due[("n2", l)][t])
                    for f in range(2):
                        turn_over(("n2", l, t, f), [hn[:, t, (4 * f + i) * P:(4 * f + i + 1) * P] for i in range(4)])
                pe.wait_ge(split, split_at[("n2", l, 1, 1)])
                for j in range(D_FF // BANK):
                    split_features(("up", l, j), [("up", l, j, b) for b in range(2)], [[2 * b * P, (2 * b + 1) * P] for b in range(2)])
                if l == L1 - 1:
                    pe.wait_ge(mem_loaded, 16)
                    for t in range(T):
                        for f in range(2):
                            turn_over(("memT", t, f), [hn[:, t, (4 * f + i) * P:(4 * f + i + 1) * P] for i in range(4)])
                long_sum("down", l, up_hi, up_lo, D_FF // P, lambda j, kn: pe.wait_ge(split, split_at[("up", l, j, 1)]))

            for l in range(L2):
                def turn_x(name, update):
                    for t in range(T):
                        pe.wait_ge(x_updated, update_at[update, t])
                        for f in range(2):
                            turn_over((name, l, t, f), [x[:, t, (4 * f + i) * P:(4 * f + i + 1) * P] for i in range(4)])
                    small.wait_moved(pe, (name, l, 1, 1))

                turn_x("hT", "ln0" if l == 0 else ("ln3", l - 1))
                n = arrived(pe, ("alow", l))
                bank = small.open(pe, ("alow", l))
                w = view(n, KT, RANK)
                for k in range(KT):
                    for part in (hT_hi, hT_lo):
                        m = pe.matmul(bank[0:RANK, 0:SEQ], w[:, k, :], part[:, k, :].bitcast(F32), start=(k == 0 and part is hT_hi), stop=(k == KT - 1 and part is hT_lo))
                m.then_inc(small.filled, 1)

                def proj(key):
                    split_tokens((key, l), [(key, l, t) for t in range(T)], by_tile(hT_hi), by_tile(hT_lo))

                proj("cg")
                proj("ca")
                for t in range(T):
                    lin.wait_moved(pe, ("ca", l, t))
                    turn_over(("uT", l, t), [u2[:, t, i * P:(i + 1) * P] for i in range(4)])
                small.wait_moved(pe, ("alow", l))
                for t in range(T):
                    bank = small.open(pe, ("zlow", l, t))
                    pe.matmul(bank[:, 0:GK], alT[0:RANK + 1, t * P:(t + 1) * P], wa2[0:RANK + 1, l, :], start=True, stop=True).then_inc(small.filled, 1)
                proj("qk")
                proj("v")
                for t in range(T):
                    pe.wait_ge(la_ready, T * l + t + 1)
                    bank = lin.open(pe, ("bc", l, t))
                    pe.matmul(bank[:, 0:GK], blk_upto[:, :], la[:, 0, t, :], start=True, stop=True)
                    pe.matmul(bank[:, GK:2 * GK], blk_after[:, :], la[:, 0, t, :], start=True, stop=True).then_inc(lin.filled, 1)
                bank = small.open(pe, ("blast", l))
                for g in range(2):
                    for t in range(T):
                        m = pe.matmul(bank[:, 4 * g + 2 * t:4 * g + 2 * t + 2], la[:, 0, t, g * P:(g + 1) * P], blk_sum[:, :], start=True, stop=True)
                m.then_inc(small.filled, 1)
                proj("r")
                for t in range(T):
                    pe.wait_ge(qkd_ready, T * l + t + 1)
                    turn_over(("qeT", l, t), [ex2[:, s, t, g * P:(g + 1) * P] for s in range(2) for g in range(2)])
                for t in range(T):
                    small.wait_moved(pe, ("qeT", l, t))
                    for e in range(2):
                        r = slice(HD * e, HD * (e + 1))
                        bank = lin.open(pe, ("att", l, t, e))
                        for g in range(2):
                            m = pe.matmul(bank[:, g * P:(g + 1) * P], keT[r, g, t * P:(t + 1) * P], qeT[r, g, t * P:(t + 1) * P], start=True, stop=True)
                        m.then_inc(lin.filled, 1)
                lin.wait_moved(pe, ("v", l, 1))
                for c in range(3):
                    bank = lin.open(pe, ("upd", l, c))
                    r = slice(CHUNK * (c % 2), CHUNK * (c % 2 + 1))
                    for g in range(2):
                        m = pe.matmul(bank[:, g * SEQ:(g + 1) * SEQ], ex2[r, 2, c // 2, g * P:(g + 1) * P], v2[r, c // 2, g * SEQ:(g + 1) * SEQ], start=True, stop=True)
                    m.then_inc(lin.filled, 1)
                small.wait_moved(pe, ("memT", 1, 1))
                for f in range(2):
                    split_features(("xk", l, f), [("xk", l, 2 * f + b) for b in range(2)], [[2 * b * P, (2 * b + 1) * P] for b in range(2)],
                                   lambda k: mem_hi[:, :, k, :], lambda k: mem_lo[:, :, k, :])

                def mem_values(f):
                    split_tokens(("xv", l, f), [("xv", l, f, t) for t in range(T)], lambda k, t: mem_hi[:, t, k, :], lambda k, t: mem_lo[:, t, k, :])

                mem_values(0)
                lin.wait_moved(pe, ("upd", l, 2))
                for t in range(T):
                    for e in range(2):
                        lin.wait_moved(pe, ("att", l, t, e))
                        bank = lin.open(pe, ("go", l, t, e))
                        r = slice(HD * e, HD * (e + 1))
                        chunks = [c for c in (2 * t, 2 * t + 1) if c > 0]
                        for g in range(2):
                            h = 2 * g + e
                            o = bank[:, g * P:(g + 1) * P]
                            pe.matmul(o, gattT[:, t, h, :], v2[:, t, h * P:(h + 1) * P], start=True, stop=False)
                            for c in chunks:
                                m = pe.matmul(o, qez[r, g, c, :], state[r, c - 1, g, :], start=False, stop=(c == chunks[-1]))
                        m.then_inc(lin.filled, 1)
                pe.wait_ge(conv_summed, l + 1)
                bank = small.open(pe, ("cmean", l))
                for c in range(CT):
                    m = pe.matmul(bank[:, 0:SEQ], ones, acc[:, c, :], start=(c == 0), stop=(c == CT - 1))
                m.then_inc(small.filled, 1)
                mem_values(1)
                for t in range(T):
                    pe.wait_ge(go_ready, T * l + t + 1)
                    turn_over(("goT", l, t), [go2[:, t, i * P:(i + 1) * P] for i in range(4)])
                pe.wait_ge(conv_squared, l + 1)
                bank = small.open(pe, ("cvar", l))
                for t in range(T):
                    for c in range(CT):
                        m = pe.matmul(bank[:, t:t + 1], sq2[:, c, t * P:(t + 1) * P], ones[:, 0:1], start=(c == 0), stop=(c == CT - 1))
                m.then_inc(small.filled, 1)
                def mix_ready(j, kn):
                    if j == 0:
                        small.wait_moved(pe, ("goT", l, 1))
                    else:
                        pe.wait_ge(split, split_at[("conv", l)])

                def spread_root(j, k):
                    if (j, k) == (0, 0):
                        pe.wait_ge(root_spread, l + 1)
                        bank = small.open(pe, ("crstd", l))
                        for t in range(T):
                            m = pe.matmul(bank[:, t * P:(t + 1) * P], ones, root_diag[:, t, :], start=True, stop=True)
                        m.then_inc(small.filled, 1)

                long_sum("mix", l, hT_hi, hT_lo2, KT, mix_ready, (CT, 0), spread_root)
                turn_x("h1T", ("ln1", l))
                for f in range(2):
                    split_features(("xq", l, f), [("xq", l, 2 * f + b) for b in range(2)], [[2 * b * P, (2 * b + 1) * P] for b in range(2)],
                                   x_lo=lambda k: hT_lo2[:, k, :])
                lin.wait_moved(pe, ("xq", l, 3))
                lin.wait_moved(pe, ("xv", l, 1, 1))

                def x_scores(t):
                    pe.wait_ge(probs_made, att2(l, t))
                    for h in range(XH):
                        for k in range(2):
                            m = pe.matmul(scores[:, h, :], xqT[:, 2 * h + k, t * P:(t + 1) * P], xkT[:, 2 * h + k, :], start=(k == 0), stop=(k == 1))
                    m.then_inc(scores_filled, 1)

                def x_out(t):
                    b = att2(l, t) % 2
                    pe.wait_ge(probs_final, T * L1 + T * l + t + 1)
                    for kb in range(T):
                        turn_over(("xPT", l, t, kb), [probs[:, b, h, kb * P:(kb + 1) * P] for h in range(XH)])
                    small.wait_moved(pe, ("xPT", l, t, 1))
                    for f in range(2):
                        bank = lin.open(pe, ("xO", l, t, f))
                        for i in range(4):
                            h, c = 2 * f + i // 2, i % 2
                            for kb in range(T):
                                m = pe.matmul(bank[:, i * P:(i + 1) * P], xv[:, kb, h * XD + c * P:h * XD + (c + 1) * P], PT[:, b, kb, h, :], start=(kb == 0), stop=(kb == 1))
                        m.then_inc(lin.filled, 1)

                x_scores(0)
                x_scores(1)
                x_out(0)
                x_out(1)
                lin.wait_moved(pe, ("xO", l, 1, 1))
                long_sum("xo", l, hT_hi, hT_lo2, KT, lambda j, kn: None)
                turn_x("h2T", ("ln2", l))
                for j in range(FT2 // 2):
                    split_features(("ffn", l, j), [("ffn", l, 2 * j + b) for b in range(2)], [[b * P, SEQ + b * P] for b in range(2)])
                long_sum("ffo", l, ff_hi, ff_lo, FT2, lambda j, kn: pe.wait_ge(split, split_at[("ffn", l, 4 * j + kn - 1)]))

        @block.scalar
        def _(act):
            step = Chain(act, act_step)

            def move(turns_, key, dst, take=lambda b: b, func=ACT.Copy, scale=1.0):
                bank = turns_.wait_filled(act, key)
                act.activation(dst, take(bank), func, scale=scale).then_inc(turns_.moved["act"], 1)

            def four(bank):
                return bank.rearrange("p (i q) -> p i q", i=4)

            def softmax_exp(aa, scale, nk, sums=True):
                b = aa % 2
                act.wait_ge(bias_ready, aa + 1)
                for h in range(HEADS):
                    m = act.activation(probs[:, b, h, 0:nk], scores[:, h, 0:nk], ACT.Exp, bias=softmax_s[:, b, 1, h:h + 1], scale=scale,
                                       accum_out=softmax_s[:, b, 2, h:h + 1] if sums else None)
                m.then_inc(probs_made, 1)

            def squares(key, sources, junk, after=lambda t: None):
                nn = norm_at[key]
                done = sq_due[key] - len(sources)
                for i, src in enumerate(sources):
                    after(i)
                    if done + i:
                        act.wait_ge(squares_summed, done + i)
                    act.activation(junk[:, 0:src.shape[-1]], src, ACT.Square, accum_out=stats[:, nn, i:i + 1]).then_inc(squares_summed, 1)

            def row_squares(key, update):
                squares(key, [x[:, t, :] for t in range(T)], up_sq.rearrange("p b n -> p (b n)"),
                        (lambda t: act.wait_ge(x_updated, update_at[update, t])) if update else (lambda t: act.wait_ge(x_loaded[t], 16)))

            def weight_hi(key, which=range(4)):
                q0, n = first_piece[key]
                arrived(act, key)
                raw = slot_of(place[key]).rearrange("p (i n) -> p i n", n=PIECE)
                for i in which[:n]:
                    q = q0 + i
                    if q >= PIECES:
                        act.wait_ge(*piece_done[q - PIECES])
                    act.activation(w_hi[:, q % PIECES, :], raw[:, i, :], ACT.Copy).then_inc(hi_ready, 1)

            def round_part(dst, src, scale=1.0):
                act.activation(dst, src, ACT.Copy, scale=scale).then_inc(rounded, 1)

            def round_turned(name, l, dst=None):
                for t in range(T):
                    for f in range(2):
                        key = (name, t, f) if l is None else (name, l, t, f)
                        bank = small.wait_filled(act, key)
                        round_part(mem_hi[:, t, 4 * f:4 * f + 4, :] if l is None else hT_hi[:, 4 * f:4 * f + 4, t * P:(t + 1) * P], four(bank),
                                   0.5 if name == "mixT" else 1.0)

            act.dma_start(g1[:, 0, 0, :], a["norm1_g"][0].rearrange("(k p) -> p k", p=P), allow_slow_non_contiguous=True).then_inc(first_gain_loaded, 16)
            act.dma_start(pos_i[:, :], a["positions"][0].rearrange("(t p) -> p t", p=P), allow_slow_non_contiguous=True).then_inc(pos_loaded, 16)
            row_squares(("n1", 0), None)
            for l in range(LAYERS):
                for w, name in enumerate(("norm1_g", "norm2_g")):
                    if (l, w) == (0, 0):
                        continue
                    act.dma_start(g1[:, w, l, :], a[name][l].rearrange("(k p) -> p k", p=P), allow_slow_non_contiguous=True).then_inc(params_loaded, 16)
                act.dma_start(gqkv[:, l, 0:2], a["mla_q_norm_g"][l].rearrange("(k p) -> p k", p=P), allow_slow_non_contiguous=True).then_inc(params_loaded, 16)
                act.dma_start(gqkv[:, l, 2:3], a["mla_kv_norm_g"][l].rearrange("(k p) -> p k", p=P), allow_slow_non_contiguous=True).then_inc(params_loaded, 16)
                act.dma_start(fbias[:, l, :], a["fox_f_bias"][l].partition_broadcast(P)).then_inc(params_loaded, 16)
                for w in range(2):
                    act.dma_start(peT[:, l, w, :], a["nsa_cmp_pe"][l, w].rearrange("(i e) d -> (e d) i", e=2), allow_slow_non_contiguous=True).then_inc(params_loaded, 16)
            for l in range(LAYERS):
                for c in range(CT):
                    act.dma_start(conv_wT[:, l, c, :], a["conv_w_2"][l, :, c * P:(c + 1) * P].rearrange("j p -> p j"), allow_slow_non_contiguous=True).then_inc(params2_loaded, 16)
                for w, name in enumerate(("conv_b_2", "conv_ln_g_2", "conv_ln_b_2")):
                    act.dma_start(conv_p[:, w, l, :], a[name][l].rearrange("(k p) -> p k", p=P), allow_slow_non_contiguous=True).then_inc(params2_loaded, 16)
                act.dma_start(gla_g[:, l, :], a["gla_norm_g_2"][l].partition_broadcast(P)).then_inc(params2_loaded, 16)
                act.dma_start(wa2[0:RANK, l, :], a["w_a2_2"][l]).then_inc(params2_loaded, 16)
                act.dma_start(wa2[RANK:RANK + 1, l, :], a["b_a_2"][l:l + 1, :]).then_inc(params2_loaded, 16)

            act.wait_ge(angles_made, 1)
            act.activation(rope[:, :, :, :], red[:, :, :, :], ACT.Sin).then_inc(rope_tables, 1)

            for l in range(L1):
                if l:
                    row_squares(("n1", l), ("down", l - 1))

                def z_out(j):
                    c0, cn = Z_TILES[j]
                    for t in range(T):
                        move(lin, ("z", l, j, t), z[:, t, c0:c0 + cn], lambda b: b[:, 0:cn])

                z_out(0)
                lin.wait_moved(act, ("z", l, 0, 1))
                squares(("mla", l), [z[:, t, 0:MLA_Q] for t in range(T)] + [z[:, t, MLA_Q:MLA_Q + MLA_KV] for t in range(T)], probs[:, 0, 0, :])
                z_out(1)
                z_out(2)
                lin.wait_moved(act, ("z", l, 2, 1))
                act.activation(gn, z[:, :, NSA_G:NSA_G + 12], ACT.Tanh, scale=0.5).then_inc(nsa_tanh, 1)
                z_out(3)
                act.wait_ge(fox_logits, l + 1)
                step(act.activation(lf[:, 1], lf[:, 0], ACT.Abs))
                step.settle()
                step(act.activation(lf[:, 1], lf[:, 1], ACT.Exp, scale=-1.0))
                step.settle()
                act.activation(lf[:, 1], lf[:, 1], ACT.Ln, bias=1.0).then_inc(fox_log, 1)
                for t in range(T):
                    move(lin, ("uq", l, t), mqk[:, t, 0:4, :], lambda b: b[:, 0:384].rearrange("p (h d) -> p h d", h=HEADS))
                    bank = lin.wait_filled(act, ("ukv", l, t)).rearrange("p (h w d) -> p h w d", h=HEADS, w=2)
                    act.activation(mqk[:, t, 4:8, 0:HD], bank[:, :, 0, :], ACT.Copy)
                    act.activation(mv[:, t, :].rearrange("p (h d) -> p h d", h=HEADS), bank[:, :, 1, :], ACT.Copy).then_inc(lin.moved["act"], 1)
                z_out(4)
                for w, s in (("foxT", S_FOX_Q), ("nsa", S_NSA_Q), ("idx", S_QI)):
                    for t in range(T):
                        move(small, (w, l, t), attT[:, s:s + 4, t * P:(t + 1) * P], four)

                def gate_out(g):
                    j, t = g // 2, g % 2
                    move(lin, ("gate", l, j, t), gate[:, t, j * BANK:(j + 1) * BANK], func=ACT.Tanh, scale=0.5)

                gate_out(0)
                gate_out(1)
                for w, s in (("mq", S_MLA_Q), ("mk", S_MLA_K)):
                    for t in range(T):
                        move(small, (w, l, t), attT[0:MLA_HD, s:s + 4, t * P:(t + 1) * P], lambda b: four(b[0:MLA_HD]))
                for t in range(T):
                    move(small, ("dsa", l, t), attT[:, S_DSA_Q:S_DSA_Q + 4, t * P:(t + 1) * P], four)
                for t in range(T):
                    nk = P * (t + 1)
                    for f in range(4):
                        n = 8 * l + 4 * t + f
                        if n >= 2:
                            act.wait_ge(index_used, n - 1)
                        move(lin, ("idx", l, t, f), relu_l[:, n % 2, :, 0:nk], lambda b: b.rearrange("p (h k) -> p h k", h=2)[:, :, 0:nk],
                             func=ACT.Relu, scale=IDX_DIM ** -0.5 * IDX_HEADS ** -0.5)
                act.wait_ge(index_used, 8 * (l + 1))
                g = 2
                for i, (path, t) in enumerate(PATHS1):
                    aa = att1(l, i)
                    b = aa % 2
                    if i == NP1 - 1:
                        weight_hi(("lift", l, 0), [0, 1])
                    softmax_exp(aa, SCALE[path], NCMP if path == "cmp" else P * (t + 1), sums=path != "cmp")
                    for _ in range(GATES_AFTER[i]):
                        if g < 2 * GATE_TILES:
                            gate_out(g)
                            g += 1
                    if path == "cmp":
                        move(small, ("PT", l, i, 0), PT[0:NCMP, b, 0], lambda bk: four(bk[0:NCMP]))
                    else:
                        for kb in range(t + 1):
                            move(small, ("PT", l, i, kb), PT[:, b, kb], four)
                weight_hi(("lift", l, 0), [2, 3])
                for b in range(4):
                    bank = small.wait_filled(act, ("oT", l, b))
                    round_part(hT_hi[:, 2 * b:2 * b + 2, :], bank.rearrange("p (c q) -> p c q", c=2))
                weight_hi(("lift", l, 1))
                weight_hi(("out", l, 0))
                round_turned("mixT", l)
                weight_hi(("out", l, 1))
                row_squares(("n2", l), ("out", l))
                weight_hi(("up", l, 0))
                for t in range(T):
                    for f in range(2):
                        act.wait_ge(made, made_at[("n2", l, t, f)])
                        round_part(hT_hi[:, 4 * f:4 * f + 4, t * P:(t + 1) * P], four(gainedT[:, f, :]))
                n_up = D_FF // BANK
                for j in range(n_up + 1):
                    if j:
                        for b in range(2):
                            bank = lin.wait_filled(act, ("up", l, j - 1, b))
                            if j > 1:
                                act.wait_ge(split, split_at[("up", l, j - 2, b)])
                            act.activation(up_sq[:, b, :], bank, ACT.Relu).then_inc(relued, 1)
                        for b in range(2):
                            act.wait_ge(made, made_at[("up", l, j - 1, b)])
                            c = 4 * (j - 1) + 2 * b
                            round_part(up_hi[:, c:c + 2, :], up_sq[:, b, :].rearrange("p (c q) -> p c q", c=2))
                    if j == n_up and l == L1 - 1:
                        round_turned("memT", None)
                    weight_hi(("up", l, j + 1) if j + 1 < n_up else ("down", l, j + 1 - n_up))
                for j in range(2, n_up):
                    weight_hi(("down", l, j))
            row_squares("final", ("down", L1 - 1))

            for l in range(L2):
                weight_hi(("cg", l))
                round_turned("hT", l)
                act.wait_ge(pads_zeroed, l + 1)
                move(small, ("alow", l), alT[0:RANK, :], lambda b: b[0:RANK, 0:SEQ])
                weight_hi(("ca", l))
                for t in range(T):
                    move(lin, ("cg", l, t), sg2[:, t, :], func=ACT.Tanh, scale=0.5)
                weight_hi(("qk", l))
                for t in range(T):
                    move(small, ("uT", l, t), uT[:, :, PAD + t * P:PAD + (t + 1) * P], four, scale=0.5)
                for t in range(T):
                    small.wait_moved(act, ("zlow", l, t))
                    step(act.activation(la[:, 1, t, :], la[:, 0, t, :], ACT.Abs))
                    step.settle()
                    step(act.activation(la[:, 1, t, :], la[:, 1, t, :], ACT.Exp, scale=-1.0))
                    step.settle()
                    act.activation(la[:, 1, t, :], la[:, 1, t, :], ACT.Ln, bias=1.0).then_inc(low_log, 1)
                weight_hi(("v", l))
                for t in range(T):
                    move(lin, ("qk", l, t), qk2[:, t, :])
                weight_hi(("r", l))
                for t in range(T):
                    move(lin, ("v", l, t), v2[:, t, :])
                for t in range(T):
                    bank = lin.wait_filled(act, ("bc", l, t))
                    act.activation(ex2[:, 0, t, :], bank[:, 0:GK], ACT.Exp, scale=1 / 16)
                    act.activation(ex2[:, 1, t, :], bank[:, 0:GK], ACT.Exp, scale=-1 / 16)
                    act.activation(ex2[:, 2, t, :], bank[:, GK:], ACT.Exp, scale=1 / 16).then_inc(lin.moved["act"], 1)
                move(small, ("blast", l), dec, lambda b: b[:, 0:8].rearrange("p (g c) -> p g c", g=2), func=ACT.Exp, scale=1 / 16)
                weight_hi(("xk", l, 0))
                for t in range(T):
                    bank = lin.wait_filled(act, ("r", l, t))
                    act.activation(sr2[:, t, :], bank, ACT.Tanh, scale=0.5).then_inc(r_tanh, 1)
                for t in range(T):
                    bank = four(small.wait_filled(act, ("qeT", l, t)))
                    act.activation(qeT[:, :, t * P:(t + 1) * P], bank[:, 0:2, :], ACT.Copy)
                    act.activation(keT[:, :, t * P:(t + 1) * P], bank[:, 2:4, :], ACT.Copy)
                    act.activation(qez[:, :, 2 * t, 0:CHUNK], bank[:, 0:2, 0:CHUNK], ACT.Copy)
                    act.activation(qez[:, :, 2 * t + 1, CHUNK:], bank[:, 0:2, CHUNK:], ACT.Copy).then_inc(small.moved["act"], 1)
                for f in range(2):
                    weight_hi(("xk", l, 1) if f == 0 else ("xv", l, 0))
                    for b in (2 * f, 2 * f + 1):
                        move(lin, ("xk", l, b), xkT[:, 2 * b:2 * b + 2, :], lambda bk: bk.rearrange("p (c q) -> p c q", c=2))

                def mem_values(f):
                    for t in range(T):
                        move(lin, ("xv", l, f, t), xv[:, t, f * BANK:(f + 1) * BANK])

                weight_hi(("xv", l, 1))
                mem_values(0)
                lin.wait_moved(act, ("go", l, 1, 1))
                nn = norm_at[("gla", l)]
                for t in range(T):
                    for h in range(HEADS):
                        act.wait_ge(squares_summed, sq_due[("gla", l)] - T * HEADS + HEADS * t + h)
                        act.activation(gla_junk, go2[:, t, h * P:(h + 1) * P], ACT.Square, accum_out=stats[:, nn, 4 * t + h:4 * t + h + 1]).then_inc(squares_summed, 1)
                act.wait_ge(conv_centred, l + 1)
                act.activation(sq2[:, :, :], acc[:, :, :], ACT.Square).then_inc(conv_squared, 1)
                weight_hi(("mix", l, 0))
                mem_values(1)
                for t in range(T):
                    bank = small.wait_filled(act, ("goT", l, t))
                    round_part(hT_hi[:, 4:8, t * P:(t + 1) * P], four(bank))
                act.wait_ge(conv_affine, l + 1)
                act.activation(sq2[:, :, :], acc[:, :, :], ACT.Tanh, scale=0.5).then_inc(conv_tanh, 1)
                act.wait_ge(conv_out, l + 1)
                round_part(hT_hi[:, 0:CT, :], acc[:, :, :])
                weight_hi(("mix", l, 1))
                weight_hi(("xq", l, 0))
                round_turned("h1T", l)
                weight_hi(("xq", l, 1))
                for b in range(4):
                    if b == 2:
                        weight_hi(("xo", l, 0))
                    move(lin, ("xq", l, b), xqT[:, 2 * b:2 * b + 2, :], lambda bk: bk.rearrange("p (c q) -> p c q", c=2))
                for t in range(T):
                    softmax_exp(att2(l, t), XD ** -0.5, SEQ)
                for t in range(T):
                    b = att2(l, t) % 2
                    for kb in range(T):
                        move(small, ("xPT", l, t, kb), PT[:, b, kb], four)
                    for f in range(2):
                        bank = lin.wait_filled(act, ("xO", l, t, f))
                        round_part(hT_hi[:, 4 * f:4 * f + 4, t * P:(t + 1) * P], four(bank))
                weight_hi(("xo", l, 1))
                weight_hi(("ffn", l, 0))
                round_turned("h2T", l)
                n_ffn, n_ffo = FT2 // 2, -(-FT2 // 4)
                for j in range(n_ffn + 1):
                    if j:
                        for f in (2 * j - 2, 2 * j - 1):
                            bank = lin.wait_filled(act, ("ffn", l, f))
                            act.activation(ffs[:, f % 2, :], bank[:, 0:SEQ], ACT.Tanh, scale=0.5).then_inc(ff_tanh, 1)
                        for f in (2 * j - 2, 2 * j - 1):
                            lin.wait_moved(act, ("ffn", l, f))
                            round_part(ff_hi[:, f, :], ffp[:, f % 2, :])
                    weight_hi(("ffn", l, j + 1) if j + 1 < n_ffn else ("ffo", l, j + 1 - n_ffn))
                for j in range(2, n_ffo):
                    weight_hi(("ffo", l, j))

        @block.vector
        def _(dve):
            step = Chain(dve, dve_step)

            def moved(ins, turns_):
                ins.then_inc(turns_.moved["dve"], 1)

            def four(bank):
                return bank.rearrange("p (i q) -> p i q", i=4)

            def norm_mean(key, parts):
                nn = norm_at[key]
                dve.wait_ge(squares_summed, sq_due[key])
                for i, (src, dst, n, eps) in enumerate(parts):
                    m = dve.tensor_scalar(stats[:, nn, dst], stats[:, nn, src], 1.0 / n, eps, ALU.mult, ALU.add)
                m.then_inc(mean_ready, 1)
                dve.wait_ge(rstd_ready, root_at[key, 0])
                return nn

            def rms_root(key, t):
                nn = norm_at[key]
                dve.wait_ge(squares_summed, sq_due[key] - T + t + 1)
                dve.tensor_scalar(stats[:, nn, 8 + t:9 + t], stats[:, nn, t:t + 1], 1.0 / D, NORM_EPS, ALU.mult, ALU.add).then_inc(mean_ready, 1)
                dve.wait_ge(rstd_ready, root_at[key, t])
                return stats[:, nn, 12 + t:13 + t]

            def rms_rows(key, t):
                root = rms_root(key, t)
                dve.tensor_scalar(hn[:, t, :], x[:, t, :], root, None, ALU.mult).then_inc(normed, 1)

            def rms_sum(name, key, l):
                for t in range(T):
                    for f in range(2):
                        bank = lin.wait_filled(dve, (name, l, t, f))
                        xv_ = x[:, t, f * BANK:(f + 1) * BANK]
                        moved(dve.tensor_tensor(xv_, bank, xv_, ALU.add), lin)
                    lin.wait_moved(dve, (name, l, t, 1))
                    dve.sem_inc(x_updated, 1)
                    if key:
                        rms_rows(key, t)

            def weight_lo(key, which=range(4)):
                q0, n = first_piece[key]
                raw = slot_of(place[key]).rearrange("p (i n) -> p i n", n=PIECE)
                for i in which:
                    if i < n:
                        q = q0 + i
                        dve.wait_ge(hi_ready, q + 1)
                        dve.tensor_tensor(w_lo[:, q % PIECES, :], raw[:, i, :], w_hi[:, q % PIECES, :], ALU.subtract).then_inc(lo_ready["dve"], 1)

            def rest_part(key, dst, src, hi):
                dve.wait_ge(rounded, part_at[key])
                return dve.tensor_tensor(dst, src, hi, ALU.subtract).then_inc(split, 1)

            def rest_bank(turns_, key, dst, hi, take=four, scale=None):
                dve.wait_ge(rounded, part_at[key])
                src = take(turns_.bank(key))
                if scale is None:
                    moved(dve.tensor_tensor(dst, src, hi, ALU.subtract), turns_)
                else:
                    moved(dve.scalar_tensor_tensor(out=dst, in0=src, scalar=scale, in1=hi, op0=ALU.mult, op1=ALU.subtract), turns_)

            def rest_turned(name, l, lo):
                for t in range(T):
                    q = slice(t * P, (t + 1) * P)
                    for f in range(2):
                        k = slice(4 * f, 4 * f + 4)
                        rest_bank(small, (name, l, t, f), lo[:, k, q], hT_hi[:, k, q], scale=0.5 if name == "mixT" else None)

            def gained(name, l, w):
                for t in range(T):
                    for f in range(2):
                        bank = four(small.wait_filled(dve, (name, l, t, f)))
                        moved(dve.tensor_tensor(hT[:, 4 * f:4 * f + 4, t * P:(t + 1) * P], bank,
                                                g1[:, w, l, 4 * f:4 * f + 4].unsqueeze(2).to_broadcast([P, 4, P]), ALU.mult), small)

            def softmax_bias(aa, nk, scale, bias=None, k0=0):
                b = aa % 2
                dve.wait_ge(scores_filled, aa + 1)
                if bias is not None:
                    step(dve.tensor_tensor(scores[:, :, k0:nk], scores[:, :, k0:nk], bias, ALU.add))
                    step.settle()
                step(dve.tensor_reduce(softmax_s[:, b, 0, :], scores[:, :, 0:nk], AX, ALU.max, negate=True))
                step.settle()
                dve.tensor_scalar(softmax_s[:, b, 1, :], softmax_s[:, b, 0, :], scale, None, ALU.mult).then_inc(bias_ready, 1)

            def heads(v, n):
                return v.unsqueeze(1).to_broadcast([P, HEADS, n])

            def take_top(t):
                nk = P * (t + 1)
                s = index_bias[t]
                for _ in range(KEEP // 8):
                    step(dve.max(best, s))
                    step.settle()
                    step(dve.match_replace(s, best, s, TAKEN))
                    step.settle()
                step(dve.tensor_scalar(s, s, TAKEN / 2, MASKED, ALU.is_gt, ALU.mult))
                step.settle()
                step(dve.tensor_tensor(s, s, causal[:, SEQ - nk:SEQ], ALU.min))
                step.settle()

            for t in range(T):
                rms_rows(("n1", 0), t)
            dve.wait_ge(first_gain_loaded, 16)
            gained("n1", 0, 0)
            dve.wait_ge(pos_loaded, 16)
            dve.wait_ge(consts_made, 1)
            step(dve.tensor_copy(pos_f[:, :], pos_i[:, :]))
            step.settle()
            for t in range(T):
                step(dve.tensor_scalar(ang[:, t, :], freq[:, :], pos_f[:, t:t + 1], None, ALU.mult))
            step.settle()
            for s, quarter in ((0, 0.0), (1, 0.25)):
                step(dve.tensor_scalar(turns[:, s], ang[:, :, :], 1 / (2 * np.pi), quarter, ALU.mult, ALU.add))
            step.settle()
            step(dve.tensor_scalar(turns[:, :], turns[:, :], ROUND, None, ALU.add))
            step.settle()
            step(dve.tensor_scalar(turns[:, :], turns[:, :], -ROUND, None, ALU.add))
            step.settle()
            for s in range(2):
                step(dve.scalar_tensor_tensor(out=red[:, s], in0=turns[:, s], scalar=-TWO_PI[0], in1=ang[:, :, :], op0=ALU.mult, op1=ALU.add))
            for part in TWO_PI[1:]:
                step.settle()
                step(dve.scalar_tensor_tensor(out=red[:, :], in0=turns[:, :], scalar=-part, in1=red[:, :], op0=ALU.mult, op1=ALU.add))
            step.settle()
            step(dve.tensor_scalar(red[:, 1], red[:, 1], np.pi / 2, None, ALU.add))
            step.settle()
            dve.tensor_scalar(red[:, :], red[:, :], PI_BELOW, -PI_BELOW, ALU.min, ALU.max).then_inc(angles_made, 1)

            dve.wait_ge(params_loaded, 16 * (7 * LAYERS - 1))
            for l in range(L1):
                if l:
                    gained("n1", l, 0)
                nn = norm_mean(("mla", l), [(slice(0, 2), slice(8, 10), MLA_Q, NORM_EPS), (slice(2, 4), slice(10, 12), MLA_KV, NORM_EPS)])
                for t in range(T):
                    dve.tensor_scalar(z[:, t, 0:MLA_Q], z[:, t, 0:MLA_Q], stats[:, nn, 12 + t:13 + t], None, ALU.mult)
                    dve.tensor_scalar(z[:, t, MLA_Q:MLA_Q + MLA_KV], z[:, t, MLA_Q:MLA_Q + MLA_KV], stats[:, nn, 14 + t:15 + t], None, ALU.mult).then_inc(normed, 1)
                for t in range(T):
                    bank = small.wait_filled(dve, ("cT", l, t))[:, 0:3 * P].rearrange("p (i q) -> p i q", i=3)
                    moved(dve.tensor_tensor(cT[:, :, t * P:(t + 1) * P], bank, gqkv[:, l, :].unsqueeze(2).to_broadcast([P, 3, P]), ALU.mult), small)
                lin.wait_moved(dve, ("z", l, 3, 1))
                dve.tensor_tensor(lf[:, 0], z[:, :, FOX_F:FOX_F + HEADS], fbias[:, l, :].unsqueeze(1).to_broadcast([P, T, HEADS]), ALU.add).then_inc(fox_logits, 1)
                dve.wait_ge(nsa_tanh, l + 1)
                step(dve.tensor_scalar(gn, gn, 0.5, 0.5, ALU.mult, ALU.add))
                dve.wait_ge(fox_log, l + 1)
                step(dve.scalar_tensor_tensor(out=lf[:, 2], in0=lf[:, 0], scalar=0.0, in1=lf[:, 1], op0=ALU.min, op1=ALU.subtract))
                step.settle()
                for s, w in ((0, SEQ), (1, P)):
                    for i, h in enumerate(BY_SLOT):
                        m = dve.tensor_scalar(decay_rows[s][:, i, :], upto[:, 0:w], lf[:, 2, s, h:h + 1], -(HD ** 0.5), ALU.mult, ALU.mult)
                m.then_inc(decay_ready, 1)
                bank = small.wait_filled(dve, ("cq", l))
                moved(dve.tensor_scalar(cq8, bank[:, 0:8].rearrange("p (t h) -> p t h", t=T), HD ** 0.5, None, ALU.mult), small)
                small.wait_moved(dve, ("cq", l))
                for f in range(2):
                    bank = lin.wait_filled(dve, ("ck", l, f)).rearrange("p (h k) -> p h k", h=2)
                    for i in range(2):
                        h = BY_SLOT[2 * f + i]
                        for t in range(T):
                            nk = P * (t + 1)
                            m = dve.scalar_tensor_tensor(out=d8[t][:, 2 * f + i, :], in0=bank[:, i, 0:nk], scalar=cq8[:, t, h:h + 1],
                                                         in1=causal[:, SEQ - nk:SEQ], op0=ALU.add, op1=ALU.add)
                    moved(m, lin)
                small.wait_moved(dve, ("idx", l, 1))
                for w, s in enumerate((S_KC, S_VC)):
                    for e in range(2):
                        r = slice(HD * e, HD * (e + 1))
                        src = attT[r, s, :].rearrange("p (c i e) -> p i c e", i=8, e=2)
                        for i1 in range(2):
                            m = dve.tensor_tensor(cmpR[r, w, 8 * i1:8 * i1 + 8, :], src[:, :, i1:i1 + NCMP, e],
                                                  peT[r, l, w, 8 * i1:8 * i1 + 8].unsqueeze(2).to_broadcast([HD, 8, NCMP]), ALU.add)
                m.then_inc(cmp_rows, 1)
                bank = small.wait_filled(dve, ("comp", l))
                dve.tensor_copy(kcmpT, bank[:, 0:NCMP])
                moved(dve.tensor_copy(vcmp[0:NCMP], bank[0:NCMP, 64:64 + HD]), small)
                for t in range(T):
                    nk = P * (t + 1)
                    for f in range(4):
                        n = 8 * l + 4 * t + f
                        lin.wait_moved(dve, ("idx", l, t, f))
                        for i in range(2):
                            h = f + 4 * i
                            w = z[:, t, DSA_W + h:DSA_W + h + 1]
                            if h == 0:
                                step(dve.tensor_scalar(index_bias[t], relu_l[:, n % 2, i, 0:nk], w, None, ALU.mult))
                            else:
                                m = dve.scalar_tensor_tensor(out=index_bias[t], in0=relu_l[:, n % 2, i, 0:nk], scalar=w, in1=index_bias[t], op0=ALU.mult, op1=ALU.add)
                                if i == 0:
                                    step(m)
                                else:
                                    m.then_inc(index_used, 1)
                            if i == 0:
                                step.settle()
                        dve.wait_ge(index_used, n + 1)
                    step(dve.tensor_tensor(index_bias[t], index_bias[t], causal[:, SEQ - nk:SEQ], ALU.add))
                    step.settle()
                seen = set()
                for i, (path, t) in enumerate(PATHS1):
                    aa = att1(l, i)
                    b = aa % 2
                    nk = NCMP if path == "cmp" else P * (t + 1)
                    if path == "fox":
                        softmax_bias(aa, nk, SCALE[path], d8[t])
                    elif path == "dsa":
                        softmax_bias(aa, nk, SCALE[path], heads(index_bias[t], nk))
                    elif path == "cmp":
                        softmax_bias(aa, nk, SCALE[path], heads(cmp_bias[:, t, :], NCMP))
                    else:
                        softmax_bias(aa, nk, SCALE[path], heads(causal[:, P:SEQ], P), t * P)
                    if i in (2, 4):
                        take_top(i // 2 - 1)
                    if i == NP1 - 1:
                        weight_lo(("lift", l, 0), [0, 1])
                    dve.wait_ge(probs_made, aa + 1)
                    total, weight = softmax_s[:, b, 2, :], softmax_s[:, b, 3, :]
                    if path == "cmp":
                        dve.tensor_tensor(probs[:, b, :, 0:NCMP], probs[:, b, :, 0:NCMP], heads(cmp_keep[:, t, :], NCMP), ALU.mult).then_inc(probs_final, 1)
                        dve.wait_ge(probs_final, cmp_final(l, t))
                        step(dve.tensor_reduce(total, probs[:, b, :, 0:NCMP], AX, ALU.add))
                        step.settle()
                        step(dve.tensor_scalar(total, total, 1e-30, None, ALU.max))
                        step.settle()
                    step(dve.reciprocal(weight, total))
                    if BRANCH[path] == 1:
                        g0 = HEADS * ("cmp", "sel", "win").index(path)
                        step.settle()
                        step(dve.tensor_tensor(weight.rearrange("p (e i) -> p e i", e=2), weight.rearrange("p (e i) -> p e i", e=2),
                                               gn[:, t, g0:g0 + HEADS].rearrange("p (i e) -> p e i", e=2), ALU.mult))
                    step.settle()
                    bank = small.wait_filled(dve, ("PV", l, i))[:, 0:HEADS * HD].rearrange("p (i e d) -> p i e d", i=2, e=2)
                    dst = osb[:, t, BRANCH[path]].rearrange("p (i e) d -> p i e d", e=2)
                    wide = weight.rearrange("p (e i) -> p i e", e=2).unsqueeze(3).to_broadcast([P, 2, 2, HD])
                    if (BRANCH[path], t) in seen:
                        moved(dve.tensor_tensor(otmp.rearrange("p (i e) d -> p i e d", e=2), bank, wide, ALU.mult), small)
                        small.wait_moved(dve, ("PV", l, i))
                        step(dve.tensor_tensor(osb[:, t, BRANCH[path]], osb[:, t, BRANCH[path]], otmp, ALU.add))
                    else:
                        moved(dve.tensor_tensor(dst, bank, wide, ALU.mult), small)
                    seen.add((BRANCH[path], t))
                weight_lo(("lift", l, 0), [2, 3])
                for b in range(4):
                    rest_bank(small, ("oT", l, b), hT_lo2[:, 2 * b:2 * b + 2, :], hT_hi[:, 2 * b:2 * b + 2, :], lambda bk: bk.rearrange("p (c q) -> p c q", c=2))
                for f in range(2):
                    for b in range(4):
                        weight_lo(("lift", l, 1) if f == 0 else ("out", l, 0), [b])
                        for t in range(T):
                            gv = gate[:, t, b * D + f * BANK:b * D + (f + 1) * BANK]
                            bank = lin.wait_filled(dve, ("lift", l, f, b, t))
                            moved(dve.scalar_tensor_tensor(out=gv, in0=gv, scalar=1.0, in1=bank, op0=ALU.add, op1=ALU.mult), lin)
                rest_turned("mixT", l, hT_lo2)
                weight_lo(("out", l, 1))
                rms_sum("out", ("n2", l), l)
                for t in range(T):
                    q = slice(t * P, (t + 1) * P)
                    for f in range(2):
                        bank = four(small.wait_filled(dve, ("n2", l, t, f)))
                        if t:
                            dve.wait_ge(split, split_at[("n2", l, t - 1, f)])
                        dve.tensor_tensor(four(gainedT[:, f, :]), bank, g1[:, 1, l, 4 * f:4 * f + 4].unsqueeze(2).to_broadcast([P, 4, P]), ALU.mult).then_inc(made, 1)
                        dve.wait_ge(made, made_at[("n2", l, t, f)])
                        dve.sem_inc(small.moved["dve"], 1)
                    for f in range(2):
                        rest_part(("n2", l, t, f), hT_lo[:, 4 * f:4 * f + 4, q], four(gainedT[:, f, :]), hT_hi[:, 4 * f:4 * f + 4, q])
                n_up = D_FF // BANK
                for j in range(n_up + 1):
                    if j:
                        for b in range(2):
                            key = ("up", l, j - 1, b)
                            bank = lin.wait_filled(dve, key)
                            dve.wait_ge(relued, 2 * (n_up * l + j - 1) + b + 1)
                            dve.tensor_tensor(up_sq[:, b, :], up_sq[:, b, :], bank, ALU.mult).then_inc(made, 1)
                            dve.wait_ge(made, made_at[key])
                            dve.sem_inc(lin.moved["dve"], 1)
                        for b in range(2):
                            c = 4 * (j - 1) + 2 * b
                            rest_part(("up", l, j - 1, b), up_lo[:, c:c + 2, :], up_sq[:, b, :].rearrange("p (c q) -> p c q", c=2), up_hi[:, c:c + 2, :])
                    if j == n_up and l == L1 - 1:
                        for t in range(T):
                            for f in range(2):
                                rest_bank(small, ("memT", t, f), mem_lo[:, t, 4 * f:4 * f + 4, :], mem_hi[:, t, 4 * f:4 * f + 4, :])
                    weight_lo(("up", l, j + 1) if j + 1 < n_up else ("down", l, j + 1 - n_up))
                for j in range(2, n_up):
                    weight_lo(("down", l, j))
                rms_sum("down", ("n1", l + 1) if l + 1 < L1 else None, l)

            def row_stats(t, f):
                step(dve.bn_stats(halves[:, t, f, :], x[:, t, f * BANK:(f + 1) * BANK]))

            def norm_rows(key, t):
                nn = norm_at[key]
                step.settle()
                step(dve.bn_aggr(stats[:, nn, 2 * t:2 * t + 2], halves[:, t, :, :]))
                step.settle()
                dve.tensor_scalar(stats[:, nn, 8 + t:9 + t], stats[:, nn, 2 * t + 1:2 * t + 2], LN_EPS, None, ALU.add).then_inc(mean_ready, 1)
                b = gains.index(key) % 2
                dve.wait_ge(lng_loaded[b], gains_due[key])
                step(dve.scalar_tensor_tensor(out=x[:, t, :], in0=x[:, t, :], scalar=stats[:, nn, 2 * t:2 * t + 1], in1=lng[:, b, 0, :], op0=ALU.subtract, op1=ALU.mult))
                step.settle()
                dve.wait_ge(rstd_ready, root_at[key, t])
                step(dve.scalar_tensor_tensor(out=x[:, t, :], in0=x[:, t, :], scalar=stats[:, nn, 12 + t:13 + t], in1=lng[:, b, 1, :], op0=ALU.mult, op1=ALU.add))
                step.settle()
                dve.sem_inc(x_updated, 1)

            for t in range(T):
                root = rms_root("final", t)
                dve.wait_ge(lng_loaded[0], gains_due["final"])
                step(dve.scalar_tensor_tensor(out=x[:, t, :], in0=x[:, t, :], scalar=root, in1=lng[:, 0, 0, :], op0=ALU.mult, op1=ALU.mult))
                step.settle()
                dve.sem_inc(x_updated, 1)
                for f in range(2):
                    row_stats(t, f)
                norm_rows("ln0", t)

            def residual_norm(name, key, l):
                for t in range(T):
                    for f in range(2):
                        bank = lin.wait_filled(dve, (name, l, t, f))
                        xv_ = x[:, t, f * BANK:(f + 1) * BANK]
                        moved(dve.scalar_tensor_tensor(out=xv_, in0=xv_, scalar=ALPHA, in1=bank, op0=ALU.mult, op1=ALU.add), lin)
                        lin.wait_moved(dve, (name, l, t, f))
                        row_stats(t, f)
                    norm_rows((key, l), t)

            def conv_taps(l, taps):
                for j in taps:
                    for c in range(CT):
                        src, w = uT[:, c, j:j + SEQ], conv_wT[:, l, c, j:j + 1]
                        if j == 0:
                            step(dve.tensor_scalar(acc[:, c, :], src, w, conv_p[:, 0, l, c:c + 1], ALU.mult, ALU.add))
                        else:
                            step.settle(CT - 1)
                            step(dve.scalar_tensor_tensor(out=acc[:, c, :], in0=src, scalar=w, in1=acc[:, c, :], op0=ALU.mult, op1=ALU.add))

            dve.wait_ge(params2_loaded, 16 * (CT + 6) * LAYERS)
            for l in range(L2):
                rest_turned("hT", l, hT_lo)
                weight_lo(("ca", l))
                weight_lo(("qk", l))
                for t in range(T):
                    lin.wait_moved(dve, ("cg", l, t))
                    bank = lin.wait_filled(dve, ("ca", l, t))
                    moved(dve.scalar_tensor_tensor(out=u2[:, t, :], in0=sg2[:, t, :], scalar=1.0, in1=bank, op0=ALU.add, op1=ALU.mult), lin)
                for t in range(T):
                    bank = small.wait_filled(dve, ("zlow", l, t))
                    moved(dve.tensor_copy(la[:, 0, t, :], bank[:, 0:GK]), small)
                small.wait_moved(dve, ("uT", l, 1))
                for i in range(4):
                    weight_lo(("v", l), [i])
                    conv_taps(l, [i])
                for t in range(T):
                    dve.wait_ge(low_log, T * l + t + 1)
                    dve.scalar_tensor_tensor(out=la[:, 0, t, :], in0=la[:, 0, t, :], scalar=0.0, in1=la[:, 1, t, :], op0=ALU.min, op1=ALU.subtract).then_inc(la_ready, 1)
                for i in range(4):
                    weight_lo(("r", l), [i])
                    conv_taps(l, [4 + i])
                for t in range(T):
                    lin.wait_moved(dve, ("bc", l, t))
                    dve.scalar_tensor_tensor(out=ex2[:, 0, t, :], in0=qk2[:, t, 0:GK], scalar=HD ** -0.5, in1=ex2[:, 0, t, :], op0=ALU.mult, op1=ALU.mult)
                    dve.tensor_tensor(ex2[:, 1, t, :], qk2[:, t, GK:], ex2[:, 1, t, :], ALU.mult)
                    dve.tensor_tensor(ex2[:, 2, t, :], qk2[:, t, GK:], ex2[:, 2, t, :], ALU.mult).then_inc(qkd_ready, 1)
                for i in range(4):
                    weight_lo(("xk", l, 0), [i])
                    conv_taps(l, [8 + i])
                for t in range(T):
                    dve.wait_ge(r_tanh, T * l + t + 1)
                    bank = lin.wait_filled(dve, ("r", l, t))
                    moved(dve.scalar_tensor_tensor(out=sr2[:, t, :], in0=sr2[:, t, :], scalar=1.0, in1=bank, op0=ALU.add, op1=ALU.mult), lin)
                dve.wait_ge(pads_zeroed, l + 1)
                for t in range(T):
                    for e in range(2):
                        bank = lin.wait_filled(dve, ("att", l, t, e))[:, 0:2 * P].rearrange("p (g c) -> p g c", g=2)
                        moved(dve.copy_predicated(gattT[:, t, :, :].rearrange("p (g e) c -> p g e c", e=2)[:, :, e, :],
                                                  blk_upto[:, :].unsqueeze(1).to_broadcast([P, 2, P]).bitcast(I32), bank), lin)
                small.wait_moved(dve, ("blast", l))
                for c in range(3):
                    bank = lin.wait_filled(dve, ("upd", l, c)).rearrange("p (g e n) -> p g e n", g=2, e=2)
                    for e in range(2):
                        r = slice(HD * e, HD * (e + 1))
                        if c == 0:
                            m = dve.tensor_copy(state[r, c, :, :], bank[r, :, e, :])
                        else:
                            for g in range(2):
                                m = dve.scalar_tensor_tensor(out=state[r, c, g, :], in0=state[r, c - 1, g, :], scalar=dec[r, g, c:c + 1], in1=bank[r, g, e, :], op0=ALU.mult, op1=ALU.add)
                    moved(m, lin)
                    lin.wait_moved(dve, ("upd", l, c))
                conv_taps(l, range(12, TAPS))
                step.settle()
                dve.sem_inc(conv_summed, 1)
                for t in range(T):
                    for e in range(2):
                        bank = lin.wait_filled(dve, ("go", l, t, e))[:, 0:2 * P].rearrange("p (g n) -> p g n", g=2)
                        moved(dve.tensor_copy(go2[:, t, :].rearrange("p (g e n) -> p g e n", g=2, e=2)[:, :, e, :], bank), lin)

                def channels(v):
                    return v.unsqueeze(1).to_broadcast([P, CT, SEQ])

                bank = small.wait_filled(dve, ("cmean", l))
                moved(dve.tensor_scalar(mean_c, bank[:, 0:SEQ], 1.0 / CONV, None, ALU.mult), small)
                small.wait_moved(dve, ("cmean", l))
                dve.tensor_tensor(acc[:, :, :], acc[:, :, :], channels(mean_c), ALU.subtract).then_inc(conv_centred, 1)
                nn = norm_mean(("gla", l), [(slice(0, 8), slice(0, 8), P, LN_EPS)])
                for t in range(T):
                    v = four(go2[:, t, :])
                    step(dve.tensor_tensor(v, v, stats[:, nn, 8 + 4 * t:12 + 4 * t].unsqueeze(2).to_broadcast([P, HEADS, P]), ALU.mult))
                    step.settle()
                    step(dve.tensor_tensor(v, v, heads(gla_g[:, l, :], P), ALU.mult))
                    step.settle()
                    dve.scalar_tensor_tensor(out=go2[:, t, :], in0=go2[:, t, :], scalar=0.5, in1=sr2[:, t, :], op0=ALU.mult, op1=ALU.mult).then_inc(go_ready, 1)
                for t in range(T):
                    rest_bank(small, ("goT", l, t), hT_lo2[:, 4:8, t * P:(t + 1) * P], hT_hi[:, 4:8, t * P:(t + 1) * P])
                bank = small.wait_filled(dve, ("cvar", l))
                nn = norm_at[("conv", l)]
                moved(dve.tensor_scalar(stats[:, nn, 8:10], bank[:, 0:2], 1.0 / CONV, LN_EPS, ALU.mult, ALU.add), small)
                small.wait_moved(dve, ("cvar", l))
                dve.sem_inc(mean_ready, 1)
                dve.wait_ge(rstd_ready, root_at[("conv", l), 0])
                for t in range(T):
                    m = dve.tensor_scalar(root_diag[:, t, :], ident[:, :], stats[:, nn, 12 + t:13 + t], None, ALU.mult)
                m.then_inc(root_spread, 1)
                bank = small.wait_filled(dve, ("crstd", l))
                dve.wait_ge(conv_squared, l + 1)
                moved(dve.tensor_tensor(acc[:, :, :], acc[:, :, :], channels(bank[:, 0:SEQ]), ALU.mult), small)
                small.wait_moved(dve, ("crstd", l))
                for c in range(CT):
                    m = dve.tensor_scalar(acc[:, c, :], acc[:, c, :], conv_p[:, 1, l, c:c + 1], conv_p[:, 2, l, c:c + 1], ALU.mult, ALU.add)
                m.then_inc(conv_affine, 1)
                dve.wait_ge(conv_tanh, l + 1)
                step(dve.tensor_scalar(sq2[:, :, :], sq2[:, :, :], 0.5, 0.5, ALU.mult, ALU.add))
                step.settle()
                dve.tensor_tensor(acc[:, :, :], acc[:, :, :], sq2[:, :, :], ALU.mult).then_inc(conv_out, 1)
                rest_part(("conv", l), hT_lo2[:, 0:CT, :], acc[:, :, :], hT_hi[:, 0:CT, :])
                residual_norm("mix", "ln1", l)
                rest_turned("h1T", l, hT_lo2)
                weight_lo(("xq", l, 1))
                weight_lo(("xo", l, 0))
                for t in range(T):
                    softmax_bias(att2(l, t), SEQ, XD ** -0.5)
                for t in range(T):
                    aa = att2(l, t)
                    b = aa % 2
                    dve.wait_ge(probs_made, aa + 1)
                    step(dve.reciprocal(softmax_s[:, b, 3, :], softmax_s[:, b, 2, :]))
                    step.settle()
                    dve.tensor_tensor(probs[:, b], probs[:, b], softmax_s[:, b, 3, :].unsqueeze(2).to_broadcast([P, XH, SEQ]), ALU.mult).then_inc(probs_final, 1)
                for t in range(T):
                    for f in range(2):
                        k, q = slice(4 * f, 4 * f + 4), slice(t * P, (t + 1) * P)
                        rest_bank(lin, ("xO", l, t, f), hT_lo2[:, k, q], hT_hi[:, k, q])
                weight_lo(("xo", l, 1))
                residual_norm("xo", "ln2", l)
                rest_turned("h2T", l, hT_lo)
                n_ffn, n_ffo = FT2 // 2, -(-FT2 // 4)
                for j in range(n_ffn + 1):
                    if j:
                        for f in (2 * j - 2, 2 * j - 1):
                            dve.wait_ge(ff_tanh, FT2 * l + f + 1)
                            bank = lin.wait_filled(dve, ("ffn", l, f))
                            step(dve.scalar_tensor_tensor(out=ffs[:, f % 2, :], in0=ffs[:, f % 2, :], scalar=1.0, in1=bank[:, 0:SEQ], op0=ALU.add, op1=ALU.mult))
                            step.settle()
                            if f >= 2:
                                dve.wait_ge(split, split_at[("ffn", l, f - 2)])
                            moved(dve.scalar_tensor_tensor(out=ffp[:, f % 2, :], in0=ffs[:, f % 2, :], scalar=0.5, in1=bank[:, SEQ:], op0=ALU.mult, op1=ALU.mult), lin)
                        for f in (2 * j - 2, 2 * j - 1):
                            rest_part(("ffn", l, f), ff_lo[:, f, :], ffp[:, f % 2, :], ff_hi[:, f, :])
                    weight_lo(("ffn", l, j + 1) if j + 1 < n_ffn else ("ffo", l, j + 1 - n_ffn))
                for j in range(2, n_ffo):
                    weight_lo(("ffo", l, j))
                residual_norm("ffo", "ln3", l)

        @block.gpsimd
        def _(pool):
            step = Chain(pool, pool_step)

            def select(v, keep, fill, base, per_row, per_column):
                step.settle()
                step(pool.affine_select(out=v, in_=v, pattern=[[per_column, v.shape[-1]]], compare_op=keep, fill=fill, base=base, channel_multiplier=per_row))

            def weight_rest(key):
                q0, n = first_piece[key]
                raw = slot_of(place[key]).rearrange("p (i n) -> p i n", n=PIECE)
                for i in range(n):
                    q = q0 + i
                    pool.wait_ge(hi_ready, q + 1)
                    pool.tensor_tensor(w_lo[:, q % PIECES, :], raw[:, i, :], w_hi[:, q % PIECES, :], ALU.subtract).then_inc(lo_ready["pool"], 1)

            def root_rows(key):
                for t in range(T):
                    root(key, slice(8 + t, 9 + t), slice(12 + t, 13 + t), t)

            def root(key, src=slice(8, 10), dst=slice(12, 14), t=0):
                nn = norm_at[key]
                pool.wait_ge(mean_ready, root_at[key, t])
                n = src.stop - src.start
                pool.tensor_tensor(stats[:, nn, dst], stats[:, nn, src], minus_half[:, 0:1].to_broadcast([P, n]), ALU.pow).then_inc(rstd_ready, 1)

            def rotate(v, kind):
                first, half = kind
                n = v.shape[2]
                shape = [P, T, n, half]
                sin = rope[:, 0, :, first:first + half].unsqueeze(2).to_broadcast(shape)
                cos = rope[:, 1, :, first:first + half].unsqueeze(2).to_broadcast(shape)
                tmp = [rope_tmp[:, s, 0:T * n * half].rearrange("p (t h d) -> p t h d", t=T, h=n) for s in range(4)]
                x1, x2 = v[:, :, :, 0:half], v[:, :, :, half:2 * half]
                for dst, src, table in zip(tmp, (x1, x2, x2, x1), (cos, sin, cos, sin)):
                    step(pool.tensor_tensor(dst, src, table, ALU.mult))
                step.settle()
                step(pool.tensor_tensor(x1, tmp[0], tmp[1], ALU.subtract))
                step(pool.tensor_tensor(x2, tmp[2], tmp[3], ALU.add))
                step.settle()

            def by_head(c0, n, d):
                return z[:, :, c0:c0 + n * d].rearrange("p t (h d) -> p t h d", d=d)

            MLA_ROPE, HEAD_ROPE, IDX_ROPE = ROPES
            step(pool.memset(minus_half[:, :], -0.5))
            step(pool.memset(ident[:, :], 0.0))
            select(ident[:, :], ALU.not_equal, 1.0, 0, 1, -1)
            step.settle()
            pool.sem_inc(ident_made, 1)
            root_rows(("n1", 0))
            for v, value in ((causal[:, :], 0.0), (upto[:, :], 1.0), (cmp_bias[:, :, :], 0.0), (cmp_keep[:, :, :], 1.0),
                             (blk_upto[:, :], 1.0), (blk_after[:, :], 1.0), (blk_sum[:, :], 1.0)):
                step(pool.memset(v, value))
            for first, half in ROPES:
                for i in range(half):
                    step(pool.memset(freq[:, first + i:first + i + 1], float(np.float32(THETA) ** (-np.float32(i) / np.float32(half)))))
            select(causal[:, P:SEQ], ALU.is_ge, MASKED, 0, 1, -1)
            select(upto[:, 0:P], ALU.is_ge, 0.0, 0, -1, 1)
            for t in range(T):
                select(cmp_bias[:, t, :], ALU.is_ge, MASKED, P * t - (CMP_LEN - 1), 1, -CMP_STRIDE)
                select(cmp_keep[:, t, :], ALU.is_ge, 0.0, P * t - (CMP_LEN - 1), 1, -CMP_STRIDE)
            select(blk_upto[:, :], ALU.is_ge, 0.0, 0, -1, 1)
            select(blk_upto[:, CHUNK:], ALU.is_ge, 0.0, -CHUNK, 1, 0)
            select(blk_after[:, :], ALU.is_ge, 0.0, -1, 1, -1)
            select(blk_after[:, 0:CHUNK], ALU.is_ge, 0.0, CHUNK - 1, -1, 0)
            select(blk_sum[:, 0:1], ALU.is_ge, 0.0, CHUNK - 1, -1, 0)
            select(blk_sum[:, 1:2], ALU.is_ge, 0.0, -CHUNK, 1, 0)
            step.settle()
            pool.sem_inc(consts_made, 1)

            for l in range(L1):
                if l:
                    root_rows(("n1", l))
                root(("mla", l), slice(8, 12), slice(12, 16))
                if l == 0:
                    pool.wait_ge(rope_tables, 1)
                lin.wait_moved(pool, ("z", l, 2, 1))
                rotate(by_head(MLA_Q + MLA_KV, 1, MLA_R), MLA_ROPE)
                rotate(by_head(NSA_Q, 4, HD), HEAD_ROPE)
                rotate(by_head(NSA_KC, 3, 2 * HD), HEAD_ROPE)
                for t in range(T):
                    step(pool.tensor_copy(stage[:, t, 0:2, :].rearrange("p w (r d) -> p w r d", r=2),
                                          z[:, t, NSA_KS:NSA_KS + 4 * HD].rearrange("p (w d) -> p w d", w=2)[:, :, 0:HD].unsqueeze(2).to_broadcast([P, 2, 2, HD])))
                    step(pool.tensor_copy(stage[:, t, 4:6, :].rearrange("p w (r d) -> p w r d", r=2),
                                          z[:, t, NSA_KC:NSA_KC + 2 * HD].rearrange("p (w d) -> p w d", w=2).unsqueeze(2).to_broadcast([P, 2, 2, HD])))
                lin.wait_moved(pool, ("ukv", l, 1))
                rotate(mqk[:, :, 0:HEADS, HD:MLA_HD], MLA_ROPE)
                for t in range(T):
                    m = pool.tensor_copy(mqk[:, t, HEADS:2 * HEADS, HD:MLA_HD], z[:, t, MLA_Q + MLA_KV:NSA0].unsqueeze(1).to_broadcast([P, HEADS, MLA_R]))
                    if t == 0:
                        step(m)
                m.then_inc(mla_roped, 1)
                lin.wait_moved(pool, ("z", l, 4, 1))
                rotate(by_head(DSA_Q, 5, HD), HEAD_ROPE)
                rotate(by_head(DSA_QI, IDX_HEADS + 1, IDX_DIM), IDX_ROPE)
                for t in range(T):
                    step(pool.tensor_copy(stage[:, t, 2, :].rearrange("p (r d) -> p r d", r=2), z[:, t, DSA_K:DSA_K + HD].unsqueeze(1).to_broadcast([P, 2, HD])))
                    step(pool.tensor_copy(stage[:, t, 3, :].rearrange("p (r d) -> p r d", r=4), z[:, t, DSA_KI:DSA_KI + IDX_DIM].unsqueeze(1).to_broadcast([P, 4, IDX_DIM])))
                step.settle()
                pool.sem_inc(staged, 1)
                for f in range(2):
                    for b in range(1, 4):
                        for t in range(T):
                            lin.wait_moved(pool, ("lift", l, f, b, t))
                            part = [gate[:, t, i * D + f * BANK:i * D + (f + 1) * BANK] for i in (0, b)]
                            if b > 1:
                                step.settle(0 if (b, t) == (3, 1) else 1)
                            m = pool.tensor_tensor(part[0], part[0], part[1], ALU.add)
                            if b < 3:
                                step(m)
                            else:
                                m.then_inc(gated, 1)
                root_rows(("n2", l))
                weight_rest(("up", l, 0))

            def load_gains(n):
                key = gains[n]
                if key == "final":
                    srcs = [a["final_g"]]
                elif key == "ln0":
                    srcs = [a["ln0_g_2"], a["ln0_b_2"]]
                else:
                    srcs = [a[key[0] + "_g_2"][key[1]], a[key[0] + "_b_2"][key[1]]]
                for w, src in enumerate(srcs):
                    pool.dma_start(lng[:, n % 2, w, :], src.partition_broadcast(P)).then_inc(lng_loaded[n % 2], 16)

            def after(key):
                n = gains.index(key)
                if n + 2 < len(gains):
                    pool.wait_ge(x_updated, update_at[key, 1])
                    load_gains(n + 2)

            pool.wait_ge(small.filled, small.at[("n2", L1 - 1, 1, 1)] + 1)
            pool.dma_start(hn[:, :, :], a["mem_2"][0].rearrange("(t p) n -> p t n", p=P)).then_inc(mem_loaded, 16)
            load_gains(0)
            load_gains(1)
            for t in range(T):
                for key in ("final", "ln0"):
                    root(key, slice(8 + t, 9 + t), slice(12 + t, 13 + t), t)
            after("final")
            after("ln0")
            for l in range(L2):
                if l == 0:
                    step(pool.memset(qez, 0.0))
                    step(pool.memset(gattT, 0.0))
                    step(pool.memset(uT[:, :, 0:PAD], 0.0))
                step(pool.memset(alT, 1.0))
                step.settle()
                pool.sem_inc(pads_zeroed, 1)
                weight_rest(("cg", l))
                for key in (("xk", l, 1), ("xv", l, 0), ("xv", l, 1)):
                    weight_rest(key)
                root(("gla", l), slice(0, 8), slice(8, 16))
                weight_rest(("mix", l, 0))
                root(("conv", l))
                weight_rest(("mix", l, 1))
                for w, first in (("ln1", ("xq", l, 0)), ("ln2", ("ffn", l, 0)), ("ln3", None)):
                    root_rows((w, l))
                    if first:
                        weight_rest(first)
                    after((w, l))


_OUTS = [((1, SEQ, D), "float32")]
_INS = ["x", "positions", "norm1_g", "w_in", "mla_q_norm_g", "mla_w_uq", "mla_kv_norm_g", "mla_w_ukv", "nsa_cmp_pe", "nsa_cmp_w",
        "fox_f_bias", "w_branch", "w_out", "norm2_g", "w_up", "w_down", "final_g", "mem_2", "ln0_g_2", "ln0_b_2", "w_in_2", "w_a2_2",
        "b_a_2", "conv_w_2", "conv_b_2", "conv_ln_g_2", "conv_ln_b_2", "gla_norm_g_2", "w_mix_out_2", "ln1_g_2", "ln1_b_2", "w_xq_2",
        "w_xkv_2", "w_xo_2", "ln2_g_2", "ln2_b_2", "w_ffn_in_2", "w_ffn_out_2", "ln3_g_2", "ln3_b_2"]


def kernel(**inputs):
    from concourse import bacc
    from concourse.bass_utils import run_bass_kernel_spmd

    nc = bacc.Bacc("TRN2", target_bir_lowering=False, num_devices=1)
    arrays, aps = {}, {}
    for name in _INS:
        arr = np.ascontiguousarray(inputs[name])
        arrays[f"in_{name}"] = arr
        aps[name] = nc.dram_tensor(f"in_{name}", arr.shape, mybir.dt.from_np(arr.dtype), kind="ExternalInput").ap()
    out = nc.dram_tensor("out", _OUTS[0][0], F32, kind="ExternalOutput").ap()
    two_decoders(nc, aps, out)
    r = run_bass_kernel_spmd(nc, [arrays], core_ids=[0])
    return r.results[0]["out"]
```

```python
from contextlib import ExitStack

import numpy as np

import concourse.bass as bass
from concourse import mybir

F32 = mybir.dt.float32
I32 = mybir.dt.int32
F32R = mybir.dt.float32r
ALU = mybir.AluOpType
ACT = mybir.ActivationFunctionType
AX = mybir.AxisListType.X

P = 128
SEQ = 256
T = SEQ // P
D = 1024
KT = D // P
HEADS = 4
HD = 64
MASKED = -1e30
TAKEN = -3e38
BANK = 512

MLA_Q, MLA_KV, MLA_R = 256, 128, 32
MLA_HD = HD + MLA_R
MLA0 = 0
NSA0 = MLA_Q + MLA_KV + MLA_R
FOX0 = NSA0 + 4 * HD + 6 * HD + 12
DSA0 = FOX0 + 3 * HEADS * HD + HEADS
GATE0 = DSA0 + 4 * HD + 2 * HD + 8 * 32 + 32 + 8
NSA_Q, NSA_KC, NSA_VC, NSA_KS, NSA_VS, NSA_KW, NSA_VW, NSA_G = [NSA0 + c for c in (0, 256, 320, 384, 448, 512, 576, 640)]
FOX_Q, FOX_K, FOX_V, FOX_F = [FOX0 + c for c in (0, 256, 512, 768)]
DSA_Q, DSA_K, DSA_V, DSA_QI, DSA_KI, DSA_W = [DSA0 + c for c in (0, 256, 320, 384, 640, 672)]
IDX_HEADS, IDX_DIM, KEEP = 8, 32, 64
CMP_LEN, CMP_STRIDE = 32, 16
NCMP = (SEQ - CMP_LEN) // CMP_STRIDE + 1
CMP_PAIRS = CMP_LEN // 2
D_FF = 4096
ROPES = ((0, 16), (16, 8), (24, 4))
NFREQ = 28
THETA = 500000.0
NORM_EPS = 1e-6

CONV = 512
TAPS = 31
PAD = TAPS - 1
CT = CONV // P
GK, GV = 256, 512
RANK = 16
CHUNK = 64
DFF2 = 2816
FT2 = DFF2 // P
XH, XD = 4, 256
IN2 = 2 * CONV + 2 * GK + 2 * GV + RANK
ALPHA = 4 ** 0.25
LN_EPS = 1e-5
SLOTS = 2
PIECES = 4
PIECE = KT * BANK // 4
ARENA = 27700
ROUND = 1.5 * 2 ** 23
TWO_PI = (6.28125, 0.0019350051879882812, 3.019915981956752e-07)
PI_BELOW = 3.1415925

S_NSA_Q, S_KS, S_KW, S_DSA_Q, S_DSA_K, S_KI, S_QI, S_KC, S_VC, S_FOX_Q, S_FOX_K, S_MLA_Q, S_MLA_K = 0, 2, 3, 4, 6, 7, 8, 10, 11, 12, 14, 16, 20
N_ATT_T = 24
BY_SLOT = (0, 2, 1, 3)


def turn_order(name):
    return [(t, f) for f in range(2) for t in range(T)] if name == "mixT" else [(t, f) for t in range(T) for f in range(2)]


def cmp_final(l, t):
    return T * l + t + 1


class Turns:

    def __init__(self, banks, plan, filled, moved):
        self.banks, self.plan, self.filled, self.moved = banks, plan, filled, moved
        self.at = {key: u for u, (key, _) in enumerate(plan)}
        self.count, seen = [], {}
        for _, engine in plan:
            seen[engine] = seen.get(engine, 0) + 1
            self.count.append(seen[engine])
        assert len(self.at) == len(plan)

    def bank(self, key):
        return self.banks[self.at[key] % len(self.banks)]

    def open(self, pe, key):
        u = self.at[key] - len(self.banks)
        if u >= 0:
            pe.wait_ge(self.moved[self.plan[u][1]], self.count[u])
        return self.bank(key)

    def wait_filled(self, eng, key):
        eng.wait_ge(self.filled, self.at[key] + 1)
        return self.bank(key)

    def wait_moved(self, eng, key):
        u = self.at[key]
        eng.wait_ge(self.moved[self.plan[u][1]], self.count[u])


class Chain:

    def __init__(self, eng, sem):
        self.eng, self.sem, self.n = eng, sem, 0

    def __call__(self, ins):
        self.n += 1
        ins.then_inc(self.sem, 1)

    def settle(self, but=0):
        if self.n > but:
            self.eng.wait_ge(self.sem, self.n - but)


PATHS1 = [("fox", 0), ("fox", 1), ("win", 0), ("win", 1), ("mla", 0), ("mla", 1), ("sel", 0), ("sel", 1),
          ("cmp", 0), ("cmp", 1), ("dsa", 0), ("dsa", 1)]
BRANCH = {"mla": 0, "sel": 1, "win": 1, "cmp": 1, "fox": 2, "dsa": 3}
SCALE = {"mla": MLA_HD ** -0.5, "sel": HD ** -0.5, "win": HD ** -0.5, "cmp": HD ** -0.5, "fox": HD ** -0.5, "dsa": HD ** -0.5}
GATE_TILES = 4 * D // BANK
FILL = [3, 3, 2, 2, 2, 2, 2, 2, 2, 2, 3, 3]
assert sum(FILL) == 4 * (GATE_TILES - 1)
Z_TILES = [(j * BANK, min(BANK, GATE0 - j * BANK)) for j in range(-(-GATE0 // BANK))]


def plans(L1, L2):
    lin, small = [], []
    for l in range(L1):
        small += [(("n1", l, t, f), "dve") for t in range(T) for f in range(2)]
        lin += [(("z", l, j, t), "act") for j in range(3) for t in range(T)]
        small += [(("cT", l, t), "dve") for t in range(T)]
        lin += [(("z", l, 3, t), "act") for t in range(T)]
        lin += [((w, l, t), "act") for t in range(T) for w in ("uq", "ukv")]
        lin += [(("z", l, 4, t), "act") for t in range(T)]
        small += [(("cq", l), "dve")]
        lin += [(("ck", l, f), "dve") for f in range(2)]
        small += [((w, l, t), "act") for w in ("foxT", "nsa", "idx") for t in range(T)]
        lin += [(("gate", l, 0, t), "act") for t in range(T)]
        small += [(("comp", l), "dve")]
        small += [((w, l, t), "act") for w in ("mq", "mk", "dsa") for t in range(T)]
        lin += [(("idx", l, t, f), "act") for t in range(T) for f in range(4)]
        lin += [(("gate", l, j, t), "act") for j in range(1, GATE_TILES) for t in range(T)]
        for i, (path, t) in enumerate(PATHS1):
            small += [(("PT", l, i, kb), "act") for kb in range(1 if path == "cmp" else t + 1)]
            small += [(("PV", l, i), "dve")]
        small += [(("oT", l, b), "dve") for b in range(4)]
        lin += [(("lift", l, f, b, t), "dve") for f in range(2) for b in range(4) for t in range(T)]
        small += [(("mixT", l, t, f), "dve") for t, f in turn_order("mixT")]
        lin += [(("out", l, t, f), "dve") for t in range(T) for f in range(2)]
        small += [(("n2", l, t, f), "dve") for t in range(T) for f in range(2)]
        lin += [(("up", l, j, b), "dve") for j in range(D_FF // BANK) for b in range(2)]
        if l == L1 - 1:
            small += [(("memT", t, f), "dve") for t in range(T) for f in range(2)]
        lin += [(("down", l, t, f), "dve") for t in range(T) for f in range(2)]
    for l in range(L2):
        lin += [(("xk", l, b), "act") for b in range(2)]
        small += [(("hT", l, t, f), "dve") for t in range(T) for f in range(2)]
        small += [(("alow", l), "act")]
        lin += [(("cg", l, t), "act") for t in range(T)]
        lin += [(("ca", l, t), "dve") for t in range(T)]
        small += [(("uT", l, t), "act") for t in range(T)]
        small += [(("zlow", l, t), "dve") for t in range(T)]
        lin += [(("qk", l, t), "act") for t in range(T)]
        lin += [(("v", l, t), "act") for t in range(T)]
        lin += [(("bc", l, t), "act") for t in range(T)]
        small += [(("blast", l), "act")]
        lin += [(("r", l, t), "dve") for t in range(T)]
        small += [(("qeT", l, t), "act") for t in range(T)]
        lin += [(("att", l, t, e), "dve") for t in range(T) for e in range(2)]
        lin += [(("upd", l, c), "dve") for c in range(3)]
        lin += [(("xk", l, b), "act") for b in (2, 3)]
        lin += [(("xv", l, 0, t), "act") for t in range(T)]
        lin += [(("go", l, t, e), "dve") for t in range(T) for e in range(2)]
        small += [(("cmean", l), "dve")]
        lin += [(("xv", l, 1, t), "act") for t in range(T)]
        small += [(("cvar", l), "dve")] + [(("goT", l, t), "dve") for t in range(T)] + [(("crstd", l), "dve")]
        lin += [(("mix", l, t, f), "dve") for t in range(T) for f in range(2)]
        small += [(("h1T", l, t, f), "dve") for t in range(T) for f in range(2)]
        lin += [(("xq", l, b), "act") for b in range(4)]
        for t in range(T):
            small += [(("xPT", l, t, m), "act") for m in range(2)]
            lin += [(("xO", l, t, f), "dve") for f in range(2)]
        lin += [(("xo", l, t, f), "dve") for t in range(T) for f in range(2)]
        small += [(("h2T", l, t, f), "dve") for t in range(T) for f in range(2)]
        lin += [(("ffn", l, f), "dve") for f in range(FT2)]
        lin += [(("ffo", l, t, f), "dve") for t in range(T) for f in range(2)]
    return lin, small


def two_decoders(nc, a, out, L1=2, L2=2):
    ctx = ExitStack()
    with ctx:
        def sb(name, shape, dt=F32):
            return ctx.enter_context(nc.sbuf_tensor(name, shape, dt))

        def sem(name):
            return ctx.enter_context(nc.semaphore(name))

        LAYERS = a["w_in"].shape[0]
        RING_AT = 0
        W_HI_AT = RING_AT + SLOTS * KT * BANK
        W_LO_AT = W_HI_AT + PIECES * PIECE
        HT_AT = W_LO_AT + PIECES * PIECE
        HN_AT = HT_AT + KT * SEQ
        ARENA_AT = HN_AT + T * D
        base = -(-nc.sbuf_base // 32) * 32
        sb("slab", [P, ARENA_AT + ARENA])

        def placed(name, shape, at, dt=F32R):
            return nc.alloc_sbuf_tensor_at(name, [P] + shape, dt, offset=base + 4 * at)

        ring = placed("ring", [SLOTS, KT * BANK], RING_AT, F32)
        w_hi = placed("w_hi", [PIECES, PIECE], W_HI_AT)
        w_lo = placed("w_lo", [PIECES, PIECE], W_LO_AT)
        hn = placed("hn", [T, D], HN_AT, F32)
        hT_hi = placed("hT_hi", [KT, SEQ], HT_AT)
        hT_lo = placed("hT_lo", [KT, SEQ], ARENA_AT + 6144)
        hT_lo2 = placed("hT_lo2", [KT, SEQ], ARENA_AT + 19376)
        hT_lo3 = placed("hT_lo3", [KT, SEQ], ARENA_AT + 8192)
        mem_hi = placed("mem_hi", [T, KT, P], ARENA_AT + 4096)
        mem_lo = placed("mem_lo", [T, KT, P], HN_AT)
        hn_lo = placed("hn_lo", [T, KT, P], HN_AT)
        up_hi = placed("up_hi", [D_FF // P, SEQ], ARENA_AT + 8192)
        up_lo = placed("up_lo", [D_FF // P, SEQ], ARENA_AT + 8192 + 2 * D_FF)
        FF_AT = T * GATE0 + T * 4 * D
        ff_hi = placed("ff_hi", [FT2, SEQ], ARENA_AT + FF_AT)
        ff_lo = placed("ff_lo", [FT2, SEQ], ARENA_AT + FF_AT + FT2 * SEQ)
        x = sb("x", [P, T, D])
        ident = sb("ident", [P, P])
        causal = sb("causal", [P, SEQ])
        upto = sb("upto", [P, SEQ])
        ones = upto[:, P:SEQ]
        cmp_bias = sb("cmp_bias", [P, T, NCMP])
        cmp_keep = sb("cmp_keep", [P, T, NCMP])
        blk_upto = sb("blk_upto", [P, P])
        blk_after = sb("blk_after", [P, P])
        blk_sum = sb("blk_sum", [P, 2])
        minus_half = sb("minus_half", [P, 1])
        N_NORMS = 3 * L1 + 2 + 5 * L2
        stats = sb("stats", [P, N_NORMS, 16])
        softmax_s = sb("softmax_s", [P, 2, 4, HEADS])
        gqkv = sb("gqkv", [P, LAYERS, 3])
        fbias = sb("fbias", [P, LAYERS, HEADS])
        peT = sb("peT", [P, LAYERS, 2, CMP_PAIRS])
        conv_wT = sb("conv_wT", [P, LAYERS, CT, TAPS])
        conv_p = sb("conv_p", [P, 3, LAYERS, CT])
        gla_g = sb("gla_g", [P, LAYERS, P])
        wa2 = sb("wa2", [32, LAYERS, GK])
        pos_i = sb("pos_i", [P, T], I32)
        pos_f = sb("pos_f", [P, T])
        freq = sb("freq", [P, NFREQ])
        ang = sb("ang", [P, T, NFREQ])
        red = sb("red", [P, 2, T, NFREQ])
        halves = sb("halves", [P, T, 2, 6])
        turns = sb("turns", [P, 2, T, NFREQ])
        rope = sb("rope", [P, 2, T, NFREQ])
        arena = placed("arena", [ARENA], ARENA_AT, F32)

        def cut(lo, n, pattern=None, **sizes):
            v = arena[:, lo:lo + n]
            return v.rearrange(pattern, **sizes) if pattern else v

        z = cut(0, T * GATE0, "p (t n) -> p t n", t=T)
        GATE_AT = T * GATE0
        gate = cut(GATE_AT, T * 4 * D, "p (t n) -> p t n", t=T)
        PROBS_AT = GATE_AT + T * 4 * D
        probs = cut(PROBS_AT, 2 * HEADS * SEQ, "p (b h k) -> p b h k", b=2, h=HEADS)
        PT_AT = PROBS_AT + 2 * HEADS * SEQ
        PT = cut(PT_AT, 2 * T * HEADS * P, "p (b m h q) -> p b m h q", b=2, m=T, h=HEADS)
        ATT_AT = PT_AT + 2 * T * HEADS * P
        attT = cut(ATT_AT, N_ATT_T * SEQ, "p (s q) -> p s q", s=N_ATT_T)
        MORE = ATT_AT + N_ATT_T * SEQ
        mv = cut(MORE, T * 256, "p (t n) -> p t n", t=T)
        d8 = [cut(MORE + 512, 512, "p (h k) -> p h k", h=HEADS), cut(MORE + 1024, 1024, "p (h k) -> p h k", h=HEADS)]
        index_bias = [cut(MORE + 2048, P), cut(MORE + 2048 + P, SEQ)]
        cmpR = cut(MORE + 2432, 2 * CMP_PAIRS * NCMP, "p (w a c) -> p w a c", w=2, a=CMP_PAIRS)
        kcmpT = cut(MORE + 2912, NCMP)
        vcmp = cut(MORE + 2928, HD)
        lf = cut(MORE + 2992, 3 * T * HEADS, "p (s t h) -> p s t h", s=3, t=T)
        cq8 = cut(MORE + 3016, T * HEADS, "p (t h) -> p t h", t=T)
        gn = cut(MORE + 3024, T * 12, "p (t g) -> p t g", t=T)
        best = cut(MORE + 3048, 8)
        cT = cut(MORE + 3312, 3 * SEQ, "p (k s) -> p k s", k=3)
        otmp = cut(MORE + 3056, 256, "p (h d) -> p h d", h=HEADS)
        LATE = 4 * D - 3 * BANK
        mqk = cut(GATE_AT + 4 * D + LATE, 3 * BANK, "p (t h d) -> p t h d", t=T, h=8)
        rope_tmp = cut(GATE_AT + LATE, 4 * P, "p (s n) -> p s n", s=4)
        relu_l = cut(GATE_AT + LATE + 512, 2 * 2 * SEQ, "p (b h k) -> p b h k", b=2, h=2)
        stage = cut(PT_AT, T * 6 * P, "p (t s n) -> p t s n", t=T, s=6)
        decay_rows = [cut(PROBS_AT, HEADS * SEQ, "p (h k) -> p h k", h=HEADS), cut(PROBS_AT + HEADS * SEQ, HEADS * P, "p (h k) -> p h k", h=HEADS)]
        osb = [z[:, :, c:c + 256].rearrange("p t (h d) -> p t h d", h=HEADS) for c in (MLA0, NSA_Q, FOX_Q, DSA_Q)]
        up_sq = cut(8192 + 4 * D_FF, 2 * BANK, "p (b n) -> p b n", b=2)
        row_gain = cut(8192 + 4 * D_FF + 2 * BANK, D)
        lng = cut(0, 4 * D, "p (b w n) -> p b w n", b=2, w=2)
        xkT = cut(6144, 2048, "p (k s) -> p k s", s=SEQ)
        xv = cut(8192, 2048, "p (t n) -> p t n", t=T)
        qez = cut(10240, 1024, "p (g c k) -> p g c k", g=2, c=4)
        gattT = cut(11264, 1024, "p (t h c) -> p t h c", t=T, h=HEADS)
        state = cut(12288, 768, "p (c g e) -> p c g e", c=3, g=2)
        dec = cut(13056, 8, "p (g c) -> p g c", g=2)
        w_alow = cut(13064, KT * RANK, "p (k n) -> p k n", k=KT)
        qeT = cut(PROBS_AT, 512, "p (g s) -> p g s", g=2)
        keT = cut(PROBS_AT + 512, 512, "p (g s) -> p g s", g=2)
        alT = arena[0:32, PROBS_AT + 1024:PROBS_AT + 1024 + SEQ]
        mean_c = cut(PT_AT, SEQ)
        root_diag = cut(PT_AT + SEQ, T * P, "p (t n) -> p t n", t=T)
        gla_junk = cut(PT_AT + 1024, P)
        Z2 = ATT_AT
        u2 = cut(Z2, 1024, "p (t n) -> p t n", t=T)
        go2 = u2
        sg2 = cut(Z2 + 1024, 1024, "p (t n) -> p t n", t=T)
        sq2 = cut(Z2 + 1024, 1024, "p (c s) -> p c s", c=CT)
        la = cut(Z2 + 2048, 1536, "p (s t n) -> p s t n", s=3, t=T)
        ex2 = cut(Z2 + 3584, 1536, "p (s t n) -> p s t n", s=3, t=T)
        sr2 = cut(Z2 + 5120, 1024, "p (t n) -> p t n", t=T)
        v2 = cut(Z2 + 6144, 1024, "p (t n) -> p t n", t=T)
        qk2 = cut(Z2 + 7168, 1024, "p (t n) -> p t n", t=T)
        xqT = cut(Z2 + 6144, 2048, "p (k s) -> p k s", s=SEQ)
        uT = cut(Z2 + 8192, CT * (PAD + SEQ), "p (c s) -> p c s", c=CT)
        acc = cut(Z2 + 8192 + CT * (PAD + SEQ), CT * SEQ, "p (c s) -> p c s", c=CT)
        ffs = cut(Z2 + 8192 + CT * (PAD + SEQ), 512, "p (b s) -> p b s", b=2)
        ffp = cut(Z2 + 8192 + CT * (PAD + SEQ) + 512, 512, "p (b s) -> p b s", b=2)

        ps = ctx.enter_context(nc.psum_tensor("ps", [P, 8, BANK], F32))
        scores = ps[:, 6:8, :].rearrange("p b (h k) -> p (b h) k", h=2)

        lin_plan, small_plan = plans(L1, L2)
        lin = Turns([ps[:, b, :] for b in range(4)], lin_plan, sem("lin_filled"), {e: sem(f"lin_moved_by_{e}") for e in ("act", "dve")})
        small = Turns([ps[:, b, :] for b in (4, 5)], small_plan, sem("small_filled"), {e: sem(f"small_moved_by_{e}") for e in ("act", "dve")})
        slot_loaded = [sem(f"slot_loaded_{i}") for i in range(SLOTS)]
        hi_ready = sem("weight_hi_ready")
        lo_ready = {e: sem(f"weight_lo_ready_by_{e}") for e in ("dve", "pool")}
        pieces_used = sem("weight_pieces_used")
        rounded = sem("activations_rounded")
        made = sem("activations_made")
        relued = sem("up_relued")
        split = sem("activations_split")
        x_loaded = [sem(f"x_loaded_{t}") for t in range(T)]
        pos_loaded = sem("pos_loaded")
        first_gain_loaded = sem("first_gain_loaded")
        row_gain_loaded = sem("row_gain_loaded")
        params_loaded = sem("params_loaded")
        ident_made = sem("ident_made")
        params2_loaded = sem("params2_loaded")
        consts_made = sem("consts_made")
        angles_made = sem("angles_made")
        rope_tables = sem("rope_tables")
        squares_summed = sem("squares_summed")
        mean_ready = sem("mean_ready")
        rstd_ready = sem("rstd_ready")
        normed = sem("normed")
        fox_logits = sem("fox_logits")
        fox_log = sem("fox_log")
        decay_ready = sem("decay_rows_ready")
        staged = sem("staged")
        mla_roped = sem("mla_roped")
        cmp_rows = sem("cmp_rows")
        nsa_tanh = sem("nsa_tanh")
        index_used = sem("index_logits_used")
        scores_filled = sem("scores_filled")
        bias_ready = sem("softmax_bias_ready")
        probs_made = sem("probs_made")
        probs_final = sem("probs_final")
        gated = sem("gates_summed")
        x_updated = sem("x_updated")
        mem_loaded = sem("mem_loaded")
        lng_loaded = [sem(f"gains_loaded_{i}") for i in range(2)]
        pads_zeroed = sem("pads_zeroed")
        alow_loaded = sem("alow_weights_loaded")
        low_log = sem("low_log")
        la_ready = sem("la_ready")
        r_tanh = sem("r_tanh")
        ff_tanh = sem("ff_tanh")
        qkd_ready = sem("qkd_ready")
        go_ready = sem("go_ready")
        conv_summed = sem("conv_summed")
        conv_centred = sem("conv_centred")
        conv_squared = sem("conv_squared")
        root_spread = sem("root_spread")
        conv_affine = sem("conv_affine")
        conv_tanh = sem("conv_tanh")
        conv_out = sem("conv_out")
        dve_step, act_step, pool_step = sem("dve_step"), sem("act_step"), sem("pool_step")
        stored = sem("stored")

        stream = []

        def slot_of(n):
            return ring[:, n % SLOTS, :]

        def rows(w, n0, nn, k0=0, kn=KT):
            return w[k0 * P:(k0 + kn) * P, n0:n0 + nn].rearrange("(k p) n -> p k n", p=P)

        def view(n, kn, nn, off=0):
            return slot_of(n)[:, off:off + kn * nn].rearrange("p (k n) -> p k n", k=kn)

        first_piece, piece_done, lo_due, used, width = {}, [], [], 0, {}
        lo_count = {"dve": 0, "pool": 0}

        def tile(key, parts, last, pieces=0, lo="dve"):
            nonlocal used
            for _ in range(pieces):
                lo_count[lo] += 1
                lo_due.append((lo_ready[lo], lo_count[lo]))
            if pieces:
                first_piece[key] = (len(piece_done), pieces)
                for i in range(pieces):
                    if key[0] == "lift":
                        piece_done.append((lin.filled, lin.at[key + (i, 1)] + 1))
                    elif last is not None and i == pieces - 1:
                        piece_done.append((last[0].filled, last[0].at[last[1]] + 1))
                    else:
                        used += 1
                        piece_done.append((pieces_used, used))
            stream.append((key, parts, last))

        def whole(key, w, n0, nn, last, k0=0, kn=KT, pieces=0, lo="dve"):
            width[key] = kn * nn // max(pieces, 1)
            tile(key, [(view(len(stream), kn, nn), rows(w, n0, nn, k0, kn))], last, pieces, lo)

        def square(name, l, w, k0s, lo="dve"):
            for j, k0 in enumerate(k0s):
                whole((name, l, j), w, 0, D, None if j == 0 else (lin, (name, l, 1, 1)), k0, 4, 4, lo)

        for l in range(L1):
            w_in = a["w_in"][l]
            for j, (c0, cn) in enumerate(Z_TILES[:4]):
                whole(("z", l, j), w_in, c0, cn, (lin, ("z", l, j, 1)), pieces=4, lo="dve" if j or l == 0 else "pool")
            n = len(stream)
            tile(("u", l), [(view(n, 2, 384), rows(a["mla_w_uq"][l], 0, 384, 0, 2)),
                            (view(n, 1, 512, 768), rows(a["mla_w_ukv"][l], 0, 512, 0, 1))], (lin, ("ukv", l, 1)))
            whole(("z", l, 4), w_in, *Z_TILES[4], (lin, ("z", l, 4, 1)), pieces=4)
            whole(("gate", l, 0), w_in, GATE0, BANK, (lin, ("gate", l, 0, 1)), pieces=4)
            slot = slot_of(len(stream))
            ck = a["nsa_cmp_w"][l, 0].rearrange("(a p) e -> p a e", p=P)
            cv = a["nsa_cmp_w"][l, 1].rearrange("(a p) e -> p a e", p=P)
            kd = slot[:, 0:CMP_PAIRS * P].rearrange("p (a e) -> p a e", e=P)
            vd = slot[:, CMP_PAIRS * P:CMP_PAIRS * (P + HD)].rearrange("p (a e) -> p a e", e=HD)
            tile(("cmp", l), [(kd[:, :, 0:HD], ck), (kd[:, :, HD:P], ck), (vd, cv)], (small, ("comp", l)))
            for j in range(1, GATE_TILES):
                whole(("gate", l, j), w_in, GATE0 + j * BANK, BANK, (lin, ("gate", l, j, 1)), pieces=4, lo="pool" if j > 1 else "dve")
            w_br = a["w_branch"][l].rearrange("b (c p) n -> p (b c) n", p=P)
            for f in range(2):
                tile(("lift", l, f), [(view(len(stream), KT, BANK), w_br[:, :, f * BANK:(f + 1) * BANK])], (lin, ("lift", l, f, 3, 1)), 4, "dve" if f else "pool")
            square("out", l, a["w_out"][l], (0, 4))
            for j in range(D_FF // BANK):
                whole(("up", l, j), a["w_up"][l], j * BANK, BANK, (lin, ("up", l, j, 1)), pieces=4, lo="dve" if j else "pool")
            for j in range(D_FF // BANK):
                whole(("down", l, j), a["w_down"][l], 0, D, None if j + 1 < D_FF // BANK else (lin, ("down", l, 1, 1)), 4 * j, 4, pieces=4)
        for l in range(L2):
            w2 = a["w_in_2"][l]
            whole(("xk", l, 0), a["w_xkv_2"][l], 0, BANK, (lin, ("xk", l, 1)), pieces=4, lo="pool")
            for key, c0 in (("cg", CONV), ("ca", 0), ("qk", 2 * CONV), ("v", 2 * CONV + 2 * GK), ("r", 2 * CONV + 2 * GK + GV)):
                whole((key, l), w2, c0, BANK, (lin, (key, l, 1)), pieces=4, lo="pool" if key in ("v", "r") else "dve")
            whole(("xk", l, 1), a["w_xkv_2"][l], BANK, BANK, (lin, ("xk", l, 3)), pieces=4, lo="pool")
            for f in range(2):
                whole(("xv", l, f), a["w_xkv_2"][l], D + f * BANK, BANK, (lin, ("xv", l, f, 1)), pieces=4, lo="pool")
            square("mix", l, a["w_mix_out_2"][l], (CT, 0), "pool")
            for f in range(2):
                whole(("xq", l, f), a["w_xq_2"][l], f * BANK, BANK, (lin, ("xq", l, 2 * f + 1)), pieces=4, lo="dve" if f else "pool")
            square("xo", l, a["w_xo_2"][l], (0, 4))
            for j in range(FT2 // 2):
                v = view(len(stream), KT, BANK)
                tile(("ffn", l, j), [(v[:, :, 0:SEQ], rows(a["w_ffn_in_2"][l], j * SEQ, SEQ)),
                                     (v[:, :, SEQ:BANK], rows(a["w_ffn_in_2"][l], DFF2 + j * SEQ, SEQ))], (lin, ("ffn", l, 2 * j + 1)), 4, "dve" if j else "pool")
            for j in range(-(-FT2 // 4)):
                whole(("ffo", l, j), a["w_ffn_out_2"][l], 0, D, None if 4 * j + 4 < FT2 else (lin, ("ffo", l, 1, 1)), 4 * j, min(4, FT2 - 4 * j), pieces=min(4, FT2 - 4 * j))
        place = {key: n for n, (key, _, _) in enumerate(stream)}
        due, loads = [], [0] * SLOTS
        for n, (_, parts, _) in enumerate(stream):
            loads[n % SLOTS] += 16 * len(parts)
            due.append(loads[n % SLOTS])

        def arrived(eng, key):
            n = place[key]
            eng.wait_ge(slot_loaded[n % SLOTS], due[n])
            return n

        parts, from_sbuf = [], []
        for l in range(L1):
            parts += [("n1", l, t, f) for t in range(T) for f in range(2)]
            parts += [("oT", l, b) for b in range(4)] + [("mixT", l, t, f) for t, f in turn_order("mixT")]
            parts += [("n2", l, t, f) for t in range(T) for f in range(2)]
            made_here = [("up", l, j, b) for j in range(D_FF // BANK) for b in range(2)]
            parts += made_here
            from_sbuf += made_here
        parts += [("memT", t, f) for t in range(T) for f in range(2)]
        for l in range(L2):
            parts += [("hT", l, t, f) for t in range(T) for f in range(2)] + [("goT", l, t) for t in range(T)] + [("conv", l)]
            parts += [("h1T", l, t, f) for t in range(T) for f in range(2)] + [("xO", l, t, f) for t in range(T) for f in range(2)]
            parts += [("h2T", l, t, f) for t in range(T) for f in range(2)] + [("ffn", l, f) for f in range(FT2)]
            from_sbuf += [("conv", l)] + [("ffn", l, f) for f in range(FT2)]
        part_at = {key: n + 1 for n, key in enumerate(parts)}
        split_at = {key: n + 1 for n, key in enumerate(from_sbuf)}
        made_at = {key: n + 1 for n, key in enumerate(k for k in from_sbuf if k[0] == "up")}

        norms = [(w, l) for l in range(L1) for w in ("n1", "mla", "n2")] + ["final", "ln0"] \
            + [(w, l) for l in range(L2) for w in ("gla", "conv", "ln1", "ln2", "ln3")]
        norm_at = {key: n for n, key in enumerate(norms)}
        SQUARES = {"n1": 2, "mla": 4, "n2": 2, "gla": 8}
        sq_due, s = {}, 0
        for key in norms:
            s += 2 if key == "final" else SQUARES.get(key[0], 0)
            sq_due[key] = s
        BY_ROWS = ("n1", "n2", "final", "ln0", "ln1", "ln2", "ln3")
        roots = [(key, t) for key in norms for t in range(T if (key if isinstance(key, str) else key[0]) in BY_ROWS else 1)]
        i = roots.index(("final", 0))
        roots[i:i + 2 * T] = [(key, t) for t in range(T) for key in ("final", "ln0")]
        root_at = {key: n + 1 for n, key in enumerate(roots)}
        normed_due = {(w, l): [6 * l + 2 * i + t + 1 for t in range(T)] for l in range(L1) for i, w in enumerate(("n1", "mla", "n2"))}
        updates = [(w, l) for l in range(L1) for w in ("out", "down")] + ["final", "ln0"] + [(w, l) for l in range(L2) for w in ("ln1", "ln2", "ln3")]
        update_at, s = {}, 0
        for keys in [[k] for k in updates if k not in ("final", "ln0")][:2 * L1] + [["final", "ln0"]] + [[k] for k in updates if k[0] in ("ln1", "ln2", "ln3")]:
            for t in range(T):
                for k in keys:
                    s += 1
                    update_at[k, t] = s
        gain_due = {(w, l): (row_gain_loaded, 16 * (2 * l + i)) if l + i else (first_gain_loaded, 16) for l in range(L1) for i, w in enumerate(("n1", "n2"))}
        gains = ["final", "ln0"] + [(w, l) for l in range(L2) for w in ("ln1", "ln2", "ln3")]
        gains_due, s = {}, [0, 0]
        for n, key in enumerate(gains):
            s[n % 2] += 16 if n == 0 else 32
            gains_due[key] = s[n % 2]
        NP1 = len(PATHS1)
        LAST_ATT1 = L1 * NP1

        def att1(l, i):
            return l * NP1 + i

        def att2(l, t):
            return LAST_ATT1 + l * T + t

        block = ctx.enter_context(nc.Block())

        @block.sync
        def _(sp):
            for t in range(T):
                sp.dma_start(x[:, t, :], a["x"][0, t * P:(t + 1) * P, :]).then_inc(x_loaded[t], 16)
            for n, (_, parts, _) in enumerate(stream):
                if n >= SLOTS:
                    key, _, last = stream[n - SLOTS]
                    if key in first_piece:
                        sp.wait_ge(*lo_due[sum(first_piece[key]) - 1])
                    else:
                        sp.wait_ge(last[0].filled, last[0].at[last[1]] + 1)
                for dst, src in parts:
                    sp.dma_start(dst, src).then_inc(slot_loaded[n % SLOTS], 16)
                if n == SLOTS - 1:
                    for l in range(LAYERS):
                        sp.dma_start(gqkv[:, l, 0:2], a["mla_q_norm_g"][l].rearrange("(k p) -> p k", p=P), allow_slow_non_contiguous=True).then_inc(params_loaded, 16)
                        sp.dma_start(gqkv[:, l, 2:3], a["mla_kv_norm_g"][l].rearrange("(k p) -> p k", p=P), allow_slow_non_contiguous=True).then_inc(params_loaded, 16)
                        sp.dma_start(fbias[:, l, :], a["fox_f_bias"][l].partition_broadcast(P)).then_inc(params_loaded, 16)
                        for w in range(2):
                            sp.dma_start(peT[:, l, w, :], a["nsa_cmp_pe"][l, w].rearrange("(i e) d -> (e d) i", e=2), allow_slow_non_contiguous=True).then_inc(params_loaded, 16)
                if n == SLOTS + 1:
                    for l in range(LAYERS):
                        for c in range(CT):
                            sp.dma_start(conv_wT[:, l, c, :], a["conv_w_2"][l, :, c * P:(c + 1) * P].rearrange("j p -> p j"), allow_slow_non_contiguous=True).then_inc(params2_loaded, 16)
                        for w, name in enumerate(("conv_b_2", "conv_ln_g_2", "conv_ln_b_2")):
                            sp.dma_start(conv_p[:, w, l, :], a[name][l].rearrange("(k p) -> p k", p=P), allow_slow_non_contiguous=True).then_inc(params2_loaded, 16)
                        sp.dma_start(gla_g[:, l, :], a["gla_norm_g_2"][l].partition_broadcast(P)).then_inc(params2_loaded, 16)
                        sp.dma_start(wa2[0:RANK, l, :], a["w_a2_2"][l]).then_inc(params2_loaded, 16)
                        sp.dma_start(wa2[RANK:RANK + 1, l, :], a["b_a_2"][l:l + 1, :]).then_inc(params2_loaded, 16)

            for t in range(T):
                sp.wait_ge(x_updated, T * (len(updates) - 1) + t + 1)
                sp.dma_start(out[0, t * P:(t + 1) * P, :], x[:, t, :]).then_inc(stored, 16)
            sp.wait_ge(stored, 16 * T)

        @block.tensor
        def _(pe):
            def by_tokens(key, xT, w, t, kn, n, c0=0):
                bank = lin.open(pe, key)
                for k in range(kn):
                    m = pe.matmul(bank[:, 0:n], xT[:, k, t * P:(t + 1) * P], w[:, k, c0:c0 + n], start=(k == 0), stop=(k == kn - 1))
                m.then_inc(lin.filled, 1)

            def turn_over(key, sources):
                bank = small.open(pe, key)
                for i, src in enumerate(sources):
                    m = pe.transpose(bank[0:src.shape[-1], i * P:i * P + src.shape[0]], src, ident[:, :])
                m.then_inc(small.filled, 1)

            def products(hi, lo, x_hi, x_lo):
                return ((hi, x_hi), (hi, x_lo), (lo, x_hi))

            def weight_piece(key, i, kn):
                q = first_piece[key][0] + i
                pe.wait_ge(*lo_due[q])
                return [w[:, q % PIECES, 0:width.get(key, PIECE)].rearrange("p (k n) -> p k n", k=kn) for w in (w_hi, w_lo)]

            def split_tokens(tile_key, keys, x_hi, x_lo, n=BANK, which=range(4)):
                banks = [(lin.open(pe, key) if 0 in which else lin.bank(key))[:, 0:n] for key in keys]
                for i in which:
                    pieces = weight_piece(tile_key, i, 2)
                    for t, bank in enumerate(banks):
                        for k in range(2):
                            for j, (v, w) in enumerate(products(x_hi, x_lo, *pieces)):
                                m = pe.matmul(bank, v(2 * i + k, t), w[:, k, :], start=(i + k + j == 0), stop=(i == 3 and k == 1 and j == 2))
                        if i == 3:
                            m.then_inc(lin.filled, 1)
                    if i < 3:
                        m.then_inc(pieces_used, 1)

            def by_tile(v):
                return lambda k, t: v[:, k, t * P:(t + 1) * P]

            def split_features(tile_key, keys, columns, x_hi=lambda k: hT_hi[:, k, :], x_lo=lambda k: hT_lo[:, k, :]):
                banks = [lin.open(pe, key) for key in keys]
                for i in range(4):
                    hi, lo = weight_piece(tile_key, i, 2)
                    for bank, c0s in zip(banks, columns):
                        for n, c0 in enumerate(c0s):
                            for k in range(2):
                                for j, (w, v) in enumerate(products(hi, lo, x_hi, x_lo)):
                                    m = pe.matmul(bank[:, n * SEQ:(n + 1) * SEQ], w[:, k, c0:c0 + P], v(2 * i + k),
                                                  start=(i + n + k + j == 0), stop=(i == 3 and n == 1 and k == 1 and j == 2), skip_group_check=True)
                        if i == 3:
                            m.then_inc(lin.filled, 1)
                    if i < 3:
                        m.then_inc(pieces_used, 1)

            def long_sum(name, l, x_hi, x_lo, n_k, ready, k0s=None, after_piece=None):
                keys = [(name, l, t, f) for t in range(T) for f in range(2)]
                banks = [None] * 4
                n_tiles = -(-n_k // 4)
                for j in range(n_tiles):
                    kn = min(4, n_k - 4 * j)
                    last = j == n_tiles - 1
                    at = [(t, f) for t in range(T) for f in range(2)]
                    ready(j, kn)
                    k0 = k0s[j] if k0s else 4 * j
                    pieces = [None] * kn
                    order = [(k, i) for i in range(4) for k in range(kn)] if last else [(k, i) for k in range(kn) for i in range(4)]
                    if j == 0 and n_tiles > 2:
                        order = [(k, i) for pair in ((0, 1), (2, 3)) for k in range(kn) for i in pair]
                    for k, i in order:
                        if pieces[k] is None:
                            pieces[k] = weight_piece((name, l, j), k, 1)
                        t, f = at[i]
                        if banks[i] is None:
                            banks[i] = lin.open(pe, keys[i])
                        for w, (xs, ws) in enumerate(products(x_hi, x_lo, *pieces[k])):
                            m = pe.matmul(banks[i], xs[:, k0 + k, t * P:(t + 1) * P], ws[:, 0, f * BANK:(f + 1) * BANK],
                                          start=(j + k + w == 0), stop=(last and k == kn - 1 and w == 2))
                        if last:
                            if k == kn - 1:
                                m.then_inc(lin.filled, 1)
                            elif i == 3:
                                m.then_inc(pieces_used, 1)
                        elif i == 3:
                            m.then_inc(pieces_used, 1)
                            if after_piece:
                                after_piece(j, k)

            pe.wait_ge(ident_made, 1)
            for l in range(L1):
                nn = norm_at[("n1", l)]
                for t in range(T):
                    pe.wait_ge(normed, normed_due[("n1", l)][t])
                    for f in range(2):
                        turn_over(("n1", l, t, f), [hn[:, t, (4 * f + i) * P:(4 * f + i + 1) * P] for i in range(4)])
                small.wait_moved(pe, ("n1", l, 1, 1))

                def z_tile(j):
                    split_tokens(("z", l, j), [("z", l, j, t) for t in range(T)], by_tile(hT_hi), lambda k, t: hn_lo[:, t, k, :], Z_TILES[j][1])

                def gate_piece(g):
                    j, i = g // 4, g % 4
                    split_tokens(("gate", l, j), [("gate", l, j, t) for t in range(T)], by_tile(hT_hi), lambda k, t: hn_lo[:, t, k, :], which=[i])

                for j in range(3):
                    z_tile(j)
                if l == 0:
                    pe.wait_ge(consts_made, 1)
                for t in range(T):
                    pe.wait_ge(normed, normed_due[("mla", l)][t])
                    turn_over(("cT", l, t), [z[:, t, i * P:(i + 1) * P] for i in range(3)])
                z_tile(3)
                n = arrived(pe, ("u", l))
                for t in range(T):
                    small.wait_moved(pe, ("cT", l, t))
                    by_tokens(("uq", l, t), cT, view(n, 2, 384), t, 2, 384)
                    by_tokens(("ukv", l, t), cT[:, 2:3, :], view(n, 1, 512, 768), t, 1, 512)
                z_tile(4)
                pe.wait_ge(decay_ready, l + 1)
                bank = small.open(pe, ("cq", l))
                pe.matmul(bank[:, 0:4], upto[:, 0:P], lf[:, 2, 0, :], start=True, stop=True)
                pe.matmul(bank[:, 4:8], ones, lf[:, 2, 0, :], start=True, stop=False)
                pe.matmul(bank[:, 4:8], upto[:, 0:P], lf[:, 2, 1, :], start=False, stop=True).then_inc(small.filled, 1)
                for f in range(2):
                    bank = lin.open(pe, ("ck", l, f)).rearrange("p (h k) -> p h k", h=2)
                    pe.matmul(bank, ones, decay_rows[0][:, 2 * f:2 * f + 2, :], start=True, stop=False)
                    for h in range(2):
                        m = pe.matmul(bank[:, h, P:SEQ], ones, decay_rows[1][:, 2 * f + h, :], start=False, stop=(h == 1))
                    m.then_inc(lin.filled, 1)
                for t in range(T):
                    turn_over(("foxT", l, t), [z[:, t, FOX_Q + i * P:FOX_Q + (i + 1) * P] for i in range(4)])
                for g in range(2):
                    gate_piece(g)
                pe.wait_ge(staged, l + 1)
                for t in range(T):
                    turn_over(("nsa", l, t), [z[:, t, NSA_Q:NSA_Q + P], z[:, t, NSA_Q + P:NSA_Q + 2 * P], stage[:, t, 0, :], stage[:, t, 1, :]])
                for t in range(T):
                    turn_over(("idx", l, t), [z[:, t, DSA_QI:DSA_QI + P], z[:, t, DSA_QI + P:DSA_QI + 2 * P], stage[:, t, 4, :], stage[:, t, 5, :]])
                for g in range(2, 4):
                    gate_piece(g)
                n = arrived(pe, ("cmp", l))
                pe.wait_ge(cmp_rows, l + 1)
                kd = slot_of(n)[:, 0:CMP_PAIRS * P].rearrange("p (a e) -> p a e", e=P)
                vd = slot_of(n)[:, CMP_PAIRS * P:CMP_PAIRS * (P + HD)].rearrange("p (a e) -> p a e", e=HD)
                bank = small.open(pe, ("comp", l))
                for i in range(CMP_PAIRS):
                    pe.matmul(bank[:, 0:NCMP], kd[:, i, :], cmpR[:, 0, i, :], start=(i == 0), stop=(i == CMP_PAIRS - 1))
                for i in range(CMP_PAIRS):
                    m = pe.matmul(bank[0:NCMP, 64:64 + HD], cmpR[:, 1, i, :], vd[:, i, :], start=(i == 0), stop=(i == CMP_PAIRS - 1))
                m.then_inc(small.filled, 1)
                pe.wait_ge(mla_roped, l + 1)
                for w, h0 in (("mq", 0), ("mk", 4)):
                    for t in range(T):
                        turn_over((w, l, t), [mqk[:, t, h0 + h, :] for h in range(4)])
                for t in range(T):
                    turn_over(("dsa", l, t), [z[:, t, DSA_Q:DSA_Q + P], z[:, t, DSA_Q + P:DSA_Q + 2 * P], stage[:, t, 2, :], stage[:, t, 3, :]])
                small.wait_moved(pe, ("dsa", l, 1))
                for t in range(T):
                    nk = P * (t + 1)
                    for f in range(4):
                        bank = lin.open(pe, ("idx", l, t, f))
                        for i in range(2):
                            h = f + 4 * i
                            r = slice(IDX_DIM * (h % 4), IDX_DIM * (h % 4 + 1))
                            m = pe.matmul(bank[:, i * SEQ:i * SEQ + nk], attT[r, S_QI + h // 4, t * P:(t + 1) * P], attT[r, S_KI, 0:nk], start=True, stop=True)
                        m.then_inc(lin.filled, 1)
                small.wait_moved(pe, ("comp", l))
                def path_scores(i):
                    path, t = PATHS1[i]
                    aa = att1(l, i)
                    nk = NCMP if path == "cmp" else P * (t + 1)
                    if aa:
                        pe.wait_ge(probs_made, aa)
                    for s, h in enumerate(BY_SLOT):
                        r = slice(HD * (h % 2), HD * (h % 2 + 1))
                        tq = slice(t * P, (t + 1) * P)
                        if path == "mla":
                            q, k = attT[0:MLA_HD, S_MLA_Q + h, tq], attT[0:MLA_HD, S_MLA_K + h, 0:nk]
                        elif path == "fox":
                            q, k = attT[r, S_FOX_Q + h // 2, tq], attT[r, S_FOX_K + h // 2, 0:nk]
                        elif path == "dsa":
                            q, k = attT[r, S_DSA_Q + h // 2, tq], attT[r, S_DSA_K, 0:nk]
                        elif path == "cmp":
                            q, k = attT[r, S_NSA_Q + h // 2, tq], kcmpT[r, :]
                        else:
                            q, k = attT[r, S_NSA_Q + h // 2, tq], attT[r, S_KS if path == "sel" else S_KW, 0:nk]
                        m = pe.matmul(scores[:, s, 0:nk], q, k, start=True, stop=True)
                    m.then_inc(scores_filled, 1)

                g = 4
                path_scores(0)
                for i, (path, t) in enumerate(PATHS1):
                    aa = att1(l, i)
                    for _ in range(FILL[i] - 1):
                        gate_piece(g)
                        g += 1
                    b = aa % 2
                    if path == "cmp":
                        pe.wait_ge(probs_final, cmp_final(l, t))
                        turn_over(("PT", l, i, 0), [probs[:, b, h, 0:NCMP] for h in range(HEADS)])
                    else:
                        pe.wait_ge(probs_made, aa + 1)
                        for kb in range(t + 1):
                            turn_over(("PT", l, i, kb), [probs[:, b, h, kb * P:(kb + 1) * P] for h in range(HEADS)])
                    if i + 1 < NP1:
                        path_scores(i + 1)
                    gate_piece(g)
                    g += 1
                    kbs = 1 if path == "cmp" else t + 1
                    bank = small.open(pe, ("PV", l, i))
                    small.wait_moved(pe, ("PT", l, i, kbs - 1))
                    for s, h in enumerate(BY_SLOT):
                        for kb in range(kbs):
                            if path == "cmp":
                                p, v = PT[0:NCMP, b, 0, s, :], vcmp[0:NCMP, :]
                            else:
                                p = PT[:, b, kb, s, :]
                                c = {"mla": 0, "fox": FOX_V + h * HD, "sel": NSA_VS, "win": NSA_VW, "dsa": DSA_V}[path]
                                v = mv[:, kb, h * HD:(h + 1) * HD] if path == "mla" else z[:, kb, c:c + HD]
                            m = pe.matmul(bank[:, h * HD:(h + 1) * HD], p, v, start=(kb == 0), stop=(kb == kbs - 1))
                    m.then_inc(small.filled, 1)
                small.wait_moved(pe, ("PV", l, NP1 - 1))
                for b in range(4):
                    turn_over(("oT", l, b), [osb[b][:, t, 2 * c:2 * c + 2, :].rearrange("p h d -> p (h d)") for c in range(2) for t in range(T)])
                for f in range(2):
                    for b in range(4):
                        if f == 0:
                            small.wait_moved(pe, ("oT", l, b))
                        banks = [lin.open(pe, ("lift", l, f, b, t)) for t in range(T)]
                        pieces = weight_piece(("lift", l, f), b, 2)
                        for t in range(T):
                            for k in range(2):
                                for j, (v, w) in enumerate(products(hT_hi, hT_lo2, *pieces)):
                                    m = pe.matmul(banks[t], v[:, 2 * b + k, t * P:(t + 1) * P], w[:, k, :], start=(k + j == 0), stop=(k == 1 and j == 2))
                            m.then_inc(lin.filled, 1)
                for t, f in turn_order("mixT"):
                    pe.wait_ge(gated, 4 * l + 2 * f + t + 1)
                    turn_over(("mixT", l, t, f), [gate[:, t, f * BANK + i * P:f * BANK + (i + 1) * P] for i in range(4)])
                small.wait_moved(pe, ("mixT", l, 1, 1))
                long_sum("out", l, hT_hi, hT_lo2, KT, lambda j, kn: None)
                for t in range(T):
                    pe.wait_ge(normed, normed_due[("n2", l)][t])
                    for f in range(2):
                        turn_over(("n2", l, t, f), [hn[:, t, (4 * f + i) * P:(4 * f + i + 1) * P] for i in range(4)])
                small.wait_moved(pe, ("n2", l, 1, 1))
                for j in range(D_FF // BANK):
                    split_features(("up", l, j), [("up", l, j, b) for b in range(2)], [[2 * b * P, (2 * b + 1) * P] for b in range(2)])

                def turn_memory(j, k):
                    if l == L1 - 1 and j == 1:
                        if k == 0:
                            pe.wait_ge(mem_loaded, 16)
                        t, f = k // 2, k % 2
                        turn_over(("memT", t, f), [hn[:, t, (4 * f + i) * P:(4 * f + i + 1) * P] for i in range(4)])

                long_sum("down", l, up_hi, up_lo, D_FF // P, lambda j, kn: pe.wait_ge(split, split_at[("up", l, j, 1)]), after_piece=turn_memory)

            for l in range(L2):
                def turn_x(name, update):
                    for t in range(T):
                        pe.wait_ge(x_updated, update_at[update, t])
                        for f in range(2):
                            turn_over((name, l, t, f), [x[:, t, (4 * f + i) * P:(4 * f + i + 1) * P] for i in range(4)])
                    small.wait_moved(pe, (name, l, 1, 1))

                def mem_keys(f):
                    split_features(("xk", l, f), [("xk", l, 2 * f + b) for b in range(2)], [[2 * b * P, (2 * b + 1) * P] for b in range(2)],
                                   lambda k: mem_hi[:, :, k, :], lambda k: mem_lo[:, :, k, :])

                small.wait_moved(pe, ("memT", 1, 1))
                mem_keys(0)
                turn_x("hT", "ln0" if l == 0 else ("ln3", l - 1))
                pe.wait_ge(alow_loaded, 16 * (l + 1))
                bank = small.open(pe, ("alow", l))
                for k in range(KT):
                    for part in (hT_hi, hT_lo3):
                        m = pe.matmul(bank[0:RANK, 0:SEQ], w_alow[:, k, :], part[:, k, :].bitcast(F32), start=(k == 0 and part is hT_hi), stop=(k == KT - 1 and part is hT_lo3))
                m.then_inc(small.filled, 1)

                def proj(key, which=range(4)):
                    split_tokens((key, l), [(key, l, t) for t in range(T)], by_tile(hT_hi), by_tile(hT_lo3), which=which)

                proj("cg")
                proj("ca")
                proj("qk", [0])
                for t in range(T):
                    lin.wait_moved(pe, ("ca", l, t))
                    turn_over(("uT", l, t), [u2[:, t, i * P:(i + 1) * P] for i in range(4)])
                proj("qk", [1])
                small.wait_moved(pe, ("alow", l))
                for t in range(T):
                    bank = small.open(pe, ("zlow", l, t))
                    pe.matmul(bank[:, 0:GK], alT[0:RANK + 1, t * P:(t + 1) * P], wa2[0:RANK + 1, l, :], start=True, stop=True).then_inc(small.filled, 1)
                proj("qk", [2, 3])
                proj("v")
                for t in range(T):
                    pe.wait_ge(la_ready, T * l + t + 1)
                    bank = lin.open(pe, ("bc", l, t))
                    pe.matmul(bank[:, 0:GK], blk_upto[:, :], la[:, 0, t, :], start=True, stop=True)
                    pe.matmul(bank[:, GK:2 * GK], blk_after[:, :], la[:, 0, t, :], start=True, stop=True).then_inc(lin.filled, 1)
                bank = small.open(pe, ("blast", l))
                for g in range(2):
                    for t in range(T):
                        m = pe.matmul(bank[:, 4 * g + 2 * t:4 * g + 2 * t + 2], la[:, 0, t, g * P:(g + 1) * P], blk_sum[:, :], start=True, stop=True)
                m.then_inc(small.filled, 1)
                proj("r", [0, 1, 2])
                for t in range(T):
                    pe.wait_ge(qkd_ready, T * l + t + 1)
                    turn_over(("qeT", l, t), [ex2[:, s, t, g * P:(g + 1) * P] for s in range(2) for g in range(2)])
                proj("r", [3])
                for t in range(T):
                    small.wait_moved(pe, ("qeT", l, t))
                    for e in range(2):
                        r = slice(HD * e, HD * (e + 1))
                        bank = lin.open(pe, ("att", l, t, e))
                        for g in range(2):
                            m = pe.matmul(bank[:, g * P:(g + 1) * P], keT[r, g, t * P:(t + 1) * P], qeT[r, g, t * P:(t + 1) * P], start=True, stop=True)
                        m.then_inc(lin.filled, 1)
                lin.wait_moved(pe, ("v", l, 1))
                for c in range(3):
                    bank = lin.open(pe, ("upd", l, c))
                    r = slice(CHUNK * (c % 2), CHUNK * (c % 2 + 1))
                    for g in range(2):
                        m = pe.matmul(bank[:, g * SEQ:(g + 1) * SEQ], ex2[r, 2, c // 2, g * P:(g + 1) * P], v2[r, c // 2, g * SEQ:(g + 1) * SEQ], start=True, stop=True)
                    m.then_inc(lin.filled, 1)
                mem_keys(1)

                def mem_values(f, which=range(4)):
                    split_tokens(("xv", l, f), [("xv", l, f, t) for t in range(T)], lambda k, t: mem_hi[:, t, k, :], lambda k, t: mem_lo[:, t, k, :], which=which)

                mem_values(0)
                lin.wait_moved(pe, ("upd", l, 2))
                for t in range(T):
                    for e in range(2):
                        lin.wait_moved(pe, ("att", l, t, e))
                        bank = lin.open(pe, ("go", l, t, e))
                        r = slice(HD * e, HD * (e + 1))
                        chunks = [c for c in (2 * t, 2 * t + 1) if c > 0]
                        for g in range(2):
                            h = 2 * g + e
                            o = bank[:, g * P:(g + 1) * P]
                            pe.matmul(o, gattT[:, t, h, :], v2[:, t, h * P:(h + 1) * P], start=True, stop=False)
                            for c in chunks:
                                m = pe.matmul(o, qez[r, g, c, :], state[r, c - 1, g, :], start=False, stop=(c == chunks[-1]))
                        m.then_inc(lin.filled, 1)
                pe.wait_ge(conv_summed, l + 1)
                bank = small.open(pe, ("cmean", l))
                for c in range(CT):
                    m = pe.matmul(bank[:, 0:SEQ], ones, acc[:, c, :], start=(c == 0), stop=(c == CT - 1))
                m.then_inc(small.filled, 1)
                mem_values(1, [0, 1])
                pe.wait_ge(conv_squared, l + 1)
                bank = small.open(pe, ("cvar", l))
                for t in range(T):
                    for c in range(CT):
                        m = pe.matmul(bank[:, t:t + 1], sq2[:, c, t * P:(t + 1) * P], ones[:, 0:1], start=(c == 0), stop=(c == CT - 1))
                m.then_inc(small.filled, 1)
                mem_values(1, [2])
                for t in range(T):
                    pe.wait_ge(go_ready, T * l + t + 1)
                    turn_over(("goT", l, t), [go2[:, t, i * P:(i + 1) * P] for i in range(4)])
                mem_values(1, [3])
                pe.wait_ge(root_spread, l + 1)
                bank = small.open(pe, ("crstd", l))
                for t in range(T):
                    m = pe.matmul(bank[:, t * P:(t + 1) * P], ones, root_diag[:, t, :], start=True, stop=True)
                m.then_inc(small.filled, 1)
                def mix_ready(j, kn):
                    if j == 0:
                        small.wait_moved(pe, ("goT", l, 1))
                    else:
                        pe.wait_ge(split, split_at[("conv", l)])

                long_sum("mix", l, hT_hi, hT_lo2, KT, mix_ready, (CT, 0))
                turn_x("h1T", ("ln1", l))
                for f in range(2):
                    split_features(("xq", l, f), [("xq", l, 2 * f + b) for b in range(2)], [[2 * b * P, (2 * b + 1) * P] for b in range(2)],
                                   x_lo=lambda k: hT_lo2[:, k, :])
                lin.wait_moved(pe, ("xq", l, 3))
                lin.wait_moved(pe, ("xv", l, 1, 1))

                def x_scores(t):
                    pe.wait_ge(probs_made, att2(l, t))
                    for h in range(XH):
                        for k in range(2):
                            m = pe.matmul(scores[:, h, :], xqT[:, 2 * h + k, t * P:(t + 1) * P], xkT[:, 2 * h + k, :], start=(k == 0), stop=(k == 1))
                    m.then_inc(scores_filled, 1)

                def x_out(t):
                    b = att2(l, t) % 2
                    pe.wait_ge(probs_final, T * L1 + T * l + t + 1)
                    for kb in range(T):
                        turn_over(("xPT", l, t, kb), [probs[:, b, h, kb * P:(kb + 1) * P] for h in range(XH)])
                    small.wait_moved(pe, ("xPT", l, t, 1))
                    for f in range(2):
                        bank = lin.open(pe, ("xO", l, t, f))
                        for i in range(4):
                            h, c = 2 * f + i // 2, i % 2
                            for kb in range(T):
                                m = pe.matmul(bank[:, i * P:(i + 1) * P], xv[:, kb, h * XD + c * P:h * XD + (c + 1) * P], PT[:, b, kb, h, :], start=(kb == 0), stop=(kb == 1))
                        m.then_inc(lin.filled, 1)

                x_scores(0)
                x_scores(1)
                x_out(0)
                x_out(1)
                lin.wait_moved(pe, ("xO", l, 1, 1))
                long_sum("xo", l, hT_hi, hT_lo2, KT, lambda j, kn: None)
                turn_x("h2T", ("ln2", l))
                for j in range(FT2 // 2):
                    split_features(("ffn", l, j), [("ffn", l, 2 * j + b) for b in range(2)], [[b * P, SEQ + b * P] for b in range(2)])
                long_sum("ffo", l, ff_hi, ff_lo, FT2, lambda j, kn: pe.wait_ge(split, split_at[("ffn", l, 4 * j + kn - 1)]))

        @block.scalar
        def _(act):
            step = Chain(act, act_step)

            def move(turns_, key, dst, take=lambda b: b, func=ACT.Copy, scale=1.0):
                bank = turns_.wait_filled(act, key)
                act.activation(dst, take(bank), func, scale=scale).then_inc(turns_.moved["act"], 1)

            def four(bank):
                return bank.rearrange("p (i q) -> p i q", i=4)

            def softmax_exp(aa, scale, nk, sums=True):
                b = aa % 2
                act.wait_ge(bias_ready, aa + 1)
                for h in range(HEADS):
                    m = act.activation(probs[:, b, h, 0:nk], scores[:, h, 0:nk], ACT.Exp, bias=softmax_s[:, b, 1, h:h + 1], scale=scale,
                                       accum_out=softmax_s[:, b, 2, h:h + 1] if sums else None)
                m.then_inc(probs_made, 1)

            def squares(key, sources, junk, after=lambda t: None):
                nn = norm_at[key]
                done = sq_due[key] - len(sources)
                for i, src in enumerate(sources):
                    after(i)
                    if done + i:
                        act.wait_ge(squares_summed, done + i)
                    act.activation(junk[:, 0:src.shape[-1]], src, ACT.Square, accum_out=stats[:, nn, i:i + 1]).then_inc(squares_summed, 1)

            def row_squares(key, update):
                squares(key, [x[:, t, :] for t in range(T)], up_sq.rearrange("p b n -> p (b n)"),
                        (lambda t: act.wait_ge(x_updated, update_at[update, t])) if update else (lambda t: act.wait_ge(x_loaded[t], 16)))

            def weight_hi(key, which=range(4)):
                q0, n = first_piece[key]
                arrived(act, key)
                size = width.get(key, PIECE)
                raw = slot_of(place[key])[:, 0:n * size].rearrange("p (i n) -> p i n", n=size)
                for i in (i for i in which if i < n):
                    q = q0 + i
                    if q >= PIECES:
                        act.wait_ge(*piece_done[q - PIECES])
                    act.activation(w_hi[:, q % PIECES, 0:size], raw[:, i, :], ACT.Copy).then_inc(hi_ready, 1)

            def round_part(dst, src, scale=1.0):
                act.activation(dst, src, ACT.Copy, scale=scale).then_inc(rounded, 1)

            def round_turned(name, l, after_first=lambda: None):
                for n, (t, f) in enumerate(turn_order(name)):
                    if n == 2:
                        after_first()
                    bank = small.wait_filled(act, (name, l, t, f))
                    round_part(hT_hi[:, 4 * f:4 * f + 4, t * P:(t + 1) * P], four(bank), 0.5 if name == "mixT" else 1.0)

            act.dma_start(row_gain, a["norm1_g"][0].partition_broadcast(P)).then_inc(first_gain_loaded, 16)
            act.dma_start(pos_i[:, :], a["positions"][0].rearrange("(t p) -> p t", p=P), allow_slow_non_contiguous=True).then_inc(pos_loaded, 16)
            row_squares(("n1", 0), None)
            for l in range(L1):
                if l:
                    row_squares(("n1", l), ("down", l - 1))
                if l:
                    round_turned("n1", l, lambda: weight_hi(("z", l, 0), [0, 1, 2]))
                    weight_hi(("z", l, 0), [3])
                else:
                    round_turned("n1", l)
                    weight_hi(("z", l, 0))
                weight_hi(("z", l, 1))
                if l == 0:
                    act.wait_ge(angles_made, 1)
                    act.activation(rope[:, :, :, :], red[:, :, :, :], ACT.Sin).then_inc(rope_tables, 1)


                def z_out(j):
                    c0, cn = Z_TILES[j]
                    for t in range(T):
                        move(lin, ("z", l, j, t), z[:, t, c0:c0 + cn], lambda b: b[:, 0:cn])

                z_out(0)
                lin.wait_moved(act, ("z", l, 0, 1))
                squares(("mla", l), [z[:, t, 0:MLA_Q] for t in range(T)] + [z[:, t, MLA_Q:MLA_Q + MLA_KV] for t in range(T)], probs[:, 0, 0, :])
                weight_hi(("z", l, 2))
                z_out(1)
                weight_hi(("z", l, 3))
                z_out(2)
                lin.wait_moved(act, ("z", l, 2, 1))
                act.activation(gn, z[:, :, NSA_G:NSA_G + 12], ACT.Tanh, scale=0.5).then_inc(nsa_tanh, 1)
                weight_hi(("z", l, 4))
                z_out(3)
                act.wait_ge(fox_logits, l + 1)
                step(act.activation(lf[:, 1], lf[:, 0], ACT.Abs))
                step.settle()
                step(act.activation(lf[:, 1], lf[:, 1], ACT.Exp, scale=-1.0))
                step.settle()
                act.activation(lf[:, 1], lf[:, 1], ACT.Ln, bias=1.0).then_inc(fox_log, 1)
                for t in range(T):
                    move(lin, ("uq", l, t), mqk[:, t, 0:4, :], lambda b: b[:, 0:384].rearrange("p (h d) -> p h d", h=HEADS))
                    bank = lin.wait_filled(act, ("ukv", l, t)).rearrange("p (h w d) -> p h w d", h=HEADS, w=2)
                    act.activation(mqk[:, t, 4:8, 0:HD], bank[:, :, 0, :], ACT.Copy)
                    act.activation(mv[:, t, :].rearrange("p (h d) -> p h d", h=HEADS), bank[:, :, 1, :], ACT.Copy).then_inc(lin.moved["act"], 1)
                weight_hi(("gate", l, 0))
                z_out(4)
                for w, s in (("foxT", S_FOX_Q), ("nsa", S_NSA_Q), ("idx", S_QI)):
                    for t in range(T):
                        move(small, (w, l, t), attT[:, s:s + 4, t * P:(t + 1) * P], four)

                def gate_out(j):
                    for t in range(T):
                        move(lin, ("gate", l, j, t), gate[:, t, j * BANK:(j + 1) * BANK], func=ACT.Tanh, scale=0.5)

                weight_hi(("gate", l, 1))
                gate_out(0)
                for w, s in (("mq", S_MLA_Q), ("mk", S_MLA_K)):
                    for t in range(T):
                        move(small, (w, l, t), attT[0:MLA_HD, s:s + 4, t * P:(t + 1) * P], lambda b: four(b[0:MLA_HD]))
                for t in range(T):
                    move(small, ("dsa", l, t), attT[:, S_DSA_Q:S_DSA_Q + 4, t * P:(t + 1) * P], four)
                for t in range(T):
                    nk = P * (t + 1)
                    for f in range(4):
                        n = 8 * l + 4 * t + f
                        if n >= 2:
                            act.wait_ge(index_used, n - 1)
                        move(lin, ("idx", l, t, f), relu_l[:, n % 2, :, 0:nk], lambda b: b.rearrange("p (h k) -> p h k", h=2)[:, :, 0:nk],
                             func=ACT.Relu, scale=IDX_DIM ** -0.5 * IDX_HEADS ** -0.5)
                act.wait_ge(index_used, 8 * (l + 1))
                ahead = [(("gate", l, j), i) for j in range(2, GATE_TILES) for i in range(4)] + [(("lift", l, 0), i) for i in range(4)]
                done = 0
                for i, (path, t) in enumerate(PATHS1):
                    aa = att1(l, i)
                    b = aa % 2
                    softmax_exp(aa, SCALE[path], NCMP if path == "cmp" else P * (t + 1), sums=path != "cmp")
                    def pieces_after(n):
                        nonlocal done
                        for key, piece in ahead[done:done + n]:
                            weight_hi(key, [piece])
                        done += n
                        if done % 4 < n:
                            gate_out(done // 4)

                    pieces_after(FILL[i] - 1)
                    if path == "cmp":
                        move(small, ("PT", l, i, 0), PT[0:NCMP, b, 0], lambda bk: four(bk[0:NCMP]))
                    else:
                        for kb in range(t + 1):
                            move(small, ("PT", l, i, kb), PT[:, b, kb], four)
                    pieces_after(1)
                for b in range(4):
                    bank = small.wait_filled(act, ("oT", l, b))
                    round_part(hT_hi[:, 2 * b:2 * b + 2, :], bank.rearrange("p (c q) -> p c q", c=2))
                weight_hi(("lift", l, 1))
                weight_hi(("out", l, 0))
                round_turned("mixT", l)
                weight_hi(("out", l, 1))
                row_squares(("n2", l), ("out", l))
                round_turned("n2", l, lambda: weight_hi(("up", l, 0), [0, 1, 2]))
                weight_hi(("up", l, 0), [3])
                n_up = D_FF // BANK
                for j in range(n_up + 1):
                    if j:
                        for b in range(2):
                            bank = lin.wait_filled(act, ("up", l, j - 1, b))
                            if j > 1:
                                act.wait_ge(split, split_at[("up", l, j - 2, b)])
                            act.activation(up_sq[:, b, :], bank, ACT.Relu).then_inc(relued, 1)
                        for b in range(2):
                            act.wait_ge(made, made_at[("up", l, j - 1, b)])
                            c = 4 * (j - 1) + 2 * b
                            round_part(up_hi[:, c:c + 2, :], up_sq[:, b, :].rearrange("p (c q) -> p c q", c=2))
                    weight_hi(("up", l, j + 1) if j + 1 < n_up else ("down", l, j + 1 - n_up))
                for j in range(2, n_up):
                    for i in range(4):
                        weight_hi(("down", l, j), [i])
                        if j == 2 and l == L1 - 1:
                            round_part(mem_hi[:, i // 2, 4 * (i % 2):4 * (i % 2) + 4, :], four(small.wait_filled(act, ("memT", i // 2, i % 2))))
            row_squares("final", ("down", L1 - 1))

            for l in range(L2):
                weight_hi(("xk", l, 0))
                round_turned("hT", l)
                weight_hi(("cg", l))

                def keys_out(f):
                    for b in (2 * f, 2 * f + 1):
                        move(lin, ("xk", l, b), xkT[:, 2 * b:2 * b + 2, :], lambda bk: bk.rearrange("p (c q) -> p c q", c=2))

                keys_out(0)
                act.wait_ge(pads_zeroed, l + 1)
                move(small, ("alow", l), alT[0:RANK, :], lambda b: b[0:RANK, 0:SEQ])
                weight_hi(("ca", l))
                for t in range(T):
                    move(lin, ("cg", l, t), sg2[:, t, :], func=ACT.Tanh, scale=0.5)
                weight_hi(("qk", l))
                for t in range(T):
                    move(small, ("uT", l, t), uT[:, :, PAD + t * P:PAD + (t + 1) * P], four, scale=0.5)
                for t in range(T):
                    small.wait_moved(act, ("zlow", l, t))
                    step(act.activation(la[:, 1, t, :], la[:, 0, t, :], ACT.Abs))
                    step.settle()
                    step(act.activation(la[:, 1, t, :], la[:, 1, t, :], ACT.Exp, scale=-1.0))
                    step.settle()
                    act.activation(la[:, 1, t, :], la[:, 1, t, :], ACT.Ln, bias=1.0).then_inc(low_log, 1)
                weight_hi(("v", l))
                for t in range(T):
                    move(lin, ("qk", l, t), qk2[:, t, :])
                weight_hi(("r", l))
                for t in range(T):
                    move(lin, ("v", l, t), v2[:, t, :])
                for t in range(T):
                    bank = lin.wait_filled(act, ("bc", l, t))
                    act.activation(ex2[:, 0, t, :], bank[:, 0:GK], ACT.Exp, scale=1 / 16)
                    act.activation(ex2[:, 1, t, :], bank[:, 0:GK], ACT.Exp, scale=-1 / 16)
                    act.activation(ex2[:, 2, t, :], bank[:, GK:], ACT.Exp, scale=1 / 16).then_inc(lin.moved["act"], 1)
                move(small, ("blast", l), dec, lambda b: b[:, 0:8].rearrange("p (g c) -> p g c", g=2), func=ACT.Exp, scale=1 / 16)
                weight_hi(("xk", l, 1), [0, 1])
                for t in range(T):
                    bank = four(small.wait_filled(act, ("qeT", l, t)))
                    act.activation(qeT[:, :, t * P:(t + 1) * P], bank[:, 0:2, :], ACT.Copy)
                    act.activation(keT[:, :, t * P:(t + 1) * P], bank[:, 2:4, :], ACT.Copy)
                    act.activation(qez[:, :, 2 * t, 0:CHUNK], bank[:, 0:2, 0:CHUNK], ACT.Copy)
                    act.activation(qez[:, :, 2 * t + 1, CHUNK:], bank[:, 0:2, CHUNK:], ACT.Copy).then_inc(small.moved["act"], 1)
                weight_hi(("xk", l, 1), [2, 3])
                for t in range(T):
                    bank = lin.wait_filled(act, ("r", l, t))
                    act.activation(sr2[:, t, :], bank, ACT.Tanh, scale=0.5).then_inc(r_tanh, 1)
                weight_hi(("xv", l, 0))
                keys_out(1)

                def mem_values(f):
                    for t in range(T):
                        move(lin, ("xv", l, f, t), xv[:, t, f * BANK:(f + 1) * BANK])

                weight_hi(("xv", l, 1))
                mem_values(0)
                lin.wait_moved(act, ("go", l, 1, 1))
                nn = norm_at[("gla", l)]
                for t in range(T):
                    for h in range(HEADS):
                        act.wait_ge(squares_summed, sq_due[("gla", l)] - T * HEADS + HEADS * t + h)
                        act.activation(gla_junk, go2[:, t, h * P:(h + 1) * P], ACT.Square, accum_out=stats[:, nn, 4 * t + h:4 * t + h + 1]).then_inc(squares_summed, 1)
                act.wait_ge(conv_centred, l + 1)
                act.activation(sq2[:, :, :], acc[:, :, :], ACT.Square).then_inc(conv_squared, 1)
                weight_hi(("mix", l, 0), [0, 1, 2])
                for t in range(T):
                    bank = small.wait_filled(act, ("goT", l, t))
                    round_part(hT_hi[:, 4:8, t * P:(t + 1) * P], four(bank))
                weight_hi(("mix", l, 0), [3])
                mem_values(1)
                act.wait_ge(conv_affine, l + 1)
                act.activation(sq2[:, :, :], acc[:, :, :], ACT.Tanh, scale=0.5).then_inc(conv_tanh, 1)
                weight_hi(("mix", l, 1), [0])
                act.wait_ge(conv_out, l + 1)
                round_part(hT_hi[:, 0:CT, :], acc[:, :, :], 0.5)
                weight_hi(("mix", l, 1), [1, 2, 3])
                round_turned("h1T", l, lambda: weight_hi(("xq", l, 0)))
                weight_hi(("xq", l, 1))
                for b in range(4):
                    if b == 2:
                        weight_hi(("xo", l, 0), [0, 1, 2])
                    move(lin, ("xq", l, b), xqT[:, 2 * b:2 * b + 2, :], lambda bk: bk.rearrange("p (c q) -> p c q", c=2))
                for t in range(T):
                    softmax_exp(att2(l, t), XD ** -0.5, SEQ)
                    if t == 0:
                        weight_hi(("xo", l, 0), [3])
                for t in range(T):
                    b = att2(l, t) % 2
                    for kb in range(T):
                        move(small, ("xPT", l, t, kb), PT[:, b, kb], four)
                    for f in range(2):
                        bank = lin.wait_filled(act, ("xO", l, t, f))
                        round_part(hT_hi[:, 4 * f:4 * f + 4, t * P:(t + 1) * P], four(bank))
                weight_hi(("xo", l, 1))
                round_turned("h2T", l, lambda: weight_hi(("ffn", l, 0)))
                n_ffn, n_ffo = FT2 // 2, -(-FT2 // 4)
                for j in range(n_ffn + 1):
                    if j:
                        for f in (2 * j - 2, 2 * j - 1):
                            bank = lin.wait_filled(act, ("ffn", l, f))
                            act.activation(ffs[:, f % 2, :], bank[:, 0:SEQ], ACT.Tanh, scale=0.5).then_inc(ff_tanh, 1)
                        for f in (2 * j - 2, 2 * j - 1):
                            lin.wait_moved(act, ("ffn", l, f))
                            round_part(ff_hi[:, f, :], ffp[:, f % 2, :])
                    weight_hi(("ffn", l, j + 1) if j + 1 < n_ffn else ("ffo", l, j + 1 - n_ffn))
                for j in range(2, n_ffo):
                    weight_hi(("ffo", l, j))

        @block.vector
        def _(dve):
            step = Chain(dve, dve_step)

            def moved(ins, turns_):
                ins.then_inc(turns_.moved["dve"], 1)

            def four(bank):
                return bank.rearrange("p (i q) -> p i q", i=4)

            def norm_mean(key, parts):
                nn = norm_at[key]
                dve.wait_ge(squares_summed, sq_due[key])
                for i, (src, dst, n, eps) in enumerate(parts):
                    m = dve.tensor_scalar(stats[:, nn, dst], stats[:, nn, src], 1.0 / n, eps, ALU.mult, ALU.add)
                m.then_inc(mean_ready, 1)
                dve.wait_ge(rstd_ready, root_at[key, 0])
                return nn

            def rms_root(key, t):
                nn = norm_at[key]
                dve.wait_ge(squares_summed, sq_due[key] - T + t + 1)
                dve.tensor_scalar(stats[:, nn, 8 + t:9 + t], stats[:, nn, t:t + 1], 1.0 / D, NORM_EPS, ALU.mult, ALU.add).then_inc(mean_ready, 1)
                dve.wait_ge(rstd_ready, root_at[key, t])
                return stats[:, nn, 12 + t:13 + t]

            def rms_rows(key, t):
                root = rms_root(key, t)
                dve.wait_ge(*gain_due[key])
                dve.scalar_tensor_tensor(out=hn[:, t, :], in0=x[:, t, :], scalar=root, in1=row_gain, op0=ALU.mult, op1=ALU.mult).then_inc(normed, 1)

            def rms_sum(name, key, l):
                for t in range(T):
                    for f in range(2):
                        bank = lin.wait_filled(dve, (name, l, t, f))
                        xv_ = x[:, t, f * BANK:(f + 1) * BANK]
                        moved(dve.tensor_tensor(xv_, bank, xv_, ALU.add), lin)
                    lin.wait_moved(dve, (name, l, t, 1))
                    dve.sem_inc(x_updated, 1)
                    if key:
                        rms_rows(key, t)

            def weight_lo(key, which=range(4)):
                q0, n = first_piece[key]
                size = width.get(key, PIECE)
                raw = slot_of(place[key])[:, 0:n * size].rearrange("p (i n) -> p i n", n=size)
                for i in which:
                    if i < n:
                        q = q0 + i
                        dve.wait_ge(hi_ready, q + 1)
                        dve.tensor_tensor(w_lo[:, q % PIECES, 0:size], raw[:, i, :], w_hi[:, q % PIECES, 0:size], ALU.subtract).then_inc(lo_ready["dve"], 1)

            def rest_part(key, dst, src, hi):
                dve.wait_ge(rounded, part_at[key])
                return dve.tensor_tensor(dst, src, hi, ALU.subtract).then_inc(split, 1)

            def rest_bank(turns_, key, dst, hi, take=four, scale=None):
                dve.wait_ge(rounded, part_at[key])
                src = take(turns_.bank(key))
                if scale is None:
                    moved(dve.tensor_tensor(dst, src, hi, ALU.subtract), turns_)
                else:
                    moved(dve.scalar_tensor_tensor(out=dst, in0=src, scalar=scale, in1=hi, op0=ALU.mult, op1=ALU.subtract), turns_)

            def rest_turned(name, l, lo):
                for t, f in turn_order(name):
                    q = slice(t * P, (t + 1) * P)
                    k = slice(4 * f, 4 * f + 4)
                    rest_bank(small, (name, l, t, f), lo[:, t, k, :] if name == "n1" else lo[:, k, q], hT_hi[:, k, q], scale=0.5 if name == "mixT" else None)

            def softmax_bias(aa, nk, scale, bias=None, k0=0):
                b = aa % 2
                dve.wait_ge(scores_filled, aa + 1)
                if bias is not None:
                    step(dve.tensor_tensor(scores[:, :, k0:nk], scores[:, :, k0:nk], bias, ALU.add))
                    step.settle()
                step(dve.tensor_reduce(softmax_s[:, b, 0, :], scores[:, :, 0:nk], AX, ALU.max, negate=True))
                step.settle()
                dve.tensor_scalar(softmax_s[:, b, 1, :], softmax_s[:, b, 0, :], scale, None, ALU.mult).then_inc(bias_ready, 1)

            def heads(v, n):
                return v.unsqueeze(1).to_broadcast([P, HEADS, n])

            def take_top(t):
                nk = P * (t + 1)
                s = index_bias[t]
                for _ in range(KEEP // 8):
                    step(dve.max(best, s))
                    step.settle()
                    step(dve.match_replace(s, best, s, TAKEN))
                    step.settle()
                step(dve.tensor_scalar(s, s, TAKEN / 2, MASKED, ALU.is_gt, ALU.mult))
                step.settle()
                step(dve.tensor_tensor(s, s, causal[:, SEQ - nk:SEQ], ALU.min))
                step.settle()

            for t in range(T):
                rms_rows(("n1", 0), t)
            rest_turned("n1", 0, hn_lo)
            weight_lo(("z", 0, 0))
            dve.wait_ge(pos_loaded, 16)
            dve.wait_ge(consts_made, 1)
            step(dve.tensor_copy(pos_f[:, :], pos_i[:, :]))
            step.settle()
            for t in range(T):
                step(dve.tensor_scalar(ang[:, t, :], freq[:, :], pos_f[:, t:t + 1], None, ALU.mult))
            step.settle()
            for s, quarter in ((0, 0.0), (1, 0.25)):
                step(dve.tensor_scalar(turns[:, s], ang[:, :, :], 1 / (2 * np.pi), quarter, ALU.mult, ALU.add))
            step.settle()
            step(dve.tensor_scalar(turns[:, :], turns[:, :], ROUND, None, ALU.add))
            step.settle()
            step(dve.tensor_scalar(turns[:, :], turns[:, :], -ROUND, None, ALU.add))
            step.settle()
            for s in range(2):
                step(dve.scalar_tensor_tensor(out=red[:, s], in0=turns[:, s], scalar=-TWO_PI[0], in1=ang[:, :, :], op0=ALU.mult, op1=ALU.add))
            for part in TWO_PI[1:]:
                step.settle()
                step(dve.scalar_tensor_tensor(out=red[:, :], in0=turns[:, :], scalar=-part, in1=red[:, :], op0=ALU.mult, op1=ALU.add))
            step.settle()
            step(dve.tensor_scalar(red[:, 1], red[:, 1], np.pi / 2, None, ALU.add))
            step.settle()
            dve.tensor_scalar(red[:, :], red[:, :], PI_BELOW, -PI_BELOW, ALU.min, ALU.max).then_inc(angles_made, 1)

            dve.wait_ge(params_loaded, 16 * 5 * LAYERS)
            for l in range(L1):
                if l:
                    rest_turned("n1", l, hn_lo)
                weight_lo(("z", l, 1))
                nn = norm_mean(("mla", l), [(slice(0, 2), slice(8, 10), MLA_Q, NORM_EPS), (slice(2, 4), slice(10, 12), MLA_KV, NORM_EPS)])
                for t in range(T):
                    dve.tensor_scalar(z[:, t, 0:MLA_Q], z[:, t, 0:MLA_Q], stats[:, nn, 12 + t:13 + t], None, ALU.mult)
                    dve.tensor_scalar(z[:, t, MLA_Q:MLA_Q + MLA_KV], z[:, t, MLA_Q:MLA_Q + MLA_KV], stats[:, nn, 14 + t:15 + t], None, ALU.mult).then_inc(normed, 1)
                weight_lo(("z", l, 2))
                weight_lo(("z", l, 3))
                for t in range(T):
                    bank = small.wait_filled(dve, ("cT", l, t))[:, 0:3 * P].rearrange("p (i q) -> p i q", i=3)
                    moved(dve.tensor_tensor(cT[:, :, t * P:(t + 1) * P], bank, gqkv[:, l, :].unsqueeze(2).to_broadcast([P, 3, P]), ALU.mult), small)
                weight_lo(("z", l, 4))
                lin.wait_moved(dve, ("z", l, 3, 1))
                dve.tensor_tensor(lf[:, 0], z[:, :, FOX_F:FOX_F + HEADS], fbias[:, l, :].unsqueeze(1).to_broadcast([P, T, HEADS]), ALU.add).then_inc(fox_logits, 1)
                dve.wait_ge(nsa_tanh, l + 1)
                step(dve.tensor_scalar(gn, gn, 0.5, 0.5, ALU.mult, ALU.add))
                dve.wait_ge(fox_log, l + 1)
                step(dve.scalar_tensor_tensor(out=lf[:, 2], in0=lf[:, 0], scalar=0.0, in1=lf[:, 1], op0=ALU.min, op1=ALU.subtract))
                step.settle()
                for s, w in ((0, SEQ), (1, P)):
                    for i, h in enumerate(BY_SLOT):
                        m = dve.tensor_scalar(decay_rows[s][:, i, :], upto[:, 0:w], lf[:, 2, s, h:h + 1], -(HD ** 0.5), ALU.mult, ALU.mult)
                m.then_inc(decay_ready, 1)
                weight_lo(("gate", l, 0))
                bank = small.wait_filled(dve, ("cq", l))
                moved(dve.tensor_scalar(cq8, bank[:, 0:8].rearrange("p (t h) -> p t h", t=T), HD ** 0.5, None, ALU.mult), small)
                small.wait_moved(dve, ("cq", l))
                for f in range(2):
                    bank = lin.wait_filled(dve, ("ck", l, f)).rearrange("p (h k) -> p h k", h=2)
                    for i in range(2):
                        h = BY_SLOT[2 * f + i]
                        for t in range(T):
                            nk = P * (t + 1)
                            m = dve.scalar_tensor_tensor(out=d8[t][:, 2 * f + i, :], in0=bank[:, i, 0:nk], scalar=cq8[:, t, h:h + 1],
                                                         in1=causal[:, SEQ - nk:SEQ], op0=ALU.add, op1=ALU.add)
                    moved(m, lin)
                small.wait_moved(dve, ("idx", l, 1))
                for w, s in enumerate((S_KC, S_VC)):
                    for e in range(2):
                        r = slice(HD * e, HD * (e + 1))
                        src = attT[r, s, :].rearrange("p (c i e) -> p i c e", i=8, e=2)
                        for i1 in range(2):
                            m = dve.tensor_tensor(cmpR[r, w, 8 * i1:8 * i1 + 8, :], src[:, :, i1:i1 + NCMP, e],
                                                  peT[r, l, w, 8 * i1:8 * i1 + 8].unsqueeze(2).to_broadcast([HD, 8, NCMP]), ALU.add)
                m.then_inc(cmp_rows, 1)
                weight_lo(("gate", l, 1))
                bank = small.wait_filled(dve, ("comp", l))
                dve.tensor_copy(kcmpT, bank[:, 0:NCMP])
                moved(dve.tensor_copy(vcmp[0:NCMP], bank[0:NCMP, 64:64 + HD]), small)
                for t in range(T):
                    nk = P * (t + 1)
                    for f in range(4):
                        n = 8 * l + 4 * t + f
                        lin.wait_moved(dve, ("idx", l, t, f))
                        for i in range(2):
                            h = f + 4 * i
                            w = z[:, t, DSA_W + h:DSA_W + h + 1]
                            if h == 0:
                                step(dve.tensor_scalar(index_bias[t], relu_l[:, n % 2, i, 0:nk], w, None, ALU.mult))
                            else:
                                m = dve.scalar_tensor_tensor(out=index_bias[t], in0=relu_l[:, n % 2, i, 0:nk], scalar=w, in1=index_bias[t], op0=ALU.mult, op1=ALU.add)
                                if i == 0:
                                    step(m)
                                else:
                                    m.then_inc(index_used, 1)
                            if i == 0:
                                step.settle()
                        dve.wait_ge(index_used, n + 1)
                    step(dve.tensor_tensor(index_bias[t], index_bias[t], causal[:, SEQ - nk:SEQ], ALU.add))
                    step.settle()

                def path_bias(i):
                    path, t = PATHS1[i]
                    aa = att1(l, i)
                    nk = NCMP if path == "cmp" else P * (t + 1)
                    if path == "fox":
                        softmax_bias(aa, nk, SCALE[path], d8[t])
                    elif path == "dsa":
                        softmax_bias(aa, nk, SCALE[path], heads(index_bias[t], nk))
                    elif path == "cmp":
                        softmax_bias(aa, nk, SCALE[path], heads(cmp_bias[:, t, :], NCMP))
                    else:
                        softmax_bias(aa, nk, SCALE[path], heads(causal[:, P:SEQ], P), t * P)

                seen = set()
                path_bias(0)
                for i, (path, t) in enumerate(PATHS1):
                    aa = att1(l, i)
                    b = aa % 2
                    if i in (2, 4):
                        take_top(i // 2 - 1)
                    dve.wait_ge(probs_made, aa + 1)
                    total, weight = softmax_s[:, b, 2, :], softmax_s[:, b, 3, :]
                    if path == "cmp":
                        dve.tensor_tensor(probs[:, b, :, 0:NCMP], probs[:, b, :, 0:NCMP], heads(cmp_keep[:, t, :], NCMP), ALU.mult).then_inc(probs_final, 1)
                        dve.wait_ge(probs_final, cmp_final(l, t))
                        step(dve.tensor_reduce(total, probs[:, b, :, 0:NCMP], AX, ALU.add))
                        step.settle()
                        step(dve.tensor_scalar(total, total, 1e-30, None, ALU.max))
                        step.settle()
                    step(dve.reciprocal(weight, total))
                    if BRANCH[path] == 1:
                        g0 = HEADS * ("cmp", "sel", "win").index(path)
                        step.settle()
                        step(dve.tensor_tensor(weight.rearrange("p (e i) -> p e i", e=2), weight.rearrange("p (e i) -> p e i", e=2),
                                               gn[:, t, g0:g0 + HEADS].rearrange("p (i e) -> p e i", e=2), ALU.mult))
                    step.settle()
                    if i + 1 < NP1:
                        path_bias(i + 1)
                    bank = small.wait_filled(dve, ("PV", l, i))[:, 0:HEADS * HD].rearrange("p (i e d) -> p i e d", i=2, e=2)
                    dst = osb[BRANCH[path]][:, t].rearrange("p (i e) d -> p i e d", e=2)
                    wide = weight.rearrange("p (e i) -> p i e", e=2).unsqueeze(3).to_broadcast([P, 2, 2, HD])
                    if (BRANCH[path], t) in seen:
                        moved(dve.tensor_tensor(otmp.rearrange("p (i e) d -> p i e d", e=2), bank, wide, ALU.mult), small)
                        small.wait_moved(dve, ("PV", l, i))
                        step(dve.tensor_tensor(osb[BRANCH[path]][:, t], osb[BRANCH[path]][:, t], otmp, ALU.add))
                    else:
                        moved(dve.tensor_tensor(dst, bank, wide, ALU.mult), small)
                    seen.add((BRANCH[path], t))
                for b in range(4):
                    rest_bank(small, ("oT", l, b), hT_lo2[:, 2 * b:2 * b + 2, :], hT_hi[:, 2 * b:2 * b + 2, :], lambda bk: bk.rearrange("p (c q) -> p c q", c=2))
                for f in range(2):
                    for b in range(4):
                        if f == 0:
                            weight_lo(("lift", l, 1), [b])
                        for t in range(T):
                            gv = gate[:, t, b * D + f * BANK:b * D + (f + 1) * BANK]
                            bank = lin.wait_filled(dve, ("lift", l, f, b, t))
                            moved(dve.scalar_tensor_tensor(out=gv, in0=gv, scalar=1.0, in1=bank, op0=ALU.add, op1=ALU.mult), lin)
                        if f == 1:
                            weight_lo(("out", l, 0), [b])
                rest_turned("mixT", l, hT_lo2)
                weight_lo(("out", l, 1))
                rms_sum("out", ("n2", l), l)
                rest_turned("n2", l, hT_lo)
                n_up = D_FF // BANK
                for j in range(n_up + 1):
                    if j:
                        for b in range(2):
                            key = ("up", l, j - 1, b)
                            bank = lin.wait_filled(dve, key)
                            dve.wait_ge(relued, 2 * (n_up * l + j - 1) + b + 1)
                            dve.tensor_tensor(up_sq[:, b, :], up_sq[:, b, :], bank, ALU.mult).then_inc(made, 1)
                            dve.wait_ge(made, made_at[key])
                            dve.sem_inc(lin.moved["dve"], 1)
                        for b in range(2):
                            c = 4 * (j - 1) + 2 * b
                            rest_part(("up", l, j - 1, b), up_lo[:, c:c + 2, :], up_sq[:, b, :].rearrange("p (c q) -> p c q", c=2), up_hi[:, c:c + 2, :])
                    weight_lo(("up", l, j + 1) if j + 1 < n_up else ("down", l, j + 1 - n_up))
                for j in range(2, n_up):
                    for i in range(4):
                        weight_lo(("down", l, j), [i])
                        if j == 2 and l == L1 - 1:
                            t, k = i // 2, slice(4 * (i % 2), 4 * (i % 2) + 4)
                            rest_bank(small, ("memT", t, i % 2), mem_lo[:, t, k, :], mem_hi[:, t, k, :])
                rms_sum("down", ("n1", l + 1) if l + 1 < L1 else None, l)

            def row_stats(t, f):
                step(dve.bn_stats(halves[:, t, f, :], x[:, t, f * BANK:(f + 1) * BANK]))

            def norm_rows(key, t):
                nn = norm_at[key]
                step.settle()
                step(dve.bn_aggr(stats[:, nn, 2 * t:2 * t + 2], halves[:, t, :, :]))
                step.settle()
                dve.tensor_scalar(stats[:, nn, 8 + t:9 + t], stats[:, nn, 2 * t + 1:2 * t + 2], LN_EPS, None, ALU.add).then_inc(mean_ready, 1)
                b = gains.index(key) % 2
                dve.wait_ge(lng_loaded[b], gains_due[key])
                step(dve.scalar_tensor_tensor(out=x[:, t, :], in0=x[:, t, :], scalar=stats[:, nn, 2 * t:2 * t + 1], in1=lng[:, b, 0, :], op0=ALU.subtract, op1=ALU.mult))
                step.settle()
                dve.wait_ge(rstd_ready, root_at[key, t])
                step(dve.scalar_tensor_tensor(out=x[:, t, :], in0=x[:, t, :], scalar=stats[:, nn, 12 + t:13 + t], in1=lng[:, b, 1, :], op0=ALU.mult, op1=ALU.add))
                step.settle()
                dve.sem_inc(x_updated, 1)

            for t in range(T):
                root = rms_root("final", t)
                dve.wait_ge(lng_loaded[0], gains_due["final"])
                step(dve.scalar_tensor_tensor(out=x[:, t, :], in0=x[:, t, :], scalar=root, in1=lng[:, 0, 0, :], op0=ALU.mult, op1=ALU.mult))
                step.settle()
                dve.sem_inc(x_updated, 1)
                for f in range(2):
                    row_stats(t, f)
                norm_rows("ln0", t)

            def residual_norm(name, key, l):
                for t in range(T):
                    for f in range(2):
                        bank = lin.wait_filled(dve, (name, l, t, f))
                        xv_ = x[:, t, f * BANK:(f + 1) * BANK]
                        moved(dve.scalar_tensor_tensor(out=xv_, in0=xv_, scalar=ALPHA, in1=bank, op0=ALU.mult, op1=ALU.add), lin)
                        lin.wait_moved(dve, (name, l, t, f))
                        row_stats(t, f)
                    norm_rows((key, l), t)

            def conv_taps(l, taps):
                for j in taps:
                    for c in range(CT):
                        src, w = uT[:, c, j:j + SEQ], conv_wT[:, l, c, j:j + 1]
                        if j == 0:
                            step(dve.tensor_scalar(acc[:, c, :], src, w, conv_p[:, 0, l, c:c + 1], ALU.mult, ALU.add))
                        else:
                            step.settle(CT - 1)
                            step(dve.scalar_tensor_tensor(out=acc[:, c, :], in0=src, scalar=w, in1=acc[:, c, :], op0=ALU.mult, op1=ALU.add))

            dve.wait_ge(params2_loaded, 16 * (CT + 6) * LAYERS)
            for l in range(L2):
                rest_turned("hT", l, hT_lo3)
                weight_lo(("cg", l))
                weight_lo(("ca", l))
                weight_lo(("qk", l), [0, 1, 2])
                for t in range(T):
                    lin.wait_moved(dve, ("cg", l, t))
                    bank = lin.wait_filled(dve, ("ca", l, t))
                    moved(dve.scalar_tensor_tensor(out=u2[:, t, :], in0=sg2[:, t, :], scalar=1.0, in1=bank, op0=ALU.add, op1=ALU.mult), lin)
                weight_lo(("qk", l), [3])
                for t in range(T):
                    bank = small.wait_filled(dve, ("zlow", l, t))
                    moved(dve.tensor_copy(la[:, 0, t, :], bank[:, 0:GK]), small)
                small.wait_moved(dve, ("uT", l, 1))
                conv_taps(l, range(5))
                for t in range(T):
                    dve.wait_ge(low_log, T * l + t + 1)
                    dve.scalar_tensor_tensor(out=la[:, 0, t, :], in0=la[:, 0, t, :], scalar=0.0, in1=la[:, 1, t, :], op0=ALU.min, op1=ALU.subtract).then_inc(la_ready, 1)
                conv_taps(l, range(5, 10))
                for t in range(T):
                    lin.wait_moved(dve, ("bc", l, t))
                    dve.scalar_tensor_tensor(out=ex2[:, 0, t, :], in0=qk2[:, t, 0:GK], scalar=HD ** -0.5, in1=ex2[:, 0, t, :], op0=ALU.mult, op1=ALU.mult)
                    dve.tensor_tensor(ex2[:, 1, t, :], qk2[:, t, GK:], ex2[:, 1, t, :], ALU.mult)
                    dve.tensor_tensor(ex2[:, 2, t, :], qk2[:, t, GK:], ex2[:, 2, t, :], ALU.mult).then_inc(qkd_ready, 1)
                conv_taps(l, range(10, 15))
                for t in range(T):
                    dve.wait_ge(r_tanh, T * l + t + 1)
                    bank = lin.wait_filled(dve, ("r", l, t))
                    moved(dve.scalar_tensor_tensor(out=sr2[:, t, :], in0=sr2[:, t, :], scalar=1.0, in1=bank, op0=ALU.add, op1=ALU.mult), lin)
                dve.wait_ge(pads_zeroed, l + 1)
                for t in range(T):
                    for e in range(2):
                        bank = lin.wait_filled(dve, ("att", l, t, e))[:, 0:2 * P].rearrange("p (g c) -> p g c", g=2)
                        moved(dve.copy_predicated(gattT[:, t, :, :].rearrange("p (g e) c -> p g e c", e=2)[:, :, e, :],
                                                  blk_upto[:, :].unsqueeze(1).to_broadcast([P, 2, P]).bitcast(I32), bank), lin)
                small.wait_moved(dve, ("blast", l))
                for c in range(3):
                    bank = lin.wait_filled(dve, ("upd", l, c)).rearrange("p (g e n) -> p g e n", g=2, e=2)
                    for e in range(2):
                        r = slice(HD * e, HD * (e + 1))
                        if c == 0:
                            m = dve.tensor_copy(state[r, c, :, :], bank[r, :, e, :])
                        else:
                            for g in range(2):
                                m = dve.scalar_tensor_tensor(out=state[r, c, g, :], in0=state[r, c - 1, g, :], scalar=dec[r, g, c:c + 1], in1=bank[r, g, e, :], op0=ALU.mult, op1=ALU.add)
                    moved(m, lin)
                    lin.wait_moved(dve, ("upd", l, c))
                conv_taps(l, range(15, TAPS))
                step.settle()
                dve.sem_inc(conv_summed, 1)
                for t in range(T):
                    for e in range(2):
                        bank = lin.wait_filled(dve, ("go", l, t, e))[:, 0:2 * P].rearrange("p (g n) -> p g n", g=2)
                        moved(dve.tensor_copy(go2[:, t, :].rearrange("p (g e n) -> p g e n", g=2, e=2)[:, :, e, :], bank), lin)

                def channels(v):
                    return v.unsqueeze(1).to_broadcast([P, CT, SEQ])

                bank = small.wait_filled(dve, ("cmean", l))
                moved(dve.tensor_scalar(mean_c, bank[:, 0:SEQ], 1.0 / CONV, None, ALU.mult), small)
                small.wait_moved(dve, ("cmean", l))
                dve.tensor_tensor(acc[:, :, :], acc[:, :, :], channels(mean_c), ALU.subtract).then_inc(conv_centred, 1)
                nn = norm_mean(("gla", l), [(slice(0, 8), slice(0, 8), P, LN_EPS)])
                for t in range(T):
                    v = four(go2[:, t, :])
                    step(dve.tensor_tensor(v, v, stats[:, nn, 8 + 4 * t:12 + 4 * t].unsqueeze(2).to_broadcast([P, HEADS, P]), ALU.mult))
                    step.settle()
                    step(dve.tensor_tensor(v, v, heads(gla_g[:, l, :], P), ALU.mult))
                    step.settle()
                    dve.scalar_tensor_tensor(out=go2[:, t, :], in0=go2[:, t, :], scalar=0.5, in1=sr2[:, t, :], op0=ALU.mult, op1=ALU.mult).then_inc(go_ready, 1)
                bank = small.wait_filled(dve, ("cvar", l))
                nn = norm_at[("conv", l)]
                moved(dve.tensor_scalar(stats[:, nn, 8:10], bank[:, 0:2], 1.0 / CONV, LN_EPS, ALU.mult, ALU.add), small)
                small.wait_moved(dve, ("cvar", l))
                dve.sem_inc(mean_ready, 1)
                dve.wait_ge(rstd_ready, root_at[("conv", l), 0])
                for t in range(T):
                    m = dve.tensor_scalar(root_diag[:, t, :], ident[:, :], stats[:, nn, 12 + t:13 + t], None, ALU.mult)
                m.then_inc(root_spread, 1)
                for t in range(T):
                    rest_bank(small, ("goT", l, t), hT_lo2[:, 4:8, t * P:(t + 1) * P], hT_hi[:, 4:8, t * P:(t + 1) * P])
                bank = small.wait_filled(dve, ("crstd", l))
                dve.wait_ge(conv_squared, l + 1)
                moved(dve.tensor_tensor(acc[:, :, :], acc[:, :, :], channels(bank[:, 0:SEQ]), ALU.mult), small)
                small.wait_moved(dve, ("crstd", l))
                for c in range(CT):
                    m = dve.tensor_scalar(acc[:, c, :], acc[:, c, :], conv_p[:, 1, l, c:c + 1], conv_p[:, 2, l, c:c + 1], ALU.mult, ALU.add)
                m.then_inc(conv_affine, 1)
                dve.wait_ge(conv_tanh, l + 1)
                dve.scalar_tensor_tensor(out=acc[:, :, :], in0=sq2[:, :, :], scalar=1.0, in1=acc[:, :, :], op0=ALU.add, op1=ALU.mult).then_inc(conv_out, 1)
                dve.wait_ge(rounded, part_at[("conv", l)])
                dve.scalar_tensor_tensor(out=hT_lo2[:, 0:CT, :], in0=acc[:, :, :], scalar=0.5, in1=hT_hi[:, 0:CT, :], op0=ALU.mult, op1=ALU.subtract).then_inc(split, 1)
                residual_norm("mix", "ln1", l)
                rest_turned("h1T", l, hT_lo2)
                weight_lo(("xq", l, 1))
                weight_lo(("xo", l, 0), [0, 1, 2])
                for t in range(T):
                    softmax_bias(att2(l, t), SEQ, XD ** -0.5)
                weight_lo(("xo", l, 0), [3])
                for t in range(T):
                    aa = att2(l, t)
                    b = aa % 2
                    dve.wait_ge(probs_made, aa + 1)
                    step(dve.reciprocal(softmax_s[:, b, 3, :], softmax_s[:, b, 2, :]))
                    step.settle()
                    dve.tensor_tensor(probs[:, b], probs[:, b], softmax_s[:, b, 3, :].unsqueeze(2).to_broadcast([P, XH, SEQ]), ALU.mult).then_inc(probs_final, 1)
                for t in range(T):
                    for f in range(2):
                        k, q = slice(4 * f, 4 * f + 4), slice(t * P, (t + 1) * P)
                        rest_bank(lin, ("xO", l, t, f), hT_lo2[:, k, q], hT_hi[:, k, q])
                weight_lo(("xo", l, 1))
                residual_norm("xo", "ln2", l)
                rest_turned("h2T", l, hT_lo)
                n_ffn, n_ffo = FT2 // 2, -(-FT2 // 4)
                for j in range(n_ffn + 1):
                    if j:
                        for f in (2 * j - 2, 2 * j - 1):
                            dve.wait_ge(ff_tanh, FT2 * l + f + 1)
                            bank = lin.wait_filled(dve, ("ffn", l, f))
                            step(dve.scalar_tensor_tensor(out=ffs[:, f % 2, :], in0=ffs[:, f % 2, :], scalar=1.0, in1=bank[:, 0:SEQ], op0=ALU.add, op1=ALU.mult))
                            step.settle()
                            if f >= 2:
                                dve.wait_ge(split, split_at[("ffn", l, f - 2)])
                            moved(dve.scalar_tensor_tensor(out=ffp[:, f % 2, :], in0=ffs[:, f % 2, :], scalar=0.5, in1=bank[:, SEQ:], op0=ALU.mult, op1=ALU.mult), lin)
                        for f in (2 * j - 2, 2 * j - 1):
                            rest_part(("ffn", l, f), ff_lo[:, f, :], ffp[:, f % 2, :], ff_hi[:, f, :])
                    weight_lo(("ffn", l, j + 1) if j + 1 < n_ffn else ("ffo", l, j + 1 - n_ffn))
                for j in range(2, n_ffo):
                    weight_lo(("ffo", l, j))
                residual_norm("ffo", "ln3", l)

        @block.gpsimd
        def _(pool):
            step = Chain(pool, pool_step)

            def select(v, keep, fill, base, per_row, per_column):
                step.settle()
                step(pool.affine_select(out=v, in_=v, pattern=[[per_column, v.shape[-1]]], compare_op=keep, fill=fill, base=base, channel_multiplier=per_row))

            def weight_rest(key, which=range(4)):
                q0, n = first_piece[key]
                size = width.get(key, PIECE)
                raw = slot_of(place[key])[:, 0:n * size].rearrange("p (i n) -> p i n", n=size)
                for i in which:
                    q = q0 + i
                    pool.wait_ge(hi_ready, q + 1)
                    pool.tensor_tensor(w_lo[:, q % PIECES, 0:size], raw[:, i, :], w_hi[:, q % PIECES, 0:size], ALU.subtract).then_inc(lo_ready["pool"], 1)

            def root_rows(key):
                for t in range(T):
                    root(key, slice(8 + t, 9 + t), slice(12 + t, 13 + t), t)

            def root(key, src=slice(8, 10), dst=slice(12, 14), t=0):
                nn = norm_at[key]
                pool.wait_ge(mean_ready, root_at[key, t])
                n = src.stop - src.start
                pool.tensor_tensor(stats[:, nn, dst], stats[:, nn, src], minus_half[:, 0:1].to_broadcast([P, n]), ALU.pow).then_inc(rstd_ready, 1)

            def rotate(v, kind):
                first, half = kind
                n = v.shape[2]
                shape = [P, T, n, half]
                sin = rope[:, 0, :, first:first + half].unsqueeze(2).to_broadcast(shape)
                cos = rope[:, 1, :, first:first + half].unsqueeze(2).to_broadcast(shape)
                tmp = [rope_tmp[:, s, 0:T * n * half].rearrange("p (t h d) -> p t h d", t=T, h=n) for s in range(4)]
                x1, x2 = v[:, :, :, 0:half], v[:, :, :, half:2 * half]
                for dst, src, table in zip(tmp, (x1, x2, x2, x1), (cos, sin, cos, sin)):
                    step(pool.tensor_tensor(dst, src, table, ALU.mult))
                step.settle()
                step(pool.tensor_tensor(x1, tmp[0], tmp[1], ALU.subtract))
                step(pool.tensor_tensor(x2, tmp[2], tmp[3], ALU.add))
                step.settle()

            def by_head(c0, n, d):
                return z[:, :, c0:c0 + n * d].rearrange("p t (h d) -> p t h d", d=d)

            MLA_ROPE, HEAD_ROPE, IDX_ROPE = ROPES
            step(pool.memset(minus_half[:, :], -0.5))
            step(pool.memset(ident[:, :], 0.0))
            select(ident[:, :], ALU.not_equal, 1.0, 0, 1, -1)
            step.settle()
            pool.sem_inc(ident_made, 1)
            root_rows(("n1", 0))
            for v, value in ((causal[:, :], 0.0), (upto[:, :], 1.0), (cmp_bias[:, :, :], 0.0), (cmp_keep[:, :, :], 1.0),
                             (blk_upto[:, :], 1.0), (blk_after[:, :], 1.0), (blk_sum[:, :], 1.0)):
                step(pool.memset(v, value))
            for first, half in ROPES:
                for i in range(half):
                    step(pool.memset(freq[:, first + i:first + i + 1], float(np.float32(THETA) ** (-np.float32(i) / np.float32(half)))))
            select(causal[:, P:SEQ], ALU.is_ge, MASKED, 0, 1, -1)
            select(upto[:, 0:P], ALU.is_ge, 0.0, 0, -1, 1)
            for t in range(T):
                select(cmp_bias[:, t, :], ALU.is_ge, MASKED, P * t - (CMP_LEN - 1), 1, -CMP_STRIDE)
                select(cmp_keep[:, t, :], ALU.is_ge, 0.0, P * t - (CMP_LEN - 1), 1, -CMP_STRIDE)
            select(blk_upto[:, :], ALU.is_ge, 0.0, 0, -1, 1)
            select(blk_upto[:, CHUNK:], ALU.is_ge, 0.0, -CHUNK, 1, 0)
            select(blk_after[:, :], ALU.is_ge, 0.0, -1, 1, -1)
            select(blk_after[:, 0:CHUNK], ALU.is_ge, 0.0, CHUNK - 1, -1, 0)
            select(blk_sum[:, 0:1], ALU.is_ge, 0.0, CHUNK - 1, -1, 0)
            select(blk_sum[:, 1:2], ALU.is_ge, 0.0, -CHUNK, 1, 0)
            step.settle()
            pool.sem_inc(consts_made, 1)

            for l in range(L1):
                if l:
                    root_rows(("n1", l))
                    weight_rest(("z", l, 0))
                root(("mla", l), slice(8, 12), slice(12, 16))
                if l == 0:
                    pool.wait_ge(rope_tables, 1)
                lin.wait_moved(pool, ("z", l, 2, 1))
                rotate(by_head(MLA_Q + MLA_KV, 1, MLA_R), MLA_ROPE)
                rotate(by_head(NSA_Q, 4, HD), HEAD_ROPE)
                rotate(by_head(NSA_KC, 3, 2 * HD), HEAD_ROPE)
                for t in range(T):
                    step(pool.tensor_copy(stage[:, t, 0:2, :].rearrange("p w (r d) -> p w r d", r=2),
                                          z[:, t, NSA_KS:NSA_KS + 4 * HD].rearrange("p (w d) -> p w d", w=2)[:, :, 0:HD].unsqueeze(2).to_broadcast([P, 2, 2, HD])))
                    step(pool.tensor_copy(stage[:, t, 4:6, :].rearrange("p w (r d) -> p w r d", r=2),
                                          z[:, t, NSA_KC:NSA_KC + 2 * HD].rearrange("p (w d) -> p w d", w=2).unsqueeze(2).to_broadcast([P, 2, 2, HD])))
                lin.wait_moved(pool, ("ukv", l, 1))
                rotate(mqk[:, :, 0:HEADS, HD:MLA_HD], MLA_ROPE)
                for t in range(T):
                    m = pool.tensor_copy(mqk[:, t, HEADS:2 * HEADS, HD:MLA_HD], z[:, t, MLA_Q + MLA_KV:NSA0].unsqueeze(1).to_broadcast([P, HEADS, MLA_R]))
                    if t == 0:
                        step(m)
                m.then_inc(mla_roped, 1)
                lin.wait_moved(pool, ("z", l, 4, 1))
                rotate(by_head(DSA_Q, 5, HD), HEAD_ROPE)
                rotate(by_head(DSA_QI, IDX_HEADS + 1, IDX_DIM), IDX_ROPE)
                for t in range(T):
                    step(pool.tensor_copy(stage[:, t, 2, :].rearrange("p (r d) -> p r d", r=2), z[:, t, DSA_K:DSA_K + HD].unsqueeze(1).to_broadcast([P, 2, HD])))
                    step(pool.tensor_copy(stage[:, t, 3, :].rearrange("p (r d) -> p r d", r=4), z[:, t, DSA_KI:DSA_KI + IDX_DIM].unsqueeze(1).to_broadcast([P, 4, IDX_DIM])))
                step.settle()
                pool.sem_inc(staged, 1)
                for j in range(2, GATE_TILES):
                    weight_rest(("gate", l, j))
                weight_rest(("lift", l, 0))
                for f in range(2):
                    for b in range(1, 4):
                        for t in range(T):
                            lin.wait_moved(pool, ("lift", l, f, b, t))
                            part = [gate[:, t, i * D + f * BANK:i * D + (f + 1) * BANK] for i in (0, b)]
                            if b > 1:
                                step.settle(0 if (b, t) == (3, 1) else 1)
                            m = pool.tensor_tensor(part[0], part[0], part[1], ALU.add)
                            if b < 3:
                                step(m)
                            else:
                                m.then_inc(gated, 1)
                pool.dma_start(row_gain, a["norm2_g"][l].partition_broadcast(P)).then_inc(row_gain_loaded, 16)
                root_rows(("n2", l))
                weight_rest(("up", l, 0))
                if l + 1 < L1:
                    pool.wait_ge(normed, normed_due[("n2", l)][1])
                    pool.dma_start(row_gain, a["norm1_g"][l + 1].partition_broadcast(P)).then_inc(row_gain_loaded, 16)

            def load_gains(n):
                key = gains[n]
                if key == "final":
                    srcs = [a["final_g"]]
                elif key == "ln0":
                    srcs = [a["ln0_g_2"], a["ln0_b_2"]]
                else:
                    srcs = [a[key[0] + "_g_2"][key[1]], a[key[0] + "_b_2"][key[1]]]
                for w, src in enumerate(srcs):
                    pool.dma_start(lng[:, n % 2, w, :], src.partition_broadcast(P)).then_inc(lng_loaded[n % 2], 16)

            def after(key):
                n = gains.index(key)
                if n + 2 < len(gains):
                    pool.wait_ge(x_updated, update_at[key, 1])
                    load_gains(n + 2)

            pool.wait_ge(small.filled, small.at[("n2", L1 - 1, 1, 1)] + 1)
            pool.dma_start(hn[:, :, :], a["mem_2"][0].rearrange("(t p) n -> p t n", p=P)).then_inc(mem_loaded, 16)
            load_gains(0)
            load_gains(1)
            def load_alow(l):
                pool.dma_start(w_alow, rows(a["w_in_2"][l], IN2 - RANK, RANK)).then_inc(alow_loaded, 16)

            for i, (key, t) in enumerate([("final", 0), ("ln0", 0), ("final", 1), ("ln0", 1)]):
                root(key, slice(8 + t, 9 + t), slice(12 + t, 13 + t), t)
                if i == 2:
                    pool.wait_ge(lin.filled, lin.at[("down", L1 - 1, 1, 1)] + 1)
                    load_alow(0)
                if i >= 2:
                    weight_rest(("xk", 0, 0), [0] if i == 2 else [1, 2, 3])
            after("final")
            after("ln0")
            for l in range(L2):
                if l == 0:
                    step(pool.memset(qez, 0.0))
                    step(pool.memset(gattT, 0.0))
                    step(pool.memset(uT[:, :, 0:PAD], 0.0))
                step(pool.memset(alT, 1.0))
                step.settle()
                pool.sem_inc(pads_zeroed, 1)
                if l + 1 < L2:
                    pool.wait_ge(small.filled, small.at[("alow", l)] + 1)
                    load_alow(l + 1)
                for key in (("v", l), ("r", l), ("xk", l, 1), ("xv", l, 0), ("xv", l, 1)):
                    weight_rest(key)
                root(("gla", l), slice(0, 8), slice(8, 16))
                root(("conv", l))
                weight_rest(("mix", l, 0))
                weight_rest(("mix", l, 1))
                for w, first in (("ln1", ("xq", l, 0)), ("ln2", ("ffn", l, 0)), ("ln3", ("xk", l + 1, 0))):
                    if w == "ln3" and l + 1 < L2:
                        root((w, l), slice(8, 9), slice(12, 13), 0)
                        weight_rest(first, [0, 1])
                        root((w, l), slice(9, 10), slice(13, 14), 1)
                        weight_rest(first, [2, 3])
                    else:
                        root_rows((w, l))
                        if w != "ln3":
                            weight_rest(first)
                    after((w, l))


_OUTS = [((1, SEQ, D), "float32")]
_INS = ["x", "positions", "norm1_g", "w_in", "mla_q_norm_g", "mla_w_uq", "mla_kv_norm_g", "mla_w_ukv", "nsa_cmp_pe", "nsa_cmp_w",
        "fox_f_bias", "w_branch", "w_out", "norm2_g", "w_up", "w_down", "final_g", "mem_2", "ln0_g_2", "ln0_b_2", "w_in_2", "w_a2_2",
        "b_a_2", "conv_w_2", "conv_b_2", "conv_ln_g_2", "conv_ln_b_2", "gla_norm_g_2", "w_mix_out_2", "ln1_g_2", "ln1_b_2", "w_xq_2",
        "w_xkv_2", "w_xo_2", "ln2_g_2", "ln2_b_2", "w_ffn_in_2", "w_ffn_out_2", "ln3_g_2", "ln3_b_2"]


def kernel(**inputs):
    from concourse import bacc
    from concourse.bass_utils import run_bass_kernel_spmd

    nc = bacc.Bacc("TRN2", target_bir_lowering=False, num_devices=1)
    arrays, aps = {}, {}
    for name in _INS:
        arr = np.ascontiguousarray(inputs[name])
        arrays[f"in_{name}"] = arr
        aps[name] = nc.dram_tensor(f"in_{name}", arr.shape, mybir.dt.from_np(arr.dtype), kind="ExternalInput").ap()
    out = nc.dram_tensor("out", _OUTS[0][0], F32, kind="ExternalOutput").ap()
    two_decoders(nc, aps, out)
    r = run_bass_kernel_spmd(nc, [arrays], core_ids=[0])
    return r.results[0]["out"]
```
